# Optimizing a Trainium2 kernel written in Bass

```python
import math
import jax, jax.numpy as jnp
from jax import lax
import numpy as np

D_MODEL = 2048
BATCH = 1
SEQ = 256
DEPTH = 1

N_BRANCH = 4
BRANCH_W = 1024

POOL_W = BRANCH_W
POOL_WINDOWS = (2, 4, 8, 16)
POOL_GROUPS = len(POOL_WINDOWS)
POOL_GW = POOL_W // POOL_GROUPS

SGU_W = BRANCH_W
SGU_HEADS = 8
SGU_HD = SGU_W // SGU_HEADS
CHUNK = 128

N_Q_HEADS = 16
N_KV_HEADS = 2
Q_PER_KV = N_Q_HEADS // N_KV_HEADS
HEAD_DIM = 64
ATTN_W = N_Q_HEADS * HEAD_DIM
KV_W = N_KV_HEADS * HEAD_DIM
WINDOW = 128
BLOCK = 128
NUM_BUCKETS = 32
MAX_DISTANCE = 128

CONV_W = BRANCH_W
CONV_K = 31

ALPHA = (2 * DEPTH) ** 0.25
BETA = (8 * DEPTH) ** -0.25
LN_EPS = 1e-5

IN_SPLITS = (POOL_W, POOL_W,
             SGU_W, SGU_W, SGU_W,
             ATTN_W, KV_W, KV_W, ATTN_W,
             2 * CONV_W, CONV_W,
             N_BRANCH * D_MODEL)
D_IN = sum(IN_SPLITS)
SPLIT_POINTS = [int(p) for p in np.cumsum(IN_SPLITS)[:-1]]


def layer_norm(x, g, b):
    xf = x.astype(jnp.float32)
    mu = jnp.mean(xf, axis=-1, keepdims=True)
    var = jnp.mean(jnp.square(xf - mu), axis=-1, keepdims=True)
    y = (xf - mu) * lax.rsqrt(var + LN_EPS) * g.astype(jnp.float32) + b.astype(jnp.float32)
    return y.astype(x.dtype)

def t5_bucket(n):
    max_exact = NUM_BUCKETS // 2
    nf = jnp.maximum(n, 1).astype(jnp.float32)
    large = max_exact + (jnp.log(nf / max_exact) / math.log(MAX_DISTANCE / max_exact)
                         * (NUM_BUCKETS - max_exact)).astype(jnp.int32)
    large = jnp.minimum(large, NUM_BUCKETS - 1)
    return jnp.where(n < max_exact, n, large)

def band_geometry():
    i = jnp.arange(BLOCK)[:, None]
    j = jnp.arange(2 * BLOCK)[None, :]
    return i + BLOCK - j

def relative_band_bias(rel_bias):
    d = jnp.clip(band_geometry(), 0, WINDOW - 1)
    bias = rel_bias[t5_bucket(d)]
    bias = jnp.transpose(bias, (2, 0, 1)).astype(jnp.float32)
    return bias.reshape(N_KV_HEADS, Q_PER_KV, BLOCK, 2 * BLOCK)

def pool_mixer(xa, w_grp, scale):
    b, s, _ = xa.shape
    xg = xa.reshape(b, s, POOL_GROUPS, POOL_GW)
    cs = jnp.cumsum(xg.astype(jnp.float32), axis=1)
    cs_pad = jnp.concatenate([jnp.zeros_like(cs[:, :1]), cs], axis=1)
    t = jnp.arange(s)[:, None]
    win = jnp.array(POOL_WINDOWS, dtype=jnp.int32)[None, :]
    lo = jnp.maximum(t + 1 - win, 0)
    cnt = jnp.minimum(t + 1, win).astype(jnp.float32)
    gidx = jnp.arange(POOL_GROUPS)[None, :]
    window_sum = cs - cs_pad[:, lo, gidx, :]
    pooled = (window_sum / cnt[None, :, :, None]).astype(xa.dtype)
    mix = pooled - xg
    y = jnp.einsum('bsgc,gcd->bsgd', mix, w_grp).reshape(b, s, POOL_W)
    return y * scale

def spatial_gating(u, v, ln_g, ln_b, w_s, b_s):
    b, s, _ = v.shape
    nc = s // CHUNK
    vn = layer_norm(v, ln_g, ln_b).reshape(b, nc, CHUNK, SGU_HEADS, SGU_HD)
    causal = jnp.tril(jnp.ones((CHUNK, CHUNK), dtype=bool))
    w = jnp.where(causal[None], w_s, jnp.zeros_like(w_s))
    sp = jnp.einsum('hts,bnshd->bnthd', w, vn) + jnp.transpose(b_s)[None, None, :, :, None]
    return u * sp.reshape(b, s, SGU_W)

def sliding_window_attention(q, k, v, sinks, band_bias):
    b, s, _ = q.shape
    nb = s // BLOCK
    qb = q.reshape(b, nb, BLOCK, N_KV_HEADS, Q_PER_KV, HEAD_DIM)
    kb = k.reshape(b, nb, BLOCK, N_KV_HEADS, HEAD_DIM)
    vb = v.reshape(b, nb, BLOCK, N_KV_HEADS, HEAD_DIM)

    def band(t):
        prev = jnp.concatenate([jnp.zeros_like(t[:, :1]), t[:, :-1]], axis=1)
        return jnp.concatenate([prev, t], axis=2)

    k_band, v_band = band(kb), band(vb)
    logits = jnp.einsum('bnqhgd,bnkhd->bnhgqk', qb, k_band).astype(jnp.float32)
    logits = logits * (HEAD_DIM ** -0.5) + band_bias[None, None]
    d = band_geometry()
    in_window = (d >= 0) & (d < WINDOW)
    has_prev = (jnp.arange(nb)[:, None] > 0) | (jnp.arange(2 * BLOCK)[None, :] >= BLOCK)
    mask = in_window[None] & has_prev[:, None, :]
    logits = jnp.where(mask[None, :, None, None], logits, jnp.float32(-1e30))
    sink = jnp.broadcast_to(sinks.astype(jnp.float32).reshape(1, 1, N_KV_HEADS, Q_PER_KV, 1, 1),
                            logits.shape[:-1] + (1,))
    probs = jax.nn.softmax(jnp.concatenate([logits, sink], axis=-1), axis=-1)[..., :-1]
    o = jnp.einsum('bnhgqk,bnkhd->bnqhgd', probs.astype(v.dtype), v_band)
    return o.reshape(b, s, ATTN_W)

def conformer_conv(d_in, conv_w, conv_b, ln_g, ln_b):
    val, gate = jnp.split(d_in, 2, axis=-1)
    glu = val * jax.nn.sigmoid(gate)
    y = lax.conv_general_dilated(glu, conv_w[:, None, :], window_strides=(1,),
                                 padding=[(CONV_K - 1, 0)],
                                 dimension_numbers=('NWC', 'WIO', 'NWC'),
                                 feature_group_count=CONV_W) + conv_b
    return jax.nn.silu(layer_norm(y, ln_g, ln_b))

def first_inputs(seed: int = 0) -> dict:
    key = jax.random.key(seed)
    ks = jax.random.split(key, 20)
    nrm = lambda k, shape: jax.random.normal(k, shape, dtype=jnp.float32)
    return {
        "x": nrm(ks[0], (BATCH, SEQ, D_MODEL)),
        "w_in": nrm(ks[1], (DEPTH, D_MODEL, D_IN)) * D_MODEL ** -0.5,
        "pool_w": nrm(ks[2], (DEPTH, POOL_GROUPS, POOL_GW, POOL_GW)) * POOL_GW ** -0.5,
        "pool_scale": 1.0 + 0.1 * nrm(ks[3], (DEPTH, POOL_W)),
        "sgu_ln_g": 1.0 + 0.1 * nrm(ks[4], (DEPTH, SGU_W)),
        "sgu_ln_b": 0.1 * nrm(ks[5], (DEPTH, SGU_W)),
        "sgu_w": nrm(ks[6], (DEPTH, SGU_HEADS, CHUNK, CHUNK)) * 0.5 * CHUNK ** -0.5,
        "sgu_b": 1.0 + 0.1 * nrm(ks[7], (DEPTH, SGU_HEADS, CHUNK)),
        "attn_sinks": 0.5 * nrm(ks[8], (DEPTH, N_Q_HEADS)),
        "rel_bias": 0.5 * nrm(ks[9], (NUM_BUCKETS, N_Q_HEADS)),
        "conv_w": nrm(ks[10], (DEPTH, CONV_K, CONV_W)) * CONV_K ** -0.5,
        "conv_b": 0.02 * nrm(ks[11], (DEPTH, CONV_W)),
        "conv_ln_g": 1.0 + 0.1 * nrm(ks[12], (DEPTH, CONV_W)),
        "conv_ln_b": 0.1 * nrm(ks[13], (DEPTH, CONV_W)),
        "w_branch": nrm(ks[14], (DEPTH, N_BRANCH, BRANCH_W, D_MODEL)) * BRANCH_W ** -0.5 * BETA,
        "w_out": nrm(ks[15], (DEPTH, D_MODEL, D_MODEL)) * D_MODEL ** -0.5 * BETA,
        "ln_g": 1.0 + 0.1 * nrm(ks[16], (DEPTH, D_MODEL)),
        "ln_b": 0.1 * nrm(ks[17], (DEPTH, D_MODEL)),
    }

def first_block(x, w_in, pool_w, pool_scale, sgu_ln_g, sgu_ln_b, sgu_w, sgu_b, attn_sinks,
              rel_bias, conv_w, conv_b, conv_ln_g, conv_ln_b, w_branch, w_out, ln_g, ln_b):
    b, s, _ = x.shape
    band_bias = relative_band_bias(rel_bias)
    for l in range(DEPTH):
        h = jnp.einsum('bsd,de->bse', x, w_in[l])
        (a_in, a_gate, u, v, b_gate, q, k, vv, c_gate,
         d_in, d_gate, g_logits) = jnp.split(h, SPLIT_POINTS, axis=-1)

        y_a = pool_mixer(a_in, pool_w[l], pool_scale[l]) * jax.nn.silu(a_gate)
        y_b = spatial_gating(u, v, sgu_ln_g[l], sgu_ln_b[l], sgu_w[l], sgu_b[l]) * jax.nn.silu(b_gate)
        y_c = sliding_window_attention(q, k, vv, attn_sinks[l], band_bias) * jax.nn.silu(c_gate)
        y_d = conformer_conv(d_in, conv_w[l], conv_b[l], conv_ln_g[l], conv_ln_b[l]) * jax.nn.silu(d_gate)

        gates = jax.nn.sigmoid(g_logits.reshape(b, s, N_BRANCH, D_MODEL))
        branches = (y_a, y_b, y_c, y_d)
        merged = gates[:, :, 0] * jnp.einsum('bsc,cd->bsd', branches[0], w_branch[l, 0])
        for i in range(1, N_BRANCH):
            merged = merged + gates[:, :, i] * jnp.einsum('bsc,cd->bsd', branches[i], w_branch[l, i])
        out = jnp.einsum('bsd,de->bse', merged, w_out[l])
        x = layer_norm(ALPHA * x + out, ln_g[l], ln_b[l])
    return x


CHUNK_2 = 64
EPS = 1e-6
MIX_WIDTH = D_MODEL

SSD_HEAD_DIM = 64
SSD_INNER = MIX_WIDTH // 2
SSD_HEADS = SSD_INNER // SSD_HEAD_DIM
SSD_GROUPS = 2
SSD_STATE = 128
SSD_CONV = 4
SSD_CONV_DIM = SSD_INNER + 2 * SSD_GROUPS * SSD_STATE

FOX_HEAD_DIM = 64
FOX_INNER = MIX_WIDTH - SSD_INNER
FOX_HEADS = FOX_INNER // FOX_HEAD_DIM
Q_BLOCK = 128

PEER_HEADS = 8
PEER_N_KEYS = 128
PEER_N_EXPERTS = PEER_N_KEYS * PEER_N_KEYS
PEER_KEY_DIM = 256
PEER_TOPK = 16
PEER_TOKEN_BLOCK = 128

IN_SPLITS_2 = (SSD_INNER, SSD_CONV_DIM, SSD_HEADS, FOX_INNER, FOX_INNER, FOX_INNER, FOX_HEADS)
IN_PROJ_DIM = sum(IN_SPLITS_2)


def rmsnorm(x, w):
    xf = x.astype(jnp.float32)
    xf = xf * lax.rsqrt(jnp.mean(xf * xf, axis=-1, keepdims=True) + EPS)
    return (xf * w.astype(jnp.float32)).astype(x.dtype)

def ssd_chunked(xs, dt, A, Bm, Cm):
    b, l = xs.shape[:2]
    nc = l // CHUNK_2
    R = SSD_HEADS // SSD_GROUPS
    x = xs.astype(jnp.float32).reshape(b, nc, CHUNK_2, SSD_GROUPS, R, SSD_HEAD_DIM)
    dtc = dt.reshape(b, nc, CHUNK_2, SSD_GROUPS, R)
    Bc = Bm.astype(jnp.float32).reshape(b, nc, CHUNK_2, SSD_GROUPS, SSD_STATE)
    Cc = Cm.astype(jnp.float32).reshape(b, nc, CHUNK_2, SSD_GROUPS, SSD_STATE)
    a = dtc * A.reshape(SSD_GROUPS, R)
    a_cum = jnp.cumsum(a, axis=2)
    xdt = x * dtc[..., None]
    seg = a_cum[:, :, :, None] - a_cum[:, :, None]
    tri = jnp.tril(jnp.ones((CHUNK_2, CHUNK_2), dtype=bool))[None, None, :, :, None, None]
    L = jnp.exp(jnp.where(tri, seg, -jnp.inf))
    cb = jnp.einsum('bctgn,bcsgn->bctsg', Cc, Bc)
    y_diag = jnp.einsum('bctsg,bctsgr,bcsgrp->bctgrp', cb, L, xdt)
    decay_states = jnp.exp(a_cum[:, :, -1:] - a_cum)
    states = jnp.einsum('bcsgn,bcsgr,bcsgrp->bcgrpn', Bc, decay_states, xdt)
    chunk_decay = jnp.exp(a_cum[:, :, -1])

    def step(h, inp):
        s_c, d_c = inp
        return h * d_c[..., None, None] + s_c, h

    h0 = jnp.zeros((b, SSD_GROUPS, R, SSD_HEAD_DIM, SSD_STATE), jnp.float32)
    _, prev = lax.scan(step, h0, (jnp.moveaxis(states, 1, 0), jnp.moveaxis(chunk_decay, 1, 0)))
    prev = jnp.moveaxis(prev, 0, 1)
    y_off = jnp.einsum('bctgn,bcgrpn,bctgr->bctgrp', Cc, prev, jnp.exp(a_cum))
    return (y_diag + y_off).reshape(b, l, SSD_HEADS, SSD_HEAD_DIM)

def ssd_group(z, xbc, dt_raw, conv_w, conv_b, dt_bias, a_log, d_skip, ssd_norm_w):
    b, l = z.shape[:2]
    xbc = lax.conv_general_dilated(
        xbc, conv_w[:, None, :], window_strides=(1,), padding=[(SSD_CONV - 1, 0)],
        dimension_numbers=('NWC', 'WIO', 'NWC'), feature_group_count=SSD_CONV_DIM) + conv_b
    xbc = jax.nn.silu(xbc)
    xs, Bm, Cm = jnp.split(xbc, [SSD_INNER, SSD_INNER + SSD_GROUPS * SSD_STATE], axis=-1)
    xs = xs.reshape(b, l, SSD_HEADS, SSD_HEAD_DIM)
    Bm = Bm.reshape(b, l, SSD_GROUPS, SSD_STATE)
    Cm = Cm.reshape(b, l, SSD_GROUPS, SSD_STATE)
    dt = jax.nn.softplus(dt_raw.astype(jnp.float32) + dt_bias.astype(jnp.float32))
    A = -jnp.exp(a_log.astype(jnp.float32))
    y = ssd_chunked(xs, dt, A, Bm, Cm)
    y = y + d_skip.astype(jnp.float32)[:, None] * xs.astype(jnp.float32)
    y = y.reshape(b, l, SSD_INNER) * jax.nn.silu(z.astype(jnp.float32))
    y = y.reshape(b, l, SSD_GROUPS, SSD_INNER // SSD_GROUPS)
    y = y * lax.rsqrt(jnp.mean(y * y, axis=-1, keepdims=True) + EPS)
    y = y.reshape(b, l, SSD_INNER) * ssd_norm_w.astype(jnp.float32)
    return y.astype(z.dtype)

def fox_group(q, k, v, f_raw, fox_f_bias):
    b, l = q.shape[:2]
    q = q.reshape(b, l, FOX_HEADS, FOX_HEAD_DIM) * (FOX_HEAD_DIM ** -0.5)
    k = k.reshape(b, l, FOX_HEADS, FOX_HEAD_DIM)
    v = v.reshape(b, l, FOX_HEADS, FOX_HEAD_DIM)
    log_f = jax.nn.log_sigmoid(f_raw.astype(jnp.float32) + fox_f_bias.astype(jnp.float32))
    cum = jnp.transpose(jnp.cumsum(log_f, axis=1), (0, 2, 1))
    outs = []
    for i in range(l // Q_BLOCK):
        qs, qe = i * Q_BLOCK, (i + 1) * Q_BLOCK
        s = jnp.einsum('bqhd,bkhd->bhqk', q[:, qs:qe], k[:, :qe]).astype(jnp.float32)
        s = s + cum[:, :, qs:qe, None] - cum[:, :, None, :qe]
        mask = (qs + jnp.arange(Q_BLOCK))[:, None] >= jnp.arange(qe)[None, :]
        p = jax.nn.softmax(jnp.where(mask, s, -jnp.inf), axis=-1)
        outs.append(jnp.einsum('bhqk,bkhd->bqhd', p.astype(v.dtype), v[:, :qe]))
    return jnp.concatenate(outs, axis=1).reshape(b, l, FOX_INNER)

def peer(h, wq, k1, k2, u, v):
    b, l, d = h.shape
    t = h.reshape(-1, d)
    T = t.shape[0]
    q = (t @ wq).reshape(T, PEER_HEADS, 2, PEER_KEY_DIM // 2)
    s1 = jnp.einsum('thd,hnd->thn', q[:, :, 0], k1).astype(jnp.float32)
    s2 = jnp.einsum('thd,hnd->thn', q[:, :, 1], k2).astype(jnp.float32)
    v1, i1 = lax.top_k(s1, PEER_TOPK)
    v2, i2 = lax.top_k(s2, PEER_TOPK)
    cand = (v1[..., :, None] + v2[..., None, :]).reshape(T, PEER_HEADS, PEER_TOPK * PEER_TOPK)
    cand_idx = (i1[..., :, None] * PEER_N_KEYS + i2[..., None, :]).reshape(T, PEER_HEADS, PEER_TOPK * PEER_TOPK)
    sc, pos = lax.top_k(cand, PEER_TOPK)
    idx = jnp.take_along_axis(cand_idx, pos, axis=-1)
    g = jax.nn.softmax(sc, axis=-1).astype(t.dtype)

    def block(args):
        tb, ib, gb = args
        act = jax.nn.gelu(jnp.einsum('thkd,td->thk', u[ib], tb), approximate=False)
        return jnp.einsum('thk,thkd->td', gb * act, v[ib])

    nb = T // PEER_TOKEN_BLOCK
    out = lax.map(block, (t.reshape(nb, PEER_TOKEN_BLOCK, d),
                          idx.reshape(nb, PEER_TOKEN_BLOCK, PEER_HEADS, PEER_TOPK),
                          g.reshape(nb, PEER_TOKEN_BLOCK, PEER_HEADS, PEER_TOPK)))
    return out.reshape(b, l, d)

def second_inputs(seed: int = 0) -> dict:
    key = jax.random.key(seed)
    ks = jax.random.split(key, 20)
    f32 = jnp.float32
    nrm = lambda k, shape: jax.random.normal(k, shape, f32)
    dt0 = jnp.exp(jax.random.uniform(ks[5], (SSD_HEADS,), f32, np.log(1e-3), np.log(1e-1)))
    return {
        "x": nrm(ks[0], (BATCH, SEQ, D_MODEL)),
        "ln1_w": 1.0 + 0.02 * nrm(ks[1], (D_MODEL,)),
        "w_in": nrm(ks[2], (D_MODEL, IN_PROJ_DIM)) * D_MODEL ** -0.5,
        "conv_w": nrm(ks[3], (SSD_CONV, SSD_CONV_DIM)) * SSD_CONV ** -0.5,
        "conv_b": 0.02 * nrm(ks[4], (SSD_CONV_DIM,)),
        "dt_bias": dt0 + jnp.log(-jnp.expm1(-dt0)),
        "a_log": jnp.log(jax.random.uniform(ks[6], (SSD_HEADS,), f32, 1.0, 16.0)),
        "d_skip": 1.0 + 0.1 * nrm(ks[7], (SSD_HEADS,)),
        "ssd_norm_w": 1.0 + 0.02 * nrm(ks[8], (SSD_INNER,)),
        "fox_f_bias": jnp.linspace(1.0, 6.0, FOX_HEADS, dtype=f32) + 0.1 * nrm(ks[9], (FOX_HEADS,)),
        "w_out": nrm(ks[10], (MIX_WIDTH, D_MODEL)) * MIX_WIDTH ** -0.5,
        "ln2_w": 1.0 + 0.02 * nrm(ks[11], (D_MODEL,)),
        "peer_wq": nrm(ks[12], (D_MODEL, PEER_HEADS * PEER_KEY_DIM)) * D_MODEL ** -0.5,
        "peer_k1": nrm(ks[13], (PEER_HEADS, PEER_N_KEYS, PEER_KEY_DIM // 2)) * (PEER_KEY_DIM // 2) ** -0.5,
        "peer_k2": nrm(ks[14], (PEER_HEADS, PEER_N_KEYS, PEER_KEY_DIM // 2)) * (PEER_KEY_DIM // 2) ** -0.5,
        "peer_u": nrm(ks[15], (PEER_N_EXPERTS, D_MODEL)) * D_MODEL ** -0.5,
        "peer_v": nrm(ks[16], (PEER_N_EXPERTS, D_MODEL)) * PEER_HEADS ** -0.5,
        "lnf_w": 1.0 + 0.02 * nrm(ks[17], (D_MODEL,)),
    }

def second_block(x, ln1_w, w_in, conv_w, conv_b, dt_bias, a_log, d_skip, ssd_norm_w,
              fox_f_bias, w_out, ln2_w, peer_wq, peer_k1, peer_k2, peer_u, peer_v, lnf_w):
    split_at = [int(s) for s in np.cumsum(IN_SPLITS_2)[:-1]]
    for _ in range(DEPTH):
        h = rmsnorm(x, ln1_w)
        proj = h @ w_in
        z, xbc, dt_raw, q, k, v, f_raw = jnp.split(proj, split_at, axis=-1)
        y_ssd = ssd_group(z, xbc, dt_raw, conv_w, conv_b, dt_bias, a_log, d_skip, ssd_norm_w)
        y_fox = fox_group(q, k, v, f_raw, fox_f_bias)
        x = x + jnp.concatenate([y_ssd, y_fox], axis=-1) @ w_out
        x = x + peer(rmsnorm(x, ln2_w), peer_wq, peer_k1, peer_k2, peer_u, peer_v)
    return rmsnorm(x, lnf_w)


def setup_inputs(seed=0):
    out = dict(first_inputs(seed))
    for name, value in second_inputs(seed + 1).items():
        if name != "x":
            out[name + "_2"] = value
    return out


def reference(
    x, w_in, pool_w, pool_scale, sgu_ln_g, sgu_ln_b, sgu_w, sgu_b, attn_sinks, rel_bias, conv_w,
    conv_b, conv_ln_g, conv_ln_b, w_branch, w_out, ln_g, ln_b, ln1_w_2, w_in_2, conv_w_2,
    conv_b_2, dt_bias_2, a_log_2, d_skip_2, ssd_norm_w_2, fox_f_bias_2, w_out_2, ln2_w_2,
    peer_wq_2, peer_k1_2, peer_k2_2, peer_u_2, peer_v_2, lnf_w_2,
):
    x = first_block(
        x, w_in, pool_w, pool_scale, sgu_ln_g, sgu_ln_b, sgu_w, sgu_b, attn_sinks, rel_bias,
        conv_w, conv_b, conv_ln_g, conv_ln_b, w_branch, w_out, ln_g, ln_b,
    )
    return second_block(
        x, ln1_w_2, w_in_2, conv_w_2, conv_b_2, dt_bias_2, a_log_2, d_skip_2, ssd_norm_w_2,
        fox_f_bias_2, w_out_2, ln2_w_2, peer_wq_2, peer_k1_2, peer_k2_2, peer_u_2, peer_v_2,
        lnf_w_2,
    )


_drawn_inputs = setup_inputs


def setup_inputs(seed=0):
    import zlib

    import numpy as np

    out = dict(_drawn_inputs(seed))
    spreads = {}
    factors = {'pool_scale': 3.246,
     'sgu_ln_g': 5.6,
     'sgu_ln_b': 5.241,
     'sgu_b': 2.956,
     'attn_sinks': 27.65,
     'rel_bias': 3.302,
     'conv_b': 6.376,
     'conv_ln_g': 3.61,
     'conv_ln_b': 4.008,
     'ssd_norm_w_2': 2.872,
     'ln2_w_2': 2.755,
     'lnf_w_2': 7.91}
    for name, (base, spread) in spreads.items():
        noise = np.random.default_rng([zlib.crc32(name.encode()), seed]).standard_normal(out[name].shape)
        drawn = base * np.exp(spread * noise) if base else spread * noise
        out[name] = __import__('jax').numpy.asarray(drawn.astype(out[name].dtype))
    for name, factor in factors.items():
        out[name] = (out[name] * factor).astype(out[name].dtype)
    return out
```

```python
import numpy as np
from contextlib import ExitStack

import concourse.bass as bass
from concourse import mybir

T = 256
NT = T // 128
D = 2048
KC = D // 128
WC = 1024 // 128
CONV_K = 31
CONV2_K = 4
HEADS = 16
TOPK = 16
PEER_HEADS = 8
KEYS = 128
RAW = 4
SPLIT = 2
BANKS = 4
NEG = -1e30
LOWEST = -3.0e38
ALPHA = 2.0 ** 0.25
LN_EPS = 1e-5
RMS_EPS = 1e-6

ORDER = [("c_kv", 2), ("c_q", 8), ("c_gate", 8), ("d_val", 8), ("d_act", 8), ("d_gate", 8),
         ("b_v", 8), ("b_u", 8), ("b_gate", 8), ("a_in", 8), ("a_gate", 8), ("a_pool", 1),
         ("merge", 96), ("w_out", 16), ("dtf", 1), ("z", 8), ("xbc", 12), ("fq", 8), ("fk", 8),
         ("fv", 8), ("w_out2", 16), ("wq", 16), ("experts", 256)]
FIRST, NBLOCKS = {}, 0
for _name, _count in ORDER:
    FIRST[_name] = NBLOCKS
    NBLOCKS += _count
COUNT = dict(ORDER)
SLICES = 8

VECS = [("pool_scale", 8), ("sgu_ln_g", 8), ("sgu_ln_b", 8), ("conv_b", 8), ("conv_ln_g", 8),
        ("conv_ln_b", 8), ("conv_w", 8 * CONV_K), ("ln_g", 16), ("ln_b", 16), ("ln1_w", 16),
        ("conv2_w", 12 * CONV2_K), ("conv2_b", 12), ("d_skip", 8), ("ssd_norm", 8), ("ln2_w", 16),
        ("lnf_w", 16), ("sinks", 16), ("dtf_bias", 1), ("dtf_sign", 1), ("a_log", 1)]
VCOL, NVEC = {}, 0
for _name, _count in VECS:
    VCOL[_name] = NVEC
    NVEC += _count


NORMS = ["d", "b", "x1", "h1", "s0", "s1", "h2", "fin"]
CENTRED = ["d", "b", "x1"]
IN_PARTS = ["h1", "s0", "s1", "h2"]


def turn(step, name):
    if step in ("sum", "centred", "normed", "out"):
        return CENTRED.index(name) + 1
    return (IN_PARTS if step in ("scaled", "hi", "lo") else NORMS).index(name) + 1


class Block:

    def __init__(self, n0, q=0):
        self.n0, self.q = n0, q
        self.raw, self.half, self.bank = n0 % RAW, n0 % SPLIT, n0 % BANKS

    def count(self, more=0):
        return self.n0 + more + 4 * self.q

    def uses(self, more=0):
        return self.n0 // 4 + 1 + more + self.q

    def ahead(self, k):
        return Block(self.n0 + k, self.q)

    def index(self, base):
        return self.n0 - base + 4 * self.q


class Steps:

    def __init__(self, eng, sem):
        self.eng, self.sem, self.n, self.turn = eng, sem, 0, None

    def link(self, ins):
        ins.then_inc(self.sem, 1)
        self.n += 1
        self.eng.wait_ge(self.sem, self.n if self.turn is None else self.n + self.turn)

    def loop(self, count, per_turn):
        return _StepsLoop(self, count, per_turn)


class _StepsLoop:
    def __init__(self, steps, count, per_turn):
        self.steps, self.count, self.per_turn = steps, count, per_turn

    def __enter__(self):
        self.fori = self.steps.eng.Fori(0, self.count)
        g = self.fori.__enter__()
        self.outer, self.start = self.steps.turn, self.steps.n
        if self.per_turn:
            self.steps.turn = g * self.per_turn if self.outer is None else self.outer + g * self.per_turn
        return g

    def __exit__(self, *e):
        if e[0] is None:
            assert self.steps.n - self.start == self.per_turn, (self.steps.n - self.start, self.per_turn)
        self.steps.turn = self.outer
        self.steps.n = self.start + self.count * self.per_turn
        return self.fori.__exit__(*e)


def blocks(eng, steps, first, count, body, per_turn=0, unit=4):
    n, left = first, count
    while left and n < 4:
        body(Block(n), n - first, 0)
        n, left = n + 1, left - 1
    turns = left // unit
    if n + turns * unit + SPLIT > NBLOCKS:
        turns -= 1
    if turns > 1:
        with steps.loop(turns, per_turn) as g:
            for i in range(unit):
                body(Block(n + i, g * (unit // 4)), n - first + i, g)
        n, left = n + turns * unit, left - turns * unit
    while left:
        body(Block(n), n - first, 0)
        n, left = n + 1, left - 1


def build(nc, stream, xt, vecs, sgu_wt, sgu_b, relb, buckets, keys, inv_cnt, out):
    f32, f32r, u32 = mybir.dt.float32, mybir.dt.float32r, mybir.dt.uint32
    ALU, ACT, AX = mybir.AluOpType, mybir.ActivationFunctionType, mybir.AxisListType

    KB = 1024
    origin = -(-nc.sbuf_base // 32) * 32
    RING = origin + 4 * KB
    XAT = RING + 64 * KB
    ARENA = XAT + 32 * KB

    def at(name, shape, offset, dtype=f32):
        return nc.alloc_sbuf_tensor_at(name, shape, dtype, offset=int(offset))

    def ar(name, shape, kb, dtype=f32):
        return at(name, shape, ARENA + kb * KB, dtype)

    vec = at("vec", [128, NVEC], origin)
    ident = at("ident", [128, 128], origin + 2 * KB)
    ones = at("ones", [128, 128], origin + 2 * KB + 512)
    iota = at("iota", [128, 128], origin + 3 * KB)
    raw = [at(f"raw{i}", [128, KC, 128], RING + 8 * KB * i) for i in range(RAW)]
    whi = [at(f"whi{i}", [128, KC, 128], RING + (32 + 8 * i) * KB, f32r) for i in range(SPLIT)]
    wlo = [at(f"wlo{i}", [128, KC, 128], RING + (48 + 8 * i) * KB, f32r) for i in range(SPLIT)]
    xhi = at("xhi", [128, KC, T], XAT, f32r)
    xlo = at("xlo", [128, KC, T], XAT + 16 * KB, f32r)

    yhi = [ar(f"yhi{i}", [128, WC, T], 16 * i, f32r) for i in range(4)]
    ylo = [ar(f"ylo{i}", [128, WC, T], 16 * i + 8, f32r) for i in range(4)]
    xraw = ar("xraw", [128, KC, T], 0)
    cq = ar("cq", [128, 2, WC, T], 64)
    cbias = ar("cbias", [128, HEADS, T], 80)
    cgate = ar("cgate", [128, WC, T], 96)
    ckv = ar("ckv", [128, 2, T], 104)
    cvtok = ar("cvtok", [128, NT, 128], 106)
    cprob = [ar(f"cprob{i}", [128, 3, 128], 32 + 2 * i) for i in range(2)]
    cprobT = [ar(f"cprobT{i}", [128, 3, 128], 36 + 2 * i) for i in range(2)]
    co = ar("co", [128, WC, T], 40)
    csmall = ar("csmall", [128, 64], 31)
    cband = ar("cband", [16, 384], 28)
    onehot_b = ar("onehot_b", [32, 128], 26)
    relb_sb = ar("relb_sb", [32, 16], 27)
    glu = ar("glu", [128, WC, T + CONV_K - 1], 64)
    dacc = ar("dacc", [128, WC, T], 73.25)
    dgate = ar("dgate", [128, WC, T], 81.25)
    bv = ar("bv", [128, WC, T], 89.25)
    bug = ar("bug", [128, WC, T], 97.25)
    PAD = 16
    ain = ar("ain", [128, WC, T + PAD], 0)
    agate = ar("agate", [128, WC, T], 64)
    sig = [ar(f"sig{i}", [128, T], 105.5 + i) for i in range(2)]
    dsq = ar("dsq", [128, WC, T], 32)
    bsq = ar("bsq", [128, WC, T], 16)
    stat = [ar(f"stat{i}", [128, T], 24 + i) for i in range(6)]
    vtok = ar("vtok", [128, NT, 1024], 73.25)
    sguw = ar("sguw", [128, WC, 128], 81.25)
    sgub = ar("sgub", [128, WC, 128], 85.25)
    win_a = ar("win_a", [128, WC, T + PAD], 72)
    win_b = ar("win_b", [128, WC - 2, T + PAD], 80.5)
    cnt = ar("cnt", [128, 4, T], 87)
    mixhi = ar("mixhi", [128, WC, T], 91, f32r)
    mixlo = ar("mixlo", [128, WC, T], 99, f32r)
    mhi = ar("mhi", [128, KC, T], 64, f32r)
    mlo = ar("mlo", [128, KC, T], 80, f32r)

    gates = [ar(f"gates{i}", [128, 4, T], 96 + 4 * i) for i in range(2)]
    msum = [ar(f"msum{i}", [128, T], 104 + i) for i in range(2)]
    zsum = ar("zsum", [128, KC, T], 0)
    xagain = ar("xagain", [128, KC, T], 16)
    x1 = ar("x1", [128, KC, T], 32)
    sq16 = ar("sq16", [128, KC, T], 48)
    st16 = [ar(f"st16_{i}", [128, T], 96 + i) for i in range(5)]
    zg = ar("zg", [128, WC, T], 0)
    xpad = ar("xpad", [128, 12, T + CONV2_K - 1], 8)
    xconv = ar("xconv", [128, 12, T], 48)
    xtok = ar("xtok", [128, NT, 1024], 21)
    dtfs = ar("dtfs", [128, T], 96)
    cum = ar("cum", [128, T], 97)
    ncum = ar("ncum", [128, T], 98)
    cumT = ar("cumT", [128, NT, 128], 99)
    dtT = ar("dtT", [128, NT, 128], 100)
    acol = ar("acol", [128, 8], 101)
    cmask = ar("cmask", [128, 128], 101.5)
    cb = ar("cb", [128, 2, 384], 29)
    dec = [ar(f"dec{i}", [128, 384], 60 + 1.5 * i) for i in range(2)]
    dtt = [ar(f"dtt{i}", [128, T], 102 + i) for i in range(4)]
    yssd = ar("yssd", [128, WC, T], 8)
    sst = [ar(f"sst{i}", [128, T], 102 + i) for i in range(5)]
    ssq = ar("ssq", [128, 4, T], 60)
    fq = ar("fq", [128, 2, WC, T], 0)
    fk = ar("fk", [128, WC, T], 16)
    fv = ar("fv", [128, WC, T], 48)
    fvtok = ar("fvtok", [128, NT, 1024], 56)
    fprob = [ar(f"fprob{i}", [128, 3, 128], 24 + 1.5 * i) for i in range(2)]
    fprobT = [ar(f"fprobT{i}", [128, 3, 128], 27 + 1.5 * i) for i in range(2)]
    fsmall = ar("fsmall", [128, 64], 30)
    fo = ar("fo", [128, WC, T], 48)

    pq = ar("pq", [128, KC, T], 0)
    pk = ar("pk", [128, KC, 128], 16)
    ps_ = ar("ps_", [128, NT, KC, 128], 48)
    cand = ar("cand", [128, KC, 256], 64)
    hit = ar("hit", [128, KC, 256], 80)
    top = ar("top", [128, NT * KC, TOPK], 96)
    topi = ar("topi", [128, NT * KC, TOPK], 98, u32)
    topf = ar("topf", [128, NT * KC, TOPK], 100)
    best = ar("best", [128, KC, TOPK], 102)
    besti = ar("besti", [128, KC, TOPK], 103, u32)
    slot_i = [ar(f"slot_i{i}", [128, KC, TOPK], 104 + i, u32) for i in range(2)]
    slot_f = [ar(f"slot_f{i}", [128, KC, TOPK], 24 + i) for i in range(2)]
    chosen = [ar(f"chosen{i}", [128, KC, TOPK], 26 + i) for i in range(3)]
    gsum = ar("gsum", [128, KC], 106)
    chosenT = [ar(f"chosenT{i}", [128, T], 29 + i) for i in range(3)]
    one1 = [ar(f"one1_{i}", [128, 4, 128], 2 * i) for i in range(2)]
    one2 = [ar(f"one2_{i}", [128, 4, 128], 4 + 2 * i) for i in range(2)]
    gstage = [ar(f"gstage{i}", [128, SLICES, 32, 16], 64 + 16 * i) for i in range(2)]
    gslice = ar("gslice", [128, T, 16], 48)
    aghi = ar("aghi", [128, 16, T], 64, f32r)
    aglo = ar("aglo", [128, 16, T], 80, f32r)
    gelu = [ar(f"gelu{i}", [128, T], 99 + i) for i in range(2)]
    gated = [ar(f"gated{i}", [128, T], 101 + i) for i in range(2)]
    fst = [ar(f"fst{i}", [128, T], 99 + i) for i in range(5)]

    def bank(i):
        return pb[i]

    es = ExitStack()
    with es:
        pb = [es.enter_context(nc.psum_tensor(f"bank{i}", [128, 512], f32)) for i in range(8)]
        made = {}

        def sem(name):
            if name not in made:
                made[name] = es.enter_context(nc.semaphore(name))
            return made[name]

        def vcol(name, i=0, p0=0, p1=128):
            return vec[p0:p1, VCOL[name] + i:VCOL[name] + i + 1]

        def chunk(buf, j):
            if isinstance(j, int):
                return buf[:, j, :]
            return buf[:, bass.ds(j, 1), :].rearrange("p a n -> p (a n)")

        def spread(tile, n):
            return tile[:, :].rearrange("p (a n) -> p a n", a=1).to_broadcast([128, n, T])

        hi_done, lo_done, mm_done = sem("hi_done"), sem("lo_done"), sem("mm_done")
        raw_loaded = [sem(f"raw_loaded{i}") for i in range(RAW)]
        evacuated = [sem(f"evacuated{i}") for i in range(BANKS)]

        def exists(n):
            return not isinstance(n, int) or n < NBLOCKS

        def load(sp, b):
            if b.n0 >= RAW:
                sp.wait_ge(lo_done, b.count(1 - RAW))
            sp.dma_start(raw[b.raw][:, :, :].rearrange("p k c -> p (k c)"),
                         stream[bass.ds(b.count(), 1)].rearrange("a p n -> (a p) n")
                         ).then_inc(raw_loaded[b.raw], 16)

        def split_hi(act, b):
            act.wait_ge(raw_loaded[b.raw], 16 * b.uses())
            if b.n0 >= SPLIT:
                act.wait_ge(mm_done, b.count(1 - SPLIT))
            nc.scalar.copy(whi[b.half][:, :, :], raw[b.raw][:, :, :]).then_inc(hi_done, 1)

        def split_lo(dve, b):
            dve.wait_ge(hi_done, b.count(1))
            nc.vector.tensor_tensor(wlo[b.half][:, :, :], raw[b.raw][:, :, :],
                                    whi[b.half][:, :, :].bitcast(f32), ALU.subtract).then_inc(lo_done, 1)

        def product(pe, b, rhi, rlo, ks=range(KC), k0=0, cols=0, first=True, last=True):
            if first:
                pe.wait_ge(lo_done, b.count(1))
                if b.n0 >= BANKS:
                    pe.wait_ge(evacuated[b.bank], b.uses(-1))
            o = bank(b.bank)[:, cols:cols + T]
            for i, k in enumerate(ks):
                r = k0 + i
                nc.tensor.matmul(o, whi[b.half][:, k, :], rhi[:, r, :], start=i == 0, stop=False)
                nc.tensor.matmul(o, whi[b.half][:, k, :], rlo[:, r, :], start=False, stop=False)
                ins = nc.tensor.matmul(o, wlo[b.half][:, k, :], rhi[:, r, :], start=False,
                                       stop=i == len(ks) - 1)
            if last:
                ins.then_inc(mm_done, 1)

        def wait_evacuated(eng, name):
            end = FIRST[name] + COUNT[name]
            for i in range(BANKS):
                eng.wait_ge(evacuated[i], (end - 1 - i) // 4 + 1)

        def expert_blocks(eng, steps, e, off, body):
            last = isinstance(e, int) and off == 16
            with steps.loop(3 if last else 4, 0) as g:
                for i in range(4):
                    body(Block(FIRST["experts"] + off + i, e * 8 + g), g * 4 + i, g)
            if last:
                for i in range(4):
                    body(Block(FIRST["experts"] + off + i, e * 8 + 3), 12 + i, 3)

        block = es.enter_context(nc.Block())

        def norm_pe(pe, name, buf, sq, n, ready, centre=True):
            if centre:
                ready(pe)
                for c in range(n):
                    ins = nc.tensor.matmul(bank(4)[:, 0:T], ones[:, :], buf[:, c, :], start=c == 0, stop=c == n - 1)
                ins.then_inc(sem("norm_sum"), 1)
            pe.wait_ge(sem("norm_squared"), turn("squared", name))
            for c in range(n):
                ins = nc.tensor.matmul(bank(5)[:, 0:T], ones[:, :], sq[:, c, :], start=c == 0, stop=c == n - 1)
            ins.then_inc(sem("norm_sumsq"), 1)

        def norm_dve(dve, st, name, buf, n, t, eps, centre=True, scale=True):
            mean, var, r, u, sd = t[:5]
            if centre:
                dve.wait_ge(sem("norm_sum"), turn("sum", name))
                st.link(nc.vector.tensor_scalar(mean[:, :], bank(4)[:, 0:T], 1.0 / (128 * n), None, ALU.mult))
                nc.vector.tensor_tensor(buf[:, :, :], buf[:, :, :], spread(mean, n),
                                        ALU.subtract).then_inc(sem("norm_centred"), 1)
            dve.wait_ge(sem("norm_sumsq"), turn("sumsq", name))
            nc.vector.tensor_scalar(var[:, :], bank(5)[:, 0:T], 1.0 / (128 * n), eps, ALU.mult,
                                    ALU.add).then_inc(sem("norm_var"), 1)
            dve.wait_ge(sem("norm_sd"), turn("sd", name))
            st.link(nc.vector.reciprocal(r[:, :], sd[:, :]))
            st.link(nc.vector.tensor_tensor(u[:, :], r[:, :], r[:, :], ALU.mult))
            st.link(nc.vector.tensor_tensor(u[:, :], u[:, :], var[:, :], ALU.mult))
            st.link(nc.vector.tensor_scalar(u[:, :], u[:, :], -0.5, 1.5, ALU.mult, ALU.add))
            st.link(nc.vector.tensor_tensor(r[:, :], r[:, :], u[:, :], ALU.mult))
            if scale:
                nc.vector.tensor_tensor(buf[:, :, :], buf[:, :, :], spread(r, n),
                                        ALU.mult).then_inc(sem("norm_normed"), 1)

        def norm_act(act, name, buf, sq, t, ready=None, centre=True):
            if centre:
                act.wait_ge(sem("norm_centred"), turn("centred", name))
            else:
                ready(act)
            nc.scalar.activation(sq[:, :, :], buf[:, :, :], ACT.Square).then_inc(sem("norm_squared"), 1)
            act.wait_ge(sem("norm_var"), turn("var", name))
            nc.scalar.activation(t[4][:, :], t[1][:, :], ACT.Sqrt).then_inc(sem("norm_sd"), 1)

        def affine_act(act, name, buf, n, gain, offset, func):
            act.wait_ge(sem("norm_normed"), turn("normed", name))
            for c in range(n):
                ins = nc.scalar.activation(buf[:, c, :], buf[:, c, :], func, bias=vcol(offset, c),
                                           scale=vcol(gain, c))
            ins.then_inc(sem("norm_out"), 1)

        def attend_pe(pe, name, q, k, kchunk, vt, prob, probT, extra):
            def scores(c, par):
                if c:
                    pe.wait_ge(sem(name + "_exp"), 4 * (c - 1) + 2 * par + 2)
                o, kc = bank(4 + par), kchunk(c)
                for lo, w, qt in ((0, 128, 0), (128, 256, 1)):
                    more = extra(c, par, qt)
                    nc.tensor.matmul(o[:, lo:lo + w], q[:, par, c, 128 * qt:128 * qt + 128], k[:, kc, 0:w],
                                     start=True, stop=not more)
                    for i, (l, r, a, b) in enumerate(more):
                        ins = nc.tensor.matmul(o[:, lo + a:lo + b], l, r, start=False, stop=i == len(more) - 1)
                ins.then_inc(sem(name + "_scores"), 1)

            scores(0, 0)
            scores(0, 1)
            for c in range(WC):
                for par in range(2):
                    pe.wait_ge(sem(name + "_prob"), 2 * c + par + 1)
                    if c:
                        pe.wait_ge(sem(name + "_o"), 2 * (c - 1) + par + 1)
                    for j in range(3):
                        ins = nc.tensor.transpose(bank(6 + par)[:, 128 * j:128 * j + 128], prob[par][:, j, :],
                                                  ident[:, :])
                    ins.then_inc(sem(name + "_turned"), 1)
                if c + 1 < WC:
                    scores(c + 1, 0)
                    scores(c + 1, 1)
                for par in range(2):
                    pe.wait_ge(sem(name + "_probT"), 2 * c + par + 1)
                    o = bank(6 + par)
                    nc.tensor.matmul(o[:, 0:128], vt(0, c), probT[par][:, 0, :], start=True, stop=True)
                    nc.tensor.matmul(o[:, 128:256], vt(0, c), probT[par][:, 1, :], start=True, stop=False)
                    nc.tensor.matmul(o[:, 128:256], vt(1, c), probT[par][:, 2, :], start=False,
                                     stop=True).then_inc(sem(name + "_sums"), 1)

        def attend_dve(dve, st, name, prob, small, o, gate, sinks, k):
            with st.loop(WC, k) as g:
                for par in range(2):
                    m = small[:, 8 * par:8 * par + 2]
                    dve.wait_ge(sem(name + "_scores"), 2 * g + par + 1)
                    nc.vector.reduce_max(m[:, 0:1], bank(4 + par)[:, 0:128], AX.X)
                    st.link(nc.vector.reduce_max(m[:, 1:2], bank(4 + par)[:, 128:384], AX.X))
                    if sinks:
                        sink = vec[:, bass.ds(g * 2 + (VCOL["sinks"] + par), 1)]
                        nc.vector.tensor_scalar(small[:, 8 * par + 2:8 * par + 4], m, sink, -1.0, ALU.max,
                                                ALU.mult).then_inc(sem(name + "_max"), 1)
                    else:
                        nc.vector.tensor_scalar(small[:, 8 * par + 2:8 * par + 4], m, -1.0, None,
                                                ALU.mult).then_inc(sem(name + "_max"), 1)
                for par in range(2):
                    den = small[:, 8 * par + 4:8 * par + 6]
                    dve.wait_ge(sem(name + "_exp"), 4 * g + 2 * par + 2)
                    if sinks:
                        dve.wait_ge(sem(name + "_sink"), 2 * g + par + 1)
                        st.link(nc.vector.tensor_tensor(den, den, small[:, 8 * par + 6:8 * par + 8], ALU.add))
                    st.link(nc.vector.reciprocal(den, den))
                    nc.vector.tensor_scalar(prob[par][:, 0, :], prob[par][:, 0, :], den[:, 0:1], None, ALU.mult)
                    nc.vector.tensor_scalar(prob[par][:, 1:3, :], prob[par][:, 1:3, :], den[:, 1:2], None,
                                            ALU.mult).then_inc(sem(name + "_prob"), 1)
                for par in range(2):
                    p0, p1 = 64 * par, 64 * par + 64
                    dve.wait_ge(sem(name + "_sums"), 2 * g + par + 1)
                    dst = o[p0:p1, bass.ds(g, 1), :].rearrange("p a n -> p (a n)")
                    if gate is not None:
                        gt = gate[p0:p1, bass.ds(g, 1), :].rearrange("p a n -> p (a n)")
                        nc.vector.tensor_tensor(dst, bank(6 + par)[p0:p1, 0:T], gt, ALU.mult
                                                ).then_inc(sem(name + "_o"), 1)
                    else:
                        nc.vector.tensor_copy(dst, bank(6 + par)[p0:p1, 0:T]).then_inc(sem(name + "_o"), 1)

        def attend_act(act, name, prob, probT, small, sinks):
            with act.Fori(0, WC) as g:
                for par in range(2):
                    act.wait_ge(sem(name + "_max"), 2 * g + par + 1)
                    nm = small[:, 8 * par + 2:8 * par + 4]
                    nc.scalar.activation(prob[par][:, 0, :], bank(4 + par)[:, 0:128], ACT.Exp, bias=nm[:, 0:1],
                                         accum_out=small[:, 8 * par + 4:8 * par + 5]).then_inc(sem(name + "_exp"), 1)
                    nc.scalar.activation(prob[par][:, 1:3, :], bank(4 + par)[:, 128:384], ACT.Exp,
                                         bias=nm[:, 1:2], accum_out=small[:, 8 * par + 5:8 * par + 6]
                                         ).then_inc(sem(name + "_exp"), 1)
                    if sinks:
                        sink = vec[:, bass.ds(g * 2 + (VCOL["sinks"] + par), 1)]
                        nc.scalar.activation(small[:, 8 * par + 6:8 * par + 8], nm, ACT.Exp, bias=sink
                                             ).then_inc(sem(name + "_sink"), 1)
                for par in range(2):
                    act.wait_ge(sem(name + "_turned"), 2 * g + par + 1)
                    nc.scalar.copy(probT[par][:, :, :], bank(6 + par)[:, 0:384]).then_inc(sem(name + "_probT"), 1)

        band_d = nc.dram_tensor("relative_band", [HEADS, 128, 384], f32, kind="Internal").ap()
        gate_d = nc.dram_tensor("gate_matrix", [SLICES, 128, T * 16], f32, kind="Internal").ap()
        YB, YA, YC, YD = 1, 0, 3, 2

        @block.sync
        def _(sp):
            sp.dma_start(xraw[:, :, :].rearrange("p k n -> p (k n)"), xt).then_inc(sem("x_loaded"), 16)
            for n in range(RAW):
                load(sp, Block(n))
            with sp.Fori(1, NBLOCKS // 4) as g:
                for i in range(4):
                    load(sp, Block(4 + i, g - 1))
            for n in range(NBLOCKS // 4 * 4, NBLOCKS):
                load(sp, Block(n))
            for half in range(4):
                sp.wait_ge(sem("out_ready"), 4 * half + 4)
                sp.dma_start(out[:, 1024 * half:1024 * half + 1024],
                             zsum[:, 4 * half:4 * half + 4, :].rearrange("p c n -> p (c n)")
                             ).then_inc(sem("out_stored"), 16)
            sp.wait_ge(sem("out_stored"), 64)

        @block.gpsimd
        def _(pool):
            nc.gpsimd.memset(ident[:, :], 0.0).then_inc(sem("pool_memset"), 1)
            nc.gpsimd.memset(cband[:, :], NEG).then_inc(sem("band_cleared"), 1)
            nc.gpsimd.memset(ones[:, :], 1.0).then_inc(sem("ones_ready"), 1)
            nc.gpsimd.iota(iota[:, :], [[1, 128]], base=0, channel_multiplier=0,
                           allow_small_or_imprecise_dtypes=True).then_inc(sem("iota_ready"), 1)
            pool.wait_ge(sem("pool_memset"), 1)
            nc.gpsimd.affine_select(out=ident[:, :], in_=ident[:, :], compare_op=ALU.not_equal, fill=1.0, base=0,
                                    pattern=[[-1, 128]], channel_multiplier=1).then_inc(sem("ident_ready"), 1)
            nc.gpsimd.memset(cq[:, :, :, :], 0.0).then_inc(sem("cq_cleared"), 1)
            pool.wait_ge(sem("band_ready"), 1)
            pool.dma_start(band_d, cband[:, :].rearrange("h (a m) -> h a m", a=1).to_broadcast([HEADS, 128, 384])
                           ).then_inc(sem("band_stored"), 16)
            pool.wait_ge(sem("band_stored"), 16)
            pool.dma_start(cbias[:, :, :], bass.AP(band_d.tensor, 127, [[383, 128], [128 * 384, HEADS], [1, T]])
                           ).then_inc(sem("bias_ready"), 16)
            pool.wait_ge(sem("c_done"), 1)
            nc.gpsimd.memset(glu[:, :, 0:CONV_K - 1], 0.0).then_inc(sem("glu_padded"), 1)
            nc.gpsimd.memset(ain[:, :, 0:PAD], 0.0).then_inc(sem("ain_padded"), 1)
            pool.wait_ge(sem("d_done"), 1)
            pool.dma_start(sguw[:, :, :].rearrange("p h n -> p (h n)"), sgu_wt).then_inc(sem("sguw_loaded"), 16)
            pool.dma_start(sgub[:, :, :].rearrange("p h n -> p (h n)"), sgu_b.partition_broadcast(128)
                           ).then_inc(sem("sgub_loaded"), 16)
            pool.wait_ge(sem("sguw_loaded"), 16)
            nc.gpsimd.affine_select(out=sguw[:, :, :], in_=sguw[:, :, :], compare_op=ALU.is_ge, fill=0.0, base=0,
                                    pattern=[[0, WC], [1, 128]], channel_multiplier=-1
                                    ).then_inc(sem("sguw_masked"), 1)
            pool.wait_ge(sem("b_done"), 1)
            pool.dma_start(cnt[:, :, :].rearrange("p g n -> p (g n)"), inv_cnt.partition_broadcast(128)
                           ).then_inc(sem("cnt_loaded"), 16)
            pool.wait_ge(mm_done, FIRST["w_out"])
            pool.dma_start(xagain[:, :, :].rearrange("p k n -> p (k n)"), xt).then_inc(sem("xagain_loaded"), 16)
            pool.wait_ge(sem("norm_lo"), turn("lo", "h1"))
            nc.gpsimd.memset(xpad[:, :, 0:CONV2_K - 1], 0.0).then_inc(sem("xpad_ready"), 1)
            nc.gpsimd.memset(cmask[:, :], 0.0).then_inc(sem("cmask_cleared"), 1)
            pool.wait_ge(sem("cmask_cleared"), 1)
            nc.gpsimd.affine_select(out=cmask[:, :], in_=cmask[:, :], compare_op=ALU.is_ge, fill=NEG, base=0,
                                    pattern=[[-1, 128]], channel_multiplier=1).then_inc(sem("cmask_ready"), 1)
            pool.wait_ge(sem("cb_copied"), 2)
            nc.gpsimd.affine_select(out=cb[:, :, 0:256], in_=cb[:, :, 0:256], compare_op=ALU.is_ge, fill=0.0, base=0,
                                    pattern=[[0, 2], [1, 256]], channel_multiplier=-1).then_inc(sem("cb_masked"), 1)
            nc.gpsimd.affine_select(out=cb[:, :, 256:384], in_=cb[:, :, 256:384], compare_op=ALU.is_ge, fill=0.0,
                                    base=0, pattern=[[0, 2], [1, 128]], channel_multiplier=-1
                                    ).then_inc(sem("cb_masked"), 1)
            pool.wait_ge(sem("norm_lo"), turn("lo", "s1"))
            nc.gpsimd.memset(fq[:, :, :, :], 0.0).then_inc(sem("fq_cleared"), 1)
            pool.wait_ge(sem("f_done"), 1)
            pool.dma_start(pk[:, :, :].rearrange("p k n -> p (k n)"), keys).then_inc(sem("keys_loaded"), 16)
            for i in range(8):
                pool.wait_ge(sem("stage_full"), 8 * (i + 1))
                pool.dma_start(gate_d[:, :, 512 * i:512 * i + 512].rearrange("e p n -> p e n"),
                               gstage[i % 2][:, :, :, :].rearrange("p e t i -> p e (t i)")
                               ).then_inc(sem(f"gate_stored{i % 2}"), 16)
            for i in range(2):
                pool.wait_ge(sem(f"gate_stored{i}"), 64)
            for e in range(SLICES):
                if e:
                    pool.wait_ge(sem("u_gated"), 16 * e)
                pool.dma_start(gslice[:, :, :].rearrange("p t i -> p (t i)"), gate_d[e]).then_inc(sem("gate_loaded"), 16)

        @block.tensor
        def _(pe):
            pe.wait_ge(sem("onehot_loaded"), 32)
            nc.tensor.matmul(bank(7)[0:16, 0:128], relb_sb[:, :], onehot_b[:, :], start=True,
                             stop=True).then_inc(sem("band_product"), 1)
            pe.wait_ge(sem("xlo_ready"), 1)
            def by_x(b, i, g):
                product(pe, b, xhi, xlo)
            pst = Steps(pe, sem("pe_steps"))
            for name in ("c_kv", "c_q", "c_gate"):
                blocks(pe, pst, FIRST[name], COUNT[name], by_x)
            wait_evacuated(pe, "c_gate")
            pe.wait_ge(sem("ident_ready"), 1)
            for j in range(NT):
                ins = nc.tensor.transpose(bank(4 + 3 * j)[:, 0:128], ckv[:, 1, 128 * j:128 * j + 128], ident[:, :])
            ins.then_inc(sem("cv_turned"), 1)
            pe.wait_ge(sem("cvtok_ready"), 1)
            pe.wait_ge(sem("bias_ready"), 16)
            def band(c, par, qt):
                h = 2 * c + par
                return [(ident[:, :], cbias[:, h, 128:256] if qt == 0 else cbias[:, h, :], 0, 128 if qt == 0 else 256)]
            attend_pe(pe, "c", cq, ckv, lambda c: 0, lambda j, c: cvtok[:, j, :], cprob, cprobT, band)
            for name in ("d_val", "d_act", "d_gate", "b_v", "b_u", "b_gate", "a_in", "a_gate"):
                blocks(pe, pst, FIRST[name], COUNT[name], by_x)
            pe.wait_ge(sem("conv_done"), 1)
            norm_pe(pe, "d", dacc, dsq, WC, lambda e: e.wait_ge(sem("ones_ready"), 1))
            def b_ready(e):
                e.wait_ge(sem("d_done"), 1)
                wait_evacuated(e, "b_gate")
            norm_pe(pe, "b", bv, bsq, WC, b_ready)
            pe.wait_ge(sem("norm_out"), turn("out", "b"))
            for r in range(4):
                for h in range(2):
                    for j in range(NT):
                        ins = nc.tensor.transpose(bank(4 + r)[:, 256 * h + 128 * j:256 * h + 128 * j + 128],
                                                  bv[:, 2 * r + h, 128 * j:128 * j + 128], ident[:, :])
                ins.then_inc(sem("bv_turned"), 1)
            pe.wait_ge(sem("sguw_masked"), 1)
            for r in range(4):
                pe.wait_ge(sem("vtok_ready"), r + 1)
                for h in range(2):
                    for j in range(NT):
                        hh = 2 * r + h
                        ins = nc.tensor.matmul(bank(4 + r)[:, 256 * h + 128 * j:256 * h + 128 * j + 128],
                                               vtok[:, j, 128 * hh:128 * hh + 128], sguw[:, hh, :],
                                               start=True, stop=True)
                ins.then_inc(sem("b_spatial"), 1)
            pe.wait_ge(sem("mixlo_ready"), 1)
            b = Block(FIRST["a_pool"])
            pe.wait_ge(lo_done, b.count(1))
            for i in range(WC):
                o = bank(4 + i // 2)[:, T * (i % 2):T * (i % 2) + T]
                for k in range(2):
                    w, r = 2 * i + k, 2 * (i // 2) + k
                    nc.tensor.matmul(o, whi[b.half][:, w, :], mixhi[:, r, :], start=k == 0, stop=False)
                    nc.tensor.matmul(o, whi[b.half][:, w, :], mixlo[:, r, :], start=False, stop=False)
                    ins = nc.tensor.matmul(o, wlo[b.half][:, w, :], mixhi[:, r, :], start=False, stop=k == 1)
            ins.then_inc(mm_done, 1)
            def merging(b, i, g):
                j = i % 6
                if j < 4:
                    product(pe, b, xhi, xlo)
                    return
                for h in range(2):
                    y = (YA, YB, YC, YD)[2 * (j - 4) + h]
                    product(pe, b, yhi[y], ylo[y], ks=range(8 * h, 8 * h + 8), cols=T * h, first=h == 0, last=h == 1)
            pe.wait_ge(sem("a_done"), 1)
            blocks(pe, pst, FIRST["merge"], 96, merging, unit=12)
            pe.wait_ge(sem("merged"), 16)
            blocks(pe, pst, FIRST["w_out"], 16, lambda b, i, g: product(pe, b, mhi, mlo))
            norm_pe(pe, "x1", zsum, sq16, KC, lambda e: wait_evacuated(e, "w_out"))
            norm_pe(pe, "h1", x1, sq16, KC, None, centre=False)
            pe.wait_ge(sem("norm_lo"), turn("lo", "h1"))
            for name in ("dtf", "z", "xbc"):
                blocks(pe, pst, FIRST[name], COUNT[name], by_x)
            pe.wait_ge(sem("cum_ready"), 1)
            for i, src in enumerate((cum, dtfs)):
                for j in range(NT):
                    ins = nc.tensor.transpose(bank(6)[:, 256 * i + 128 * j:256 * i + 128 * j + 128],
                                              src[:, 128 * j:128 * j + 128], ident[:, :])
            ins.then_inc(sem("cum_turned"), 1)

            def turn_chunks(name, src):
                for r in range(4):
                    for h in range(2):
                        for j in range(NT):
                            ins = nc.tensor.transpose(bank(4 + r)[:, 256 * h + 128 * j:256 * h + 128 * j + 128],
                                                      src[:, 2 * r + h, 128 * j:128 * j + 128], ident[:, :])
                    ins.then_inc(sem(name), 1)
            pe.wait_ge(sem("cumT_ready"), 1)
            pe.wait_ge(sem("xconv_ready"), 1)
            turn_chunks("xs_turned", xconv)
            pe.wait_ge(sem("xtok_ready"), 4)
            for g in range(2):
                B, C, o = xconv[:, 8 + g, :], xconv[:, 10 + g, :], bank(4 + g)
                nc.tensor.matmul(o[:, 0:256], B[:, 0:128], C, start=True, stop=True)
                nc.tensor.matmul(o[:, 256:384], B[:, 128:256], C[:, 128:256], start=True,
                                 stop=True).then_inc(sem("cb_product"), 1)
            pe.wait_ge(sem("cb_copied"), 2)

            def head_row(h):
                if h >= 2:
                    pe.wait_ge(sem("ssd_diff"), h - 1)
                nc.tensor.matmul(bank(4 + h % 2)[:, 0:T], ident[:, h:h + 1].to_broadcast([128, 128]), cum[:, :],
                                 start=True, stop=True).then_inc(sem("ssd_row"), 1)
            head_row(0)
            head_row(1)
            for h in range(HEADS):
                if h >= 2:
                    pe.wait_ge(sem("ssd_out"), h - 1)
                pe.wait_ge(sem("ssd_mat"), h + 1)
                c, m, o = h // 2, dec[h % 2], bank(6 + h % 2)
                nc.tensor.matmul(o[:, 0:256], xtok[:, 0, 128 * c:128 * c + 128], m[:, 0:256], start=True, stop=False)
                nc.tensor.matmul(o[:, 128:256], xtok[:, 1, 128 * c:128 * c + 128], m[:, 256:384], start=False,
                                 stop=True).then_inc(sem("ssd_y"), 1)
                if h + 2 < HEADS:
                    head_row(h + 2)
            for g in range(2):
                norm_pe(pe, f"s{g}", None, ssq, 4, None, centre=False)
            for name in ("fq", "fk", "fv"):
                blocks(pe, pst, FIRST[name], COUNT[name], by_x)
            wait_evacuated(pe, "fv")
            turn_chunks("fv_turned", fv)
            pe.wait_ge(sem("fvtok_ready"), 4)
            pe.wait_ge(sem("cmask_ready"), 1)

            def forgetting(c, par, qt):
                f = 32 + 2 * c + par
                w = 128 + 128 * qt
                return [(cum[:, 128 * qt:128 * qt + 128], ident[:, f:f + 1].to_broadcast([128, w]), 0, w),
                        (ident[:, f:f + 1].to_broadcast([128, 128]), ncum[:, 0:w], 0, w),
                        (ident[:, :], cmask[:, :], w - 128, w)]
            attend_pe(pe, "f", fq, fk, lambda c: c, lambda j, c: fvtok[:, j, 128 * c:128 * c + 128], fprob, fprobT,
                      forgetting)
            pe.wait_ge(sem("f_done"), 1)
            blocks(pe, pst, FIRST["w_out2"], 16, lambda b, i, g: product(pe, b, mhi, mlo))
            norm_pe(pe, "h2", x1, sq16, KC, None, centre=False)
            pe.wait_ge(sem("norm_lo"), turn("lo", "h2"))
            blocks(pe, pst, FIRST["wq"], 16, by_x)
            wait_evacuated(pe, "wq")
            pe.wait_ge(sem("keys_loaded"), 16)
            for n in range(8):
                j, q = n // 4, n % 4
                if n >= 4:
                    pe.wait_ge(sem("scores_out"), n - 3)
                for i in range(4):
                    hs = 4 * q + i
                    ins = nc.tensor.matmul(bank(4 + n % 4)[:, 128 * i:128 * i + 128], pq[:, hs, 128 * j:128 * j + 128],
                                           pk[:, hs, :], start=True, stop=True)
                ins.then_inc(sem("scores_ready"), 1)
            pe.wait_ge(sem("chosen_ready"), 1)
            for i in range(3):
                for j in range(NT):
                    ins = nc.tensor.transpose(bank(4 + i)[:, 128 * j:128 * j + 128],
                                              chosen[i][:, 8 * j:8 * j + 8, :].rearrange("p h k -> p (h k)"), ident[:, :])
            ins.then_inc(sem("chosen_turned"), 1)
            with pst.loop(8, 0) as g:
                for i in range(8):
                    pe.wait_ge(sem("onehots"), 8 * g + i + 1)
                    pe.wait_ge(sem("bank_free"), 8 * g + i + 1)
                    for t in range(4):
                        ins = nc.tensor.matmul(bank(4 + i % 4)[:, 128 * t:128 * t + 128], one2[i % 2][:, t, :],
                                               one1[i % 2][:, t, :], start=True, stop=True)
                    ins.then_inc(sem("gate_product"), 1)

            def slice_pe(e):
                def upward(b, i, g):
                    product(pe, b, xhi, xlo)
                expert_blocks(pe, pst, e, 0, upward)
                def downward(b, i, g):
                    pe.wait_ge(sem("ag_lo"), e * 16 + 16)
                    product(pe, b, aghi, aglo)
                expert_blocks(pe, pst, e, 16, downward)
            with pst.loop(SLICES - 1, 0) as e:
                slice_pe(e)
            slice_pe(SLICES - 1)
            norm_pe(pe, "fin", x1, sq16, KC, None, centre=False)

        @block.vector
        def _(dve):
            st = Steps(dve, sem("dve_steps"))
            dve.sem_inc(sem("sig_used"), 2)
            nc.vector.memset(csmall[:, :], 0.0)
            dve.wait_ge(sem("band_product"), 1)
            dve.wait_ge(sem("band_cleared"), 1)
            nc.vector.tensor_copy(cband[:, 128:256], bank(7)[0:16, 0:128]).then_inc(sem("band_ready"), 1)
            dve.wait_ge(sem("x_loaded"), 16)
            dve.wait_ge(sem("xhi_ready"), 1)
            nc.vector.tensor_tensor(xlo[:, :, :], xraw[:, :, :], xhi[:, :, :].bitcast(f32),
                                    ALU.subtract).then_inc(sem("xlo_ready"), 1)
            for n in range(SPLIT):
                split_lo(dve, Block(n))

            def lo_only(b, i, g):
                if exists(b.count(SPLIT)):
                    split_lo(dve, b.ahead(SPLIT))
            for name in ("c_kv", "c_q", "c_gate"):
                blocks(dve, st, FIRST[name], COUNT[name], lo_only)
            dve.wait_ge(sem("cv_turned"), 1)
            nc.vector.tensor_copy(cvtok[:, 0, :], bank(4)[:, 0:128])
            nc.vector.tensor_copy(cvtok[:, 1, :], bank(7)[:, 0:128]).then_inc(sem("cvtok_ready"), 1)
            dve.wait_ge(sem("vec_loaded"), 16)
            attend_dve(dve, st, "c", cprob, csmall, co, cgate, True, 6)
            dve.wait_ge(sem("c_hi"), 1)
            nc.vector.tensor_tensor(ylo[YC][:, :, :], co[:, :, :], yhi[YC][:, :, :].bitcast(f32),
                                    ALU.subtract).then_inc(sem("c_done"), 1)
            blocks(dve, st, FIRST["d_val"], COUNT["d_val"], lo_only)

            def glu_gate(b, i, g):
                lo_only(b, i, g)
                dve.wait_ge(evacuated[b.bank], b.uses())
                dst = chunk(glu, b.index(FIRST["d_act"]))[:, CONV_K - 1:]
                nc.vector.tensor_tensor(dst, dst, sig[b.n0 % 2][:, :], ALU.mult).then_inc(sem("sig_used"), 1)
            blocks(dve, st, FIRST["d_act"], COUNT["d_act"], glu_gate)
            blocks(dve, st, FIRST["d_gate"], COUNT["d_gate"], lo_only)

            def taps(i, c):
                acc = chunk(dacc, c)
                g = chunk(glu, c)
                for k in range(8 * i, min(8 * i + 8, CONV_K)):
                    w = vec[:, bass.ds(c * CONV_K + (VCOL["conv_w"] + k), 1)]
                    if k == 0:
                        st.link(nc.vector.tensor_scalar(acc, g[:, 0:T], w, vec[:, bass.ds(c + VCOL["conv_b"], 1)],
                                                        ALU.mult, ALU.add))
                    else:
                        st.link(nc.vector.scalar_tensor_tensor(acc, g[:, k:k + T], w, acc, ALU.mult, ALU.add))

            def conv_body(base, mult):
                def body(b, i, g):
                    lo_only(b, i, g)
                    if mult:
                        j = b.index(FIRST["b_gate"])
                        dve.wait_ge(evacuated[b.bank], b.uses())
                        dst = chunk(bug, j)
                        nc.vector.tensor_tensor(dst, dst, sig[b.n0 % 2][:, :], ALU.mult).then_inc(sem("sig_used"), 1)
                    taps(i % 4, g + base)
                return body
            blocks(dve, st, FIRST["b_v"], 16, conv_body(0, False), per_turn=CONV_K)
            blocks(dve, st, FIRST["b_gate"], 8, conv_body(4, True), per_turn=CONV_K)
            blocks(dve, st, FIRST["a_in"], 8, conv_body(6, False), per_turn=CONV_K)
            dve.sem_inc(sem("conv_done"), 1)
            blocks(dve, st, FIRST["a_gate"], COUNT["a_gate"], lo_only)
            norm_dve(dve, st, "d", dacc, WC, stat, LN_EPS)
            dve.wait_ge(sem("norm_out"), turn("out", "d"))
            nc.vector.tensor_tensor(dacc[:, :, :], dacc[:, :, :], dgate[:, :, :], ALU.mult).then_inc(sem("d_gated"), 1)
            dve.wait_ge(sem("d_hi"), 1)
            nc.vector.tensor_tensor(ylo[YD][:, :, :], dacc[:, :, :], yhi[YD][:, :, :].bitcast(f32),
                                    ALU.subtract).then_inc(sem("d_done"), 1)
            norm_dve(dve, st, "b", bv, WC, stat, LN_EPS)
            for r in range(4):
                dve.wait_ge(sem("bv_turned"), r + 1)
                nc.vector.tensor_copy(
                    vtok[:, :, 256 * r:256 * r + 256].rearrange("p j (h d) -> p h j d", h=2),
                    bank(4 + r)[:, :].rearrange("p (h j d) -> p h j d", h=2, j=NT)).then_inc(sem("vtok_ready"), 1)
            dve.wait_ge(sem("sgub_loaded"), 16)
            for r in range(4):
                dve.wait_ge(sem("b_spatial"), r + 1)
                t = bsq[:, 2 * r:2 * r + 2, :]
                for h in range(2):
                    bias_h = sgub[:, 2 * r + h, :].rearrange("p (a n) -> p a n", a=1).to_broadcast([128, NT, 128])
                    ins = nc.vector.tensor_tensor(bsq[:, 2 * r + h, :].rearrange("p (j n) -> p j n", j=NT),
                                                  bank(4 + r)[:, T * h:T * h + T].rearrange("p (j n) -> p j n", j=NT),
                                                  bias_h, ALU.add)
                st.link(ins)
                last = nc.vector.tensor_tensor(bug[:, 2 * r:2 * r + 2, :], bug[:, 2 * r:2 * r + 2, :], t, ALU.mult)
            last.then_inc(sem("b_gated"), 1)
            dve.wait_ge(sem("b_hi"), 1)
            nc.vector.tensor_tensor(ylo[YB][:, :, :], bug[:, :, :], yhi[YB][:, :, :].bitcast(f32),
                                    ALU.subtract).then_inc(sem("b_done"), 1)
            L = T + PAD
            wait_evacuated(dve, "a_gate")
            st.link(nc.vector.tensor_tensor(win_a[:, :, 1:L], ain[:, :, 1:L], ain[:, :, 0:L - 1], ALU.add))
            st.link(nc.vector.tensor_tensor(win_b[:, :, 3:L], win_a[:, 2:8, 3:L], win_a[:, 2:8, 1:L - 2], ALU.add))
            st.link(nc.vector.tensor_tensor(win_a[:, 4:8, 7:L], win_b[:, 2:6, 7:L], win_b[:, 2:6, 3:L - 4], ALU.add))
            st.link(nc.vector.tensor_tensor(win_b[:, 4:6, 15:L], win_a[:, 6:8, 15:L], win_a[:, 6:8, 7:L - 8], ALU.add))
            dve.wait_ge(sem("cnt_loaded"), 16)
            for g, src in enumerate((win_a[:, 0:2, PAD:], win_b[:, 0:2, PAD:], win_a[:, 4:6, PAD:],
                                     win_b[:, 4:6, PAD:])):
                by = cnt[:, g, :].rearrange("p (a n) -> p a n", a=1).to_broadcast([128, 2, T])
                ins = nc.vector.tensor_tensor(src, src, by, ALU.mult)
                st.link(ins)
                dst = ain[:, 2 * g:2 * g + 2, PAD:]
                last = nc.vector.tensor_tensor(dst, src, dst, ALU.subtract)
            last.then_inc(sem("mix_ready"), 1)
            dve.wait_ge(sem("mixhi_ready"), 1)
            nc.vector.tensor_tensor(mixlo[:, :, :], ain[:, :, PAD:], mixhi[:, :, :].bitcast(f32),
                                    ALU.subtract).then_inc(sem("mixlo_ready"), 1)
            b = Block(FIRST["a_pool"])
            lo_only(b, 0, 0)
            dve.wait_ge(mm_done, b.count(1))
            for i in range(WC):
                st.link(nc.vector.scalar_tensor_tensor(win_a[:, i, 0:T], bank(4 + i // 2)[:, T * (i % 2):T * (i % 2) + T],
                                                       vcol("pool_scale", i), agate[:, i, :], ALU.mult, ALU.mult))
            dve.sem_inc(evacuated[b.bank], 1)
            dve.sem_inc(sem("a_gated"), 1)
            dve.wait_ge(sem("a_hi"), 1)
            nc.vector.tensor_tensor(ylo[YA][:, :, :], win_a[:, :, 0:T], yhi[YA][:, :, :].bitcast(f32),
                                    ALU.subtract).then_inc(sem("a_done"), 1)
            def merging(b, i, g):
                lo_only(b, i, g)
                j, m = i % 6, i // 6
                if j < 4:
                    return
                part = msum[0] if j == 4 else msum[1]
                dve.wait_ge(mm_done, b.count(1))
                o = bank(b.bank)[:, :].rearrange("p (h n) -> p h n", h=2)
                st.link(nc.vector.tensor_tensor(gates[m][:, 2 * (j - 4):2 * (j - 4) + 2, :], o,
                                                gates[m][:, 2 * (j - 4):2 * (j - 4) + 2, :], ALU.mult))
                ins = nc.vector.tensor_tensor(part[:, :], gates[m][:, 2 * (j - 4), :], gates[m][:, 2 * (j - 4) + 1, :],
                                              ALU.add)
                ins.then_inc(evacuated[b.bank], 1)
                if j == 5:
                    dve.wait_ge(evacuated[b.bank], b.uses())
                    dve.sem_inc(sem("gates_free"), 1)
                    col = 2 * g + m
                    nc.vector.tensor_tensor(msum[0][:, :], msum[0][:, :], msum[1][:, :], ALU.add
                                            ).then_inc(sem("merge_sum"), 1)
                    dve.wait_ge(sem("mhi_done"), col + 1)
                    nc.vector.tensor_tensor(chunk(mlo, col), msum[0][:, :], chunk(mhi, col).bitcast(f32),
                                            ALU.subtract).then_inc(sem("merged"), 1)
            dve.sem_inc(sem("gates_free"), 2)
            blocks(dve, st, FIRST["merge"], 96, merging, per_turn=4, unit=12)
            dve.wait_ge(sem("xagain_loaded"), 16)

            def residual(b, i, g):
                lo_only(b, i, g)
                j = b.index(FIRST["w_out"])
                dve.wait_ge(mm_done, b.count(1))
                nc.vector.scalar_tensor_tensor(chunk(zsum, j), chunk(xagain, j), ALPHA, bank(b.bank)[:, 0:T],
                                               ALU.mult, ALU.add).then_inc(evacuated[b.bank], 1)
            blocks(dve, st, FIRST["w_out"], 16, residual)
            norm_dve(dve, st, "x1", zsum, KC, st16, LN_EPS)
            norm_dve(dve, st, "h1", x1, KC, st16, RMS_EPS, centre=False, scale=False)

            def rms_split(name, src, r, gain, n, dhi, dlo, tmp, j0=0, c0=0):
                for c in range(n):
                    st.link(nc.vector.scalar_tensor_tensor(tmp[:, c, :], src[:, c, :], vcol(gain, c0 + c), r[:, :],
                                                           ALU.mult, ALU.mult))
                dve.sem_inc(sem("norm_scaled"), 1)
                dve.wait_ge(sem("norm_hi"), turn("hi", name))
                nc.vector.tensor_tensor(dlo[:, j0:j0 + n, :], tmp[:, 0:n, :], dhi[:, j0:j0 + n, :].bitcast(f32),
                                        ALU.subtract).then_inc(sem("norm_lo"), 1)
            rms_split("h1", x1, st16[2], "ln1_w", KC, xhi, xlo, zsum)
            b = Block(FIRST["dtf"])
            y, u, w1, lg = dtt
            lo_only(b, 0, 0)
            dve.wait_ge(mm_done, b.count(1))
            ins = nc.vector.tensor_scalar(y[:, :], bank(b.bank)[:, 0:T], vcol("dtf_bias"), vcol("dtf_sign"), ALU.add,
                                          ALU.mult)
            ins.then_inc(evacuated[b.bank], 1)
            dve.wait_ge(evacuated[b.bank], b.uses())
            nc.vector.scalar_tensor_tensor(u[:, :], y[:, :], -1.0, y[:, :], ALU.mult, ALU.max).then_inc(sem("dt_abs"), 1)
            dve.wait_ge(sem("dt_exp"), 1)
            nc.vector.tensor_scalar(w1[:, :], u[:, :], 1.0, None, ALU.add).then_inc(sem("dt_one"), 1)
            dve.wait_ge(sem("dt_log"), 1)
            st.link(nc.vector.tensor_scalar(cum[:, :], w1[:, :], -1.0, None, ALU.add))
            st.link(nc.vector.tensor_tensor(u[:, :], u[:, :], cum[:, :], ALU.subtract))
            st.link(nc.vector.reciprocal(w1[:, :], w1[:, :]))
            st.link(nc.vector.tensor_tensor(u[:, :], u[:, :], w1[:, :], ALU.mult))
            st.link(nc.vector.tensor_tensor(lg[:, :], lg[:, :], u[:, :], ALU.add))
            st.link(nc.vector.scalar_tensor_tensor(dtfs[:, :], y[:, :], 0.0, lg[:, :], ALU.max, ALU.add))
            dve.wait_ge(sem("acol_exp"), 1)
            st.link(nc.vector.tensor_scalar(acol[:, 1:2], acol[:, 0:1], -1.0, None, ALU.mult))
            st.link(nc.vector.tensor_scalar(u[:, :], dtfs[:, :], acol[:, 1:2], None, ALU.mult))
            st.link(nc.vector.memset(w1[:, :], 1.0))
            st.link(nc.vector.tensor_tensor_scan(cum[:, :], w1[:, :], u[:, :], 0.0, ALU.mult, ALU.add))
            nc.vector.tensor_scalar(ncum[:, :], cum[:, :], -1.0, None, ALU.mult).then_inc(sem("cum_ready"), 1)
            for name in ("z", "xbc"):
                blocks(dve, st, FIRST[name], COUNT[name], lo_only)
            dve.wait_ge(sem("cum_turned"), 1)
            nc.vector.tensor_copy(cumT[:, :, :], bank(6)[:, 0:256])
            nc.vector.tensor_copy(dtT[:, :, :], bank(6)[:, 256:512]).then_inc(sem("cumT_ready"), 1)
            dve.wait_ge(sem("cumT_ready"), 1)
            dve.wait_ge(sem("xpad_ready"), 1)
            wait_evacuated(dve, "xbc")
            with st.loop(12, CONV2_K) as c:
                acc, src = chunk(xconv, c), chunk(xpad, c)
                for k in range(CONV2_K):
                    w = vec[:, bass.ds(c * CONV2_K + (VCOL["conv2_w"] + k), 1)]
                    if k == 0:
                        st.link(nc.vector.tensor_scalar(acc, src[:, 0:T], w, vec[:, bass.ds(c + VCOL["conv2_b"], 1)],
                                                        ALU.mult, ALU.add))
                    else:
                        st.link(nc.vector.scalar_tensor_tensor(acc, src[:, k:k + T], w, acc, ALU.mult, ALU.add))
            dve.sem_inc(sem("conv2_done"), 1)
            for r in range(4):
                dve.wait_ge(sem("xs_turned"), r + 1)
                for h in range(2):
                    c = 2 * r + h
                    ins = nc.vector.tensor_tensor(
                        xtok[:, :, 128 * c:128 * c + 128].rearrange("p j (a d) -> p j a d", a=2),
                        bank(4 + r)[:, 256 * h:256 * h + 256].rearrange("p (j a d) -> p j a d", j=NT, a=2),
                        dtT[:, :, 2 * c:2 * c + 2].rearrange("p j (a d) -> p j a d", d=1).to_broadcast([128, NT, 2, 64]),
                        ALU.mult)
                ins.then_inc(sem("xtok_ready"), 1)
            for g in range(2):
                dve.wait_ge(sem("cb_product"), g + 1)
                nc.vector.tensor_copy(cb[:, g, :], bank(4 + g)[:, 0:384]).then_inc(sem("cb_copied"), 1)
            dve.wait_ge(sem("cb_masked"), 2)
            for grp in range(2):
                with st.loop(4, 2) as c4:
                    c = c4 + 4 * grp
                    for par in range(2):
                        h = c * 2 + par
                        m = dec[par]
                        dve.wait_ge(sem("ssd_row"), h + 1)
                        nc.vector.tensor_scalar(m[:, 0:256], bank(4 + par)[:, 0:256], cumT[:, 0, bass.ds(h, 1)], 0.0,
                                                ALU.subtract, ALU.min)
                        nc.vector.tensor_scalar(m[:, 256:384], bank(4 + par)[:, 128:256], cumT[:, 1, bass.ds(h, 1)],
                                                0.0, ALU.subtract, ALU.min).then_inc(sem("ssd_diff"), 1)
                    for par in range(2):
                        h = c * 2 + par
                        dve.wait_ge(sem("ssd_decay"), h + 1)
                        nc.vector.tensor_tensor(dec[par][:, :], dec[par][:, :], cb[:, grp, :], ALU.mult
                                                ).then_inc(sem("ssd_mat"), 1)
                    for par in range(2):
                        h = c * 2 + par
                        p0, p1 = 64 * par, 64 * par + 64
                        dve.wait_ge(sem("ssd_y"), h + 1)
                        xc = xconv[p0:p1, bass.ds(c, 1), :].rearrange("p a n -> p (a n)")
                        yy = yssd[p0:p1, bass.ds(c, 1), :].rearrange("p a n -> p (a n)")
                        zz = zg[p0:p1, bass.ds(c, 1), :].rearrange("p a n -> p (a n)")
                        ins = nc.vector.scalar_tensor_tensor(yy, xc, vec[p0:p1, bass.ds(c + VCOL["d_skip"], 1)],
                                                             bank(6 + par)[p0:p1, 0:T], ALU.mult, ALU.add)
                        ins.then_inc(sem("ssd_out"), 1)
                        dve.wait_ge(sem("ssd_out"), h + 1)
                        st.link(nc.vector.tensor_tensor(yy, yy, zz, ALU.mult))
            dve.sem_inc(sem("ssd_gated"), 1)
            for g in range(2):
                norm_dve(dve, st, f"s{g}", None, 4, sst, RMS_EPS, centre=False, scale=False)
                rms_split(f"s{g}", yssd[:, 4 * g:4 * g + 4, :], sst[2], "ssd_norm", 4, mhi, mlo,
                          xconv[:, 4 * g:4 * g + 4, :], j0=4 * g, c0=4 * g)
            for name in ("fq", "fk", "fv"):
                blocks(dve, st, FIRST[name], COUNT[name], lo_only)
            for r in range(4):
                dve.wait_ge(sem("fv_turned"), r + 1)
                nc.vector.tensor_copy(
                    fvtok[:, :, 256 * r:256 * r + 256].rearrange("p j (h d) -> p h j d", h=2),
                    bank(4 + r)[:, :].rearrange("p (h j d) -> p h j d", h=2, j=NT)).then_inc(sem("fvtok_ready"), 1)
            attend_dve(dve, st, "f", fprob, fsmall, fo, None, False, 4)
            dve.wait_ge(sem("f_hi"), 1)
            nc.vector.tensor_tensor(mlo[:, 8:16, :], fo[:, :, :], mhi[:, 8:16, :].bitcast(f32),
                                    ALU.subtract).then_inc(sem("f_done"), 1)

            def add_x1(b, i, g, base=FIRST["w_out2"]):
                lo_only(b, i, g)
                j = b.index(base) if base is not None else i
                dve.wait_ge(mm_done, b.count(1))
                nc.vector.tensor_tensor(chunk(x1, j), chunk(x1, j), bank(b.bank)[:, 0:T], ALU.add
                                        ).then_inc(evacuated[b.bank], 1)
            blocks(dve, st, FIRST["w_out2"], 16, add_x1)
            norm_dve(dve, st, "h2", x1, KC, st16, RMS_EPS, centre=False, scale=False)
            rms_split("h2", x1, st16[2], "ln2_w", KC, xhi, xlo, zsum)
            blocks(dve, st, FIRST["wq"], 16, lo_only)
            def best16(n, values, vals, idx, ready):
                for r in range(n):
                    ready(r)
                    ins = nc.vector.max(vals[:, r, 0:8], values[:, r, :])
                st.link(ins)
                for r in range(n):
                    ins = nc.vector.max_index(idx[:, r, 0:8], vals[:, r, 0:8], values[:, r, :])
                st.link(ins)
                for r in range(n):
                    ins = nc.vector.match_replace(values[:, r, :], vals[:, r, 0:8], values[:, r, :], LOWEST)
                st.link(ins)
                for r in range(n):
                    ins = nc.vector.max(vals[:, r, 8:16], values[:, r, :])
                st.link(ins)
                for r in range(n):
                    ins = nc.vector.max_index(idx[:, r, 8:16], vals[:, r, 8:16], values[:, r, :])
                st.link(ins)

            def scores_out(r):
                if r % 4 == 0:
                    dve.wait_ge(sem("scores_out"), r // 4 + 1)
            best16(NT * KC, ps_[:, :, :, :].rearrange("p j h n -> p (j h) n"), top, topi, scores_out)
            st.link(nc.vector.tensor_copy(topf[:, :, :], topi[:, :, :]))
            pair = top[:, :, :].rearrange("p (r s) a -> p r s a", s=2)
            for r0 in (0, 8):
                first = pair[:, r0:r0 + 8, 0, :].rearrange("p r (a b) -> p r a b", b=1).to_broadcast([128, 8, 16, 16])
                second = pair[:, r0:r0 + 8, 1, :].rearrange("p r (a b) -> p r a b", a=1).to_broadcast([128, 8, 16, 16])
                ins = nc.vector.tensor_tensor(cand[:, r0:r0 + 8, :].rearrange("p r (a b) -> p r a b", a=16), first,
                                              second, ALU.add)
            st.link(ins)
            best16(KC, cand, best, besti, lambda r: None)
            st.link(nc.vector.tensor_scalar(slot_i[0][:, :, :], besti[:, :, :], 4, None, ALU.logical_shift_right))
            st.link(nc.vector.tensor_scalar(slot_i[1][:, :, :], besti[:, :, :], 15, None, ALU.bitwise_and))
            idx = topf[:, :, :].rearrange("p (r s) a -> p r s a", s=2)
            for i in range(2):
                st.link(nc.vector.tensor_copy(slot_f[i][:, :, :], slot_i[i][:, :, :]))
                for r0 in (0, 8):
                    h4 = hit[:, r0:r0 + 8, :].rearrange("p r (k a) -> p r k a", k=16)
                    st.link(nc.vector.tensor_tensor(
                        h4, slot_f[i][:, r0:r0 + 8, :].rearrange("p r (k a) -> p r k a", a=1).to_broadcast([128, 8, 16, 16]),
                        iota[:, 0:16].rearrange("p (r k a) -> p r k a", r=1, k=1).to_broadcast([128, 8, 16, 16]),
                        ALU.is_equal))
                    st.link(nc.vector.tensor_tensor(
                        h4, h4, idx[:, r0:r0 + 8, i, :].rearrange("p r (k a) -> p r k a", k=1).to_broadcast([128, 8, 16, 16]),
                        ALU.mult))
                st.link(nc.vector.reduce_sum(chosen[i][:, :, :], hit[:, :, :].rearrange("p r (k a) -> p r k a", k=16),
                                             AX.X))
            st.link(nc.vector.tensor_tensor(best[:, :, 1:16], best[:, :, 1:16],
                                            best[:, :, 0:1].to_broadcast([128, KC, 15]), ALU.subtract))
            st.link(nc.vector.tensor_tensor(best[:, :, 0:1], best[:, :, 0:1], best[:, :, 0:1], ALU.subtract))
            dve.sem_inc(sem("best_shifted"), 1)
            dve.wait_ge(sem("best_exp"), 1)
            st.link(nc.vector.reduce_sum(gsum[:, :], best[:, :, :], AX.X))
            st.link(nc.vector.reciprocal(gsum[:, :], gsum[:, :]))
            nc.vector.tensor_tensor(chosen[2][:, :, :], best[:, :, :],
                                    gsum[:, :].rearrange("p (r a) -> p r a", a=1).to_broadcast([128, KC, 16]),
                                    ALU.mult).then_inc(sem("chosen_ready"), 1)
            dve.wait_ge(sem("chosen_turned"), 1)
            for i in range(3):
                st.link(nc.vector.tensor_copy(chosenT[i][:, :], bank(4 + i)[:, 0:T]))
            dve.sem_inc(sem("chosenT_ready"), 1)
            with st.loop(8, 0) as g:
                for i in range(8):
                    dve.wait_ge(sem("onehot_free"), 8 * g + i + 1)
                    for t in range(4):
                        tok = bass.ds(g * 32 + (4 * i + t), 1)
                        nc.vector.tensor_scalar(one1[i % 2][:, t, :], iota[:, :], chosenT[0][:, tok],
                                                chosenT[2][:, tok], ALU.is_equal, ALU.mult)
                        ins = nc.vector.tensor_scalar(one2[i % 2][:, t, :], iota[:, :], chosenT[1][:, tok], None,
                                                      ALU.is_equal)
                    ins.then_inc(sem("onehots"), 1)

            def slice_dve(e):
                def upward(b, i, g):
                    lo_only(b, i, g)
                    dve.wait_ge(sem("gate_loaded"), e * 16 + 16)
                    p = b.n0 % 2
                    dve.wait_ge(evacuated[b.bank], b.uses())
                    nc.vector.tensor_tensor(gated[p][:, :], gelu[p][:, :],
                                            gslice[:, :, bass.ds(i, 1)].rearrange("p t a -> p (t a)"), ALU.mult
                                            ).then_inc(sem("u_gated"), 1)
                    dve.wait_ge(sem("ag_hi"), e * 16 + i + 1)
                    nc.vector.tensor_tensor(chunk(aglo, i), gated[p][:, :], chunk(aghi, i).bitcast(f32), ALU.subtract
                                            ).then_inc(sem("ag_lo"), 1)
                expert_blocks(dve, st, e, 0, upward)
                expert_blocks(dve, st, e, 16, lambda b, i, g: add_x1(b, i, g, None))
            with st.loop(SLICES - 1, 0) as e:
                slice_dve(e)
            slice_dve(SLICES - 1)
            norm_dve(dve, st, "fin", x1, KC, fst, RMS_EPS, centre=False, scale=False)
            for c in range(KC):
                ins = nc.vector.scalar_tensor_tensor(zsum[:, c, :], x1[:, c, :], vcol("lnf_w", c), fst[2][:, :],
                                                     ALU.mult, ALU.mult)
                ins.then_inc(sem("out_ready"), 1)

        @block.scalar
        def _(act):
            st = Steps(act, sem("act_steps"))
            act.dma_start(onehot_b[:, :], buckets).then_inc(sem("onehot_loaded"), 16)
            act.dma_start(relb_sb[:, :], relb).then_inc(sem("onehot_loaded"), 16)
            act.dma_start(vec[:, :], vecs).then_inc(sem("vec_loaded"), 16)
            act.wait_ge(sem("x_loaded"), 16)
            nc.scalar.copy(xhi[:, :, :], xraw[:, :, :]).then_inc(sem("xhi_ready"), 1)
            for n in range(SPLIT):
                split_hi(act, Block(n))

            def evac(first, put):
                def body(b, i, g):
                    if exists(b.count(SPLIT)):
                        split_hi(act, b.ahead(SPLIT))
                    act.wait_ge(mm_done, b.count(1))
                    put(bank(b.bank)[:, 0:T], b.index(first), b)
                return body

            def to(buf, func=ACT.Copy, off=0):
                def put(ps, j, b):
                    nc.scalar.activation(chunk(buf, j)[:, off:off + T], ps, func).then_inc(evacuated[b.bank], 1)
                return put

            def run(name, put):
                blocks(act, st, FIRST[name], COUNT[name], evac(FIRST[name], put))

            run("c_kv", to(ckv))
            act.wait_ge(sem("cq_cleared"), 1)

            def put_q(q):
                def put(ps, j, b):
                    for par in range(2):
                        p0, p1 = 64 * par, 64 * par + 64
                        dst = q[p0:p1, par, :, :]
                        dst = dst[:, j, :] if isinstance(j, int) else \
                            dst[:, bass.ds(j, 1), :].rearrange("p a n -> p (a n)")
                        ins = nc.scalar.mul(dst, ps[p0:p1, :], 0.125)
                    ins.then_inc(evacuated[b.bank], 1)
                return put
            run("c_q", put_q(cq))
            run("c_gate", to(cgate, ACT.Silu))
            act.wait_ge(sem("vec_loaded"), 16)
            attend_act(act, "c", cprob, cprobT, csmall, True)
            act.wait_ge(sem("c_o"), 2 * WC)
            nc.scalar.copy(yhi[YC][:, :, :], co[:, :, :]).then_inc(sem("c_hi"), 1)
            act.wait_ge(sem("glu_padded"), 1)
            act.wait_ge(sem("c_done"), 1)
            run("d_val", to(glu, off=CONV_K - 1))

            def put_sig(func, used0):
                def put(ps, j, b):
                    act.wait_ge(sem("sig_used"), j + used0 + 1)
                    nc.scalar.activation(sig[b.n0 % 2][:, :], ps, func).then_inc(evacuated[b.bank], 1)
                return put
            run("d_act", put_sig(ACT.Sigmoid, 0))
            run("d_gate", to(dgate, ACT.Silu))
            run("b_v", to(bv))
            run("b_u", to(bug))
            run("b_gate", put_sig(ACT.Silu, 8))
            run("a_in", to(ain, off=PAD))
            act.wait_ge(sem("conv_done"), 1)
            run("a_gate", to(agate, ACT.Silu))
            norm_act(act, "d", dacc, dsq, stat)
            affine_act(act, "d", dacc, WC, "conv_ln_g", "conv_ln_b", ACT.Silu)
            act.wait_ge(sem("d_gated"), 1)
            nc.scalar.copy(yhi[YD][:, :, :], dacc[:, :, :]).then_inc(sem("d_hi"), 1)
            norm_act(act, "b", bv, bsq, stat)
            affine_act(act, "b", bv, WC, "sgu_ln_g", "sgu_ln_b", ACT.Identity)
            act.wait_ge(sem("b_gated"), 1)
            nc.scalar.copy(yhi[YB][:, :, :], bug[:, :, :]).then_inc(sem("b_hi"), 1)
            act.wait_ge(sem("mix_ready"), 1)
            nc.scalar.copy(mixhi[:, :, :], ain[:, :, PAD:]).then_inc(sem("mixhi_ready"), 1)
            if exists(FIRST["a_pool"] + SPLIT):
                split_hi(act, Block(FIRST["a_pool"] + SPLIT))
            act.wait_ge(sem("a_gated"), 1)
            act.wait_ge(mm_done, FIRST["a_pool"] + 1)
            nc.scalar.copy(yhi[YA][:, :, :], win_a[:, :, 0:T]).then_inc(sem("a_hi"), 1)
            def merging(b, i, g):
                if exists(b.count(SPLIT)):
                    split_hi(act, b.ahead(SPLIT))
                j, m = i % 6, i // 6
                if j < 4:
                    act.wait_ge(mm_done, b.count(1))
                    if j == 0:
                        act.wait_ge(sem("gates_free"), 2 * g + m + 1)
                    nc.scalar.activation(gates[m][:, j, :], bank(b.bank)[:, 0:T], ACT.Sigmoid
                                         ).then_inc(evacuated[b.bank], 1)
                elif j == 5:
                    col = 2 * g + m
                    act.wait_ge(sem("merge_sum"), col + 1)
                    nc.scalar.copy(chunk(mhi, col), msum[0][:, :]).then_inc(sem("mhi_done"), 1)
            blocks(act, st, FIRST["merge"], 96, merging, unit=12)

            def hi_only(b, i, g):
                if exists(b.count(SPLIT)):
                    split_hi(act, b.ahead(SPLIT))
            blocks(act, st, FIRST["w_out"], 16, hi_only)
            norm_act(act, "x1", zsum, sq16, st16)
            act.wait_ge(sem("norm_normed"), turn("normed", "x1"))
            for c in range(KC):
                ins = nc.scalar.activation(x1[:, c, :], zsum[:, c, :], ACT.Identity, bias=vcol("ln_b", c),
                                           scale=vcol("ln_g", c))
            ins.then_inc(sem("norm_out"), 1)
            norm_act(act, "h1", x1, sq16, st16, lambda e: e.wait_ge(sem("norm_out"), turn("out", "x1")), centre=False)
            act.wait_ge(sem("norm_scaled"), turn("scaled", "h1"))
            nc.scalar.copy(xhi[:, :, :], zsum[:, :, :]).then_inc(sem("norm_hi"), 1)
            nc.scalar.activation(acol[:, 0:1], vcol("a_log"), ACT.Exp).then_inc(sem("acol_exp"), 1)
            hi_only(Block(FIRST["dtf"]), 0, 0)
            act.wait_ge(sem("dt_abs"), 1)
            nc.scalar.activation(dtt[1][:, :], dtt[1][:, :], ACT.Exp, scale=-1.0).then_inc(sem("dt_exp"), 1)
            act.wait_ge(sem("dt_one"), 1)
            nc.scalar.activation(dtt[3][:, :], dtt[2][:, :], ACT.Ln).then_inc(sem("dt_log"), 1)
            run("z", to(zg, ACT.Silu))
            run("xbc", to(xpad, off=CONV2_K - 1))
            act.wait_ge(sem("conv2_done"), 1)
            nc.scalar.activation(xconv[:, :, :], xconv[:, :, :], ACT.Silu).then_inc(sem("xconv_ready"), 1)
            with act.Fori(0, WC) as c:
                for par in range(2):
                    act.wait_ge(sem("ssd_diff"), c * 2 + par + 1)
                    nc.scalar.activation(dec[par][:, :], dec[par][:, :], ACT.Exp).then_inc(sem("ssd_decay"), 1)
            for g in range(2):
                norm_act(act, f"s{g}", yssd[:, 4 * g:4 * g + 4, :], ssq, sst,
                         lambda e: e.wait_ge(sem("ssd_gated"), 1), centre=False)
                act.wait_ge(sem("norm_scaled"), turn("scaled", f"s{g}"))
                nc.scalar.copy(mhi[:, 4 * g:4 * g + 4, :], xconv[:, 4 * g:4 * g + 4, :]).then_inc(sem("norm_hi"), 1)
            act.wait_ge(sem("fq_cleared"), 1)
            run("fq", put_q(fq))
            run("fk", to(fk))
            run("fv", to(fv))
            attend_act(act, "f", fprob, fprobT, fsmall, False)
            act.wait_ge(sem("f_o"), HEADS)
            nc.scalar.copy(mhi[:, 8:16, :], fo[:, :, :]).then_inc(sem("f_hi"), 1)
            blocks(act, st, FIRST["w_out2"], 16, hi_only)
            norm_act(act, "h2", x1, sq16, st16, lambda e: wait_evacuated(e, "w_out2"), centre=False)
            act.wait_ge(sem("norm_scaled"), turn("scaled", "h2"))
            nc.scalar.copy(xhi[:, :, :], zsum[:, :, :]).then_inc(sem("norm_hi"), 1)
            run("wq", to(pq))
            for n in range(8):
                act.wait_ge(sem("scores_ready"), n + 1)
                nc.scalar.copy(ps_[:, n // 4, 4 * (n % 4):4 * (n % 4) + 4, :], bank(4 + n % 4)[:, :]
                               ).then_inc(sem("scores_out"), 1)
            act.wait_ge(sem("best_shifted"), 1)
            nc.scalar.activation(best[:, :, :], best[:, :, :], ACT.Exp).then_inc(sem("best_exp"), 1)
            act.wait_ge(sem("chosenT_ready"), 1)
            act.sem_inc(sem("bank_free"), 4)
            act.sem_inc(sem("onehot_free"), 2)
            for half in range(8):
                if half >= 2:
                    act.wait_ge(sem(f"gate_stored{half % 2}"), 16 * (half // 2))
                for i in range(8):
                    act.wait_ge(sem("gate_product"), 8 * half + i + 1)
                    act.sem_inc(sem("onehot_free"), 1)
                    nc.scalar.copy(gstage[half % 2][:, :, 4 * i:4 * i + 4, :],
                                   bank(4 + i % 4)[:, :].rearrange("p (t e i) -> p e t i", t=4, e=SLICES)
                                   ).then_inc(sem("stage_full"), 1)
                    act.wait_ge(sem("stage_full"), 8 * half + i + 1)
                    act.sem_inc(sem("bank_free"), 1)
            for i in range(2):
                act.wait_ge(sem(f"gate_stored{i}"), 64)

            def slice_act(e):
                def upward(b, i, g):
                    if exists(b.count(SPLIT)):
                        split_hi(act, b.ahead(SPLIT))
                    p = b.n0 % 2
                    act.wait_ge(mm_done, b.count(1))
                    nc.scalar.activation(gelu[p][:, :], bank(b.bank)[:, 0:T], ACT.Gelu).then_inc(evacuated[b.bank], 1)
                    act.wait_ge(sem("u_gated"), e * 16 + i + 1)
                    nc.scalar.copy(chunk(aghi, i), gated[p][:, :]).then_inc(sem("ag_hi"), 1)
                expert_blocks(act, st, e, 0, upward)
                expert_blocks(act, st, e, 16, hi_only)
            with st.loop(SLICES - 1, 0) as e:
                slice_act(e)
            slice_act(SLICES - 1)
            norm_act(act, "fin", x1, sq16, fst, lambda e: wait_evacuated(e, "experts"), centre=False)


def layout(x, w_in, pool_w, pool_scale, sgu_ln_g, sgu_ln_b, sgu_w, sgu_b, attn_sinks, rel_bias, conv_w, conv_b,
           conv_ln_g, conv_ln_b, w_branch, w_out, ln_g, ln_b, ln1_w_2, w_in_2, conv_w_2, conv_b_2, dt_bias_2,
           a_log_2, d_skip_2, ssd_norm_w_2, fox_f_bias_2, w_out_2, ln2_w_2, peer_wq_2, peer_k1_2, peer_k2_2,
           peer_u_2, peer_v_2, lnf_w_2):
    f = np.float32
    stream = np.empty((NBLOCKS, 128, KC * 128), f)

    def put(name, w):
        n = w.shape[1] // 128
        assert n == COUNT[name]
        stream[FIRST[name]:FIRST[name] + n] = w.reshape(KC, 128, n, 128).transpose(2, 1, 0, 3).reshape(n, 128, -1)

    def pairs(w):
        return w.reshape(*w.shape[:-1], 2, 8, 64).swapaxes(-3, -2).reshape(*w.shape[:-1], 1024)

    w = w_in[0]
    at = 0
    for name, n in [("a_in", 1024), ("a_gate", 1024), ("b_u", 1024), ("b_v", 1024), ("b_gate", 1024),
                    ("c_q", 1024), ("c_kv", 256), ("c_gate", 1024), ("d_val", 1024), ("d_act", 1024),
                    ("d_gate", 1024)]:
        cols = w[:, at:at + n]
        put(name, pairs(cols) if name in ("c_q", "c_gate") else cols)
        at += n
    merge = stream[FIRST["merge"]:FIRST["merge"] + 96].reshape(16, 6, 128, 2048)
    merge[:, 0:4] = w[:, at:].reshape(KC, 128, 4, 16, 128).transpose(3, 2, 1, 0, 4).reshape(16, 4, 128, 2048)
    wb = [w_branch[0, 0], w_branch[0, 1], pairs(w_branch[0, 2].T).T, w_branch[0, 3]]
    for i in range(4):
        merge[:, 4 + i // 2].reshape(16, 128, 2, 1024)[:, :, i % 2] = \
            wb[i].reshape(8, 128, 16, 128).transpose(2, 1, 0, 3).reshape(16, 128, 1024)
    stream[FIRST["a_pool"]] = pool_w[0].reshape(4, 2, 128, 2, 128).transpose(2, 0, 3, 1, 4).reshape(128, 2048)
    put("w_out", w_out[0])
    w = w_in_2
    put("z", w[:, 0:1024])
    put("xbc", w[:, 1024:2560])
    dtf = np.zeros((D, 128), f)
    dtf[:, 0:16], dtf[:, 32:48] = w[:, 2560:2576], w[:, 5648:5664]
    put("dtf", dtf)
    for i, name in enumerate(("fq", "fk", "fv")):
        put(name, w[:, 2576 + 1024 * i:3600 + 1024 * i])
    put("w_out2", w_out_2)
    put("wq", peer_wq_2)
    ex = stream[FIRST["experts"]:].reshape(SLICES, 2, 16, 128, 2048)
    ex[:, 0] = peer_u_2.reshape(SLICES, 16, 128, KC, 128).transpose(0, 1, 4, 3, 2).reshape(SLICES, 16, 128, 2048)
    ex[:, 1] = peer_v_2.reshape(SLICES, 16, 128, 16, 128).transpose(0, 3, 2, 1, 4).reshape(SLICES, 16, 128, 2048)

    vecs = np.zeros((128, NVEC), f)

    def vput(name, a):
        vecs[:, VCOL[name]:VCOL[name] + a.shape[1]] = a

    for name, a in [("pool_scale", pool_scale[0]), ("sgu_ln_g", sgu_ln_g[0]), ("sgu_ln_b", sgu_ln_b[0]),
                    ("conv_b", conv_b[0]), ("conv_ln_g", conv_ln_g[0]), ("conv_ln_b", conv_ln_b[0]),
                    ("ln_g", ln_g[0]), ("ln_b", ln_b[0]), ("ln1_w", ln1_w_2), ("conv2_b", conv_b_2),
                    ("ssd_norm", ssd_norm_w_2), ("ln2_w", ln2_w_2), ("lnf_w", lnf_w_2)]:
        vput(name, a.reshape(-1, 128).T)
    vput("conv_w", conv_w[0].reshape(CONV_K, 8, 128).transpose(2, 1, 0).reshape(128, -1))
    vput("conv2_w", conv_w_2.reshape(CONV2_K, 12, 128).transpose(2, 1, 0).reshape(128, -1))
    vput("d_skip", np.repeat(d_skip_2.reshape(8, 2).T, 64, axis=0))
    vput("sinks", np.broadcast_to(attn_sinks[0].reshape(2, 8).T.reshape(1, 16), (128, 16)))
    vecs[0:16, VCOL["dtf_bias"]], vecs[32:48, VCOL["dtf_bias"]] = dt_bias_2, fox_f_bias_2
    vecs[0:16, VCOL["dtf_sign"]], vecs[32:48, VCOL["dtf_sign"]] = 1.0, -1.0
    vecs[0:16, VCOL["a_log"]] = a_log_2
    dist = 127 - np.arange(128)
    large = 16 + (np.log(np.maximum(dist, 1).astype(f) / 16) / np.log(8.0) * 16).astype(np.int32)
    buckets = (np.where(dist < 16, dist, np.minimum(large, 31))[None, :] == np.arange(32)[:, None]).astype(f)
    count = np.minimum(np.arange(T)[None, :] + 1, np.array([2, 4, 8, 16])[:, None])
    return {
        "stream": stream,
        "xt": x[0].reshape(T, KC, 128).transpose(2, 1, 0).reshape(128, -1),
        "vecs": vecs,
        "sgu_wt": sgu_w[0].transpose(2, 0, 1).reshape(128, -1),
        "sgu_b": sgu_b[0].reshape(-1),
        "relb": rel_bias.reshape(32, 2, 8).transpose(0, 2, 1).reshape(32, 16),
        "buckets": buckets,
        "keys": np.stack([peer_k1_2, peer_k2_2], axis=1).transpose(3, 0, 1, 2).reshape(128, -1),
        "inv_cnt": (1.0 / count).astype(f).reshape(-1),
    }


def kernel(**inputs):
    import concourse.bacc as bacc
    from concourse.bass_utils import run_bass_kernel_spmd

    nc = bacc.Bacc("TRN2", target_bir_lowering=False, num_devices=1)
    arrays = {n: np.ascontiguousarray(a) for n, a in layout(**{n: np.asarray(a) for n, a in inputs.items()}).items()}
    args = {n: nc.dram_tensor(n, a.shape, mybir.dt.from_np(a.dtype), kind="ExternalInput").ap()
            for n, a in arrays.items()}
    out = nc.dram_tensor("out", (128, KC * T), mybir.dt.float32, kind="ExternalOutput").ap()
    build(nc, out=out, **args)
    r = run_bass_kernel_spmd(nc, [arrays], core_ids=[0])
    got = r.results[0]["out"]
    return got.reshape(128, KC, T).transpose(2, 1, 0).reshape(1, T, D)
```

```python
import numpy as np
from contextlib import ExitStack

import concourse.bass as bass
from concourse import mybir

T = 256
NT = T // 128
D = 2048
KC = D // 128
WC = 1024 // 128
CONV_K = 31
CONV2_K = 4
HEADS = 16
TOPK = 16
PEER_HEADS = 8
KEYS = 128
RAW = 4
SPLIT = 2
BANKS = 4
NEG = -1e30
LOWEST = -3.0e38
ALPHA = 2.0 ** 0.25
LN_EPS = 1e-5
RMS_EPS = 1e-6

ORDER = [("c_kv", 2), ("c_q", 8), ("c_gate", 8), ("d_val", 8), ("d_act", 8), ("d_gate", 8),
         ("b_v", 8), ("b_u", 8), ("b_gate", 8), ("a_in", 8), ("a_gate", 8), ("a_pool", 1),
         ("merge", 96), ("w_out", 16), ("dtf", 1), ("z", 8), ("xbc", 12), ("fk", 8), ("fv", 8),
         ("fq", 8), ("w_out2", 16), ("wq", 16), ("experts", 256)]
FIRST, NBLOCKS = {}, 0
for _name, _count in ORDER:
    FIRST[_name] = NBLOCKS
    NBLOCKS += _count
COUNT = dict(ORDER)
SLICES = 8

VECS = [("pool_scale", 8), ("sgu_ln_g", 8), ("sgu_ln_b", 8), ("conv_b", 8), ("conv_ln_g", 8),
        ("conv_ln_b", 8), ("conv_w", 8 * CONV_K), ("ln_g", 16), ("ln_b", 16), ("ln1_w", 16),
        ("conv2_w", 12 * CONV2_K), ("conv2_b", 12), ("d_skip", 8), ("ssd_norm", 8), ("ln2_w", 16),
        ("lnf_w", 16), ("sinks", 16), ("dtf_bias", 1), ("dtf_sign", 1), ("a_log", 1)]
VCOL, NVEC = {}, 0
for _name, _count in VECS:
    VCOL[_name] = NVEC
    NVEC += _count


NORMS = ["d", "b", "x1", "h1", "s0", "s1", "h2", "fin"]
TAKING_PART = {"sum": ["d", "b", "x1"], "centred": ["d", "b"], "normed": ["d", "b"], "out": ["d", "b"],
               "squared": ["d", "b", "s0", "s1"], "scaled": ["s0", "s1"], "hi": ["s0", "s1"], "lo": ["s0", "s1"]}


def turn(step, name):
    return TAKING_PART.get(step, NORMS).index(name) + 1


class Block:

    def __init__(self, n0, q=0):
        self.n0, self.q = n0, q
        self.raw, self.half, self.bank = n0 % RAW, n0 % SPLIT, n0 % BANKS

    def count(self, more=0):
        return self.n0 + more + 4 * self.q

    def uses(self, more=0):
        return self.n0 // 4 + 1 + more + self.q

    def ahead(self, k):
        return Block(self.n0 + k, self.q)

    def index(self, base):
        return self.n0 - base + 4 * self.q


class Steps:

    def __init__(self, eng, sem):
        self.eng, self.sem, self.n, self.turn = eng, sem, 0, None

    def link(self, ins):
        ins.then_inc(self.sem, 1)
        self.n += 1
        self.eng.wait_ge(self.sem, self.n if self.turn is None else self.n + self.turn)

    def loop(self, count, per_turn):
        return _StepsLoop(self, count, per_turn)


class _StepsLoop:
    def __init__(self, steps, count, per_turn):
        self.steps, self.count, self.per_turn = steps, count, per_turn

    def __enter__(self):
        self.fori = self.steps.eng.Fori(0, self.count)
        g = self.fori.__enter__()
        self.outer, self.start = self.steps.turn, self.steps.n
        if self.per_turn:
            self.steps.turn = g * self.per_turn if self.outer is None else self.outer + g * self.per_turn
        return g

    def __exit__(self, *e):
        if e[0] is None:
            assert self.steps.n - self.start == self.per_turn, (self.steps.n - self.start, self.per_turn)
        self.steps.turn = self.outer
        self.steps.n = self.start + self.count * self.per_turn
        return self.fori.__exit__(*e)


def blocks(eng, steps, first, count, body, per_turn=0, unit=4):
    n, left = first, count
    while left and n < 4:
        body(Block(n), n - first, 0)
        n, left = n + 1, left - 1
    turns = left // unit
    if n + turns * unit + SPLIT > NBLOCKS:
        turns -= 1
    if turns > 1:
        with steps.loop(turns, per_turn) as g:
            for i in range(unit):
                body(Block(n + i, g * (unit // 4)), n - first + i, g)
        n, left = n + turns * unit, left - turns * unit
    while left:
        body(Block(n), n - first, 0)
        n, left = n + 1, left - 1


def build(nc, stream, xt, vecs, sgu_wt, sgu_b, relb, buckets, keys, inv_cnt, out):
    f32, f32r, u32 = mybir.dt.float32, mybir.dt.float32r, mybir.dt.uint32
    ALU, ACT, AX = mybir.AluOpType, mybir.ActivationFunctionType, mybir.AxisListType

    KB = 1024
    origin = -(-nc.sbuf_base // 32) * 32
    RING = origin + 4 * KB
    XAT = RING + 64 * KB
    ARENA = XAT + 32 * KB

    def at(name, shape, offset, dtype=f32):
        return nc.alloc_sbuf_tensor_at(name, shape, dtype, offset=int(offset))

    def ar(name, shape, kb, dtype=f32):
        return at(name, shape, ARENA + kb * KB, dtype)

    vec = at("vec", [128, NVEC], origin)
    ident = at("ident", [128, 128], origin + 2 * KB)
    ones = at("ones", [128, 128], origin + 2 * KB + 512)
    iota = at("iota", [128, 128], origin + 3 * KB)
    raw = [at(f"raw{i}", [128, KC, 128], RING + 8 * KB * i) for i in range(RAW)]
    whi = [at(f"whi{i}", [128, KC, 128], RING + (32 + 8 * i) * KB, f32r) for i in range(SPLIT)]
    wlo = [at(f"wlo{i}", [128, KC, 128], RING + (48 + 8 * i) * KB, f32r) for i in range(SPLIT)]
    xhi = at("xhi", [128, KC, T], XAT, f32r)
    xlo = at("xlo", [128, KC, T], XAT + 16 * KB, f32r)

    yhi = [ar(f"yhi{i}", [128, WC, T], 16 * i, f32r) for i in range(4)]
    ylo = [ar(f"ylo{i}", [128, WC, T], 16 * i + 8, f32r) for i in range(4)]
    xraw = ar("xraw", [128, KC, T], 0)
    cq = ar("cq", [128, 2, WC, T], 64)
    cbias = ar("cbias", [128, HEADS, T], 80)
    cgate = ar("cgate", [128, WC, T], 96)
    ckv = ar("ckv", [128, 2, T], 104)
    cvtok = ar("cvtok", [128, NT, 128], 106)
    cprob = [ar(f"cprob{i}", [128, 3, 128], 32 + 2 * i) for i in range(2)]
    cprobT = [ar(f"cprobT{i}", [128, 3, 128], 36 + 2 * i) for i in range(2)]
    co = ar("co", [128, WC, T], 40)
    csmall = ar("csmall", [128, 64], 31)
    cband = ar("cband", [16, 384], 28)
    onehot_b = ar("onehot_b", [32, 128], 26)
    relb_sb = ar("relb_sb", [32, 16], 27)
    glu = ar("glu", [128, WC, T + CONV_K - 1], 0)
    dacc = ar("dacc", [128, WC, T], 73.25)
    dgate = ar("dgate", [128, WC, T], 81.25)
    bv = ar("bv", [128, WC, T], 89.25)
    bug = ar("bug", [128, WC, T], 97.25)
    PAD = 16
    ain = ar("ain", [128, WC, T + PAD], 64)
    agate = ar("agate", [128, WC, T], 0)
    sig = [ar(f"sig{i}", [128, T], 10 + i) for i in range(2)]
    dsq = ar("dsq", [128, WC, T], 32)
    bsq = ar("bsq", [128, WC, T], 16)
    stat = [ar(f"stat{i}", [128, T], 24 + i) for i in range(6)]
    vtok = ar("vtok", [128, NT, 1024], 73.25)
    sguw = ar("sguw", [128, WC, 128], 81.25)
    sgub = ar("sgub", [128, WC, 128], 85.25)
    win_a = ar("win_a", [128, WC, T + PAD], 72.5)
    win_b = ar("win_b", [128, WC - 2, T + PAD], 81)
    cnt = ar("cnt", [128, 4, T], 87.5)
    mixhi = ar("mixhi", [128, WC, T], 91.5, f32r)
    mixlo = ar("mixlo", [128, WC, T], 99.5, f32r)
    mhi = ar("mhi", [128, KC, T], 64, f32r)
    mlo = ar("mlo", [128, KC, T], 80, f32r)

    gates = [ar(f"gates{i}", [128, 4, T], 96 + 4 * i) for i in range(2)]
    msum = [ar(f"msum{i}", [128, T], 104 + i) for i in range(2)]
    zsum = ar("zsum", [128, KC, T], 0)
    xagain = ar("xagain", [128, KC, T], 16)
    x1 = ar("x1", [128, KC, T], 32)
    sq16 = ar("sq16", [128, KC, T], 48)
    st16 = [ar(f"st16_{i}", [128, T], 96 + i) for i in range(5)]
    zg = ar("zg", [128, WC, T], 0)
    xpad = ar("xpad", [128, 12, T + CONV2_K - 1], 8)
    xconv = ar("xconv", [128, 12, T], 48)
    xtok = ar("xtok", [128, NT, 1024], 21)
    dtfs = ar("dtfs", [128, T], 96)
    cum = ar("cum", [128, T], 97)
    ncum = ar("ncum", [128, T], 98)
    cumT = ar("cumT", [128, NT, 128], 99)
    dtT = ar("dtT", [128, NT, 128], 100)
    acol = ar("acol", [128, 8], 101)
    cmask = ar("cmask", [128, 128], 101.5)
    cb = ar("cb", [128, 2, 384], 29)
    dec = [ar(f"dec{i}", [128, 384], 60 + 1.5 * i) for i in range(2)]
    dtt = [ar(f"dtt{i}", [128, T], 102 + i) for i in range(4)]
    yssd = ar("yssd", [128, WC, T], 8)
    sst = [ar(f"sst{i}", [128, T], 102 + i) for i in range(5)]
    ssq = ar("ssq", [128, 4, T], 60)
    fq = [ar(f"fq{i}", [128, WC, T], 16 * i) for i in range(2)]
    fk = ar("fk", [128, WC, T], 72)
    fv = ar("fv", [128, WC, T], 88)
    fvtok = ar("fvtok", [128, NT, 1024], 56)
    fprob = [ar(f"fprob{i}", [128, 3, 128], 24 + 1.5 * i) for i in range(2)]
    fprobT = [ar(f"fprobT{i}", [128, 3, 128], 27 + 1.5 * i) for i in range(2)]
    fsmall = ar("fsmall", [128, 64], 30)
    fo = ar("fo", [128, WC, T], 48)

    pq = ar("pq", [128, KC, T], 0)
    pk = ar("pk", [128, KC, 128], 16)
    ps_ = ar("ps_", [128, NT, KC, 128], 48)
    cand = ar("cand", [128, KC, 256], 64)
    hit = ar("hit", [128, KC, 256], 48)
    top = ar("top", [128, NT * KC, TOPK], 96)
    topi = ar("topi", [128, NT * KC, TOPK], 98, u32)
    topf = ar("topf", [128, NT * KC, TOPK], 100)
    best = ar("best", [128, KC, TOPK], 102)
    besti = ar("besti", [128, KC, TOPK], 103, u32)
    slot_i = [ar(f"slot_i{i}", [128, KC, TOPK], 104 + i, u32) for i in range(2)]
    slot_f = [ar(f"slot_f{i}", [128, KC, TOPK], 24 + i) for i in range(2)]
    chosen = [ar(f"chosen{i}", [128, KC, TOPK], 26 + i) for i in range(3)]
    gsum = ar("gsum", [128, KC], 106)
    chosenT = [ar(f"chosenT{i}", [128, T], 29 + i) for i in range(3)]
    one1 = [ar(f"one1_{i}", [128, 4, 128], 16 + 2 * i) for i in range(4)]
    one2 = [ar(f"one2_{i}", [128, 4, 128], 96 + 2 * i) for i in range(4)]
    gstage = [ar(f"gstage{i}", [128, SLICES, 32, 16], 64 - 16 * i) for i in range(2)]
    gslice = ar("gslice", [128, T, 16], 48)
    uact = [ar(f"uact{i}", [128, 16, T], 80 * i) for i in range(2)]
    aghi = [ar(f"aghi{i}", [128, 16, T], 64 - 48 * i, f32r) for i in range(2)]
    aglo = [ar(f"aglo{i}", [128, 16, T], 80 * i, f32r) for i in range(2)]
    gelu = [ar(f"gelu{i}", [128, T], 99 + i) for i in range(2)]
    gated = [ar(f"gated{i}", [128, T], 101 + i) for i in range(2)]
    fst = [ar(f"fst{i}", [128, T], 99 + i) for i in range(5)]

    def bank(i):
        return pb[i]

    es = ExitStack()
    with es:
        pb = [es.enter_context(nc.psum_tensor(f"bank{i}", [128, 512], f32)) for i in range(8)]
        made = {}

        def sem(name):
            if name not in made:
                made[name] = es.enter_context(nc.semaphore(name))
            return made[name]

        def vcol(name, i=0, p0=0, p1=128):
            return vec[p0:p1, VCOL[name] + i:VCOL[name] + i + 1]

        def chunk(buf, j):
            if isinstance(j, int):
                return buf[:, j, :]
            return buf[:, bass.ds(j, 1), :].rearrange("p a n -> p (a n)")

        def spread(tile, n):
            return tile[:, :].rearrange("p (a n) -> p a n", a=1).to_broadcast([128, n, T])

        hi_done, lo_done, mm_half, mm_done = sem("hi_done"), sem("lo_done"), sem("mm_half"), sem("mm_done")
        raw_loaded = [sem(f"raw_loaded{i}") for i in range(RAW)]
        evacuated = [sem(f"evacuated{i}") for i in range(BANKS)]

        def exists(n):
            return not isinstance(n, int) or n < NBLOCKS

        def load(sp, b):
            if b.n0 >= RAW:
                sp.wait_ge(lo_done, 2 * b.count(1 - RAW))
            sp.dma_start(raw[b.raw][:, :, :].rearrange("p k c -> p (k c)"),
                         stream[bass.ds(b.count(), 1)].rearrange("a p n -> (a p) n")
                         ).then_inc(raw_loaded[b.raw], 16)

        def split_hi(act, b, halves=(0, 1)):
            for h in halves:
                k = slice(8 * h, 8 * h + 8)
                if h == 0:
                    act.wait_ge(raw_loaded[b.raw], 16 * b.uses())
                if b.n0 >= SPLIT:
                    act.wait_ge(mm_done if h else mm_half, b.count(1 - SPLIT))
                nc.scalar.copy(whi[b.half][:, k, :], raw[b.raw][:, k, :]).then_inc(hi_done, 1)

        def split_lo(dve, b, halves=(0, 1)):
            for h in halves:
                k = slice(8 * h, 8 * h + 8)
                dve.wait_ge(hi_done, 2 * b.count() + h + 1)
                nc.vector.tensor_tensor(wlo[b.half][:, k, :], raw[b.raw][:, k, :],
                                        whi[b.half][:, k, :].bitcast(f32), ALU.subtract).then_inc(lo_done, 1)

        def product(pe, b, rhi, rlo, ks=range(KC), k0=0, cols=0, first=True, last=True, ready=None):
            if first and b.n0 >= BANKS:
                pe.wait_ge(evacuated[b.bank], b.uses(-1))
            o = bank(b.bank)[:, cols:cols + T]
            for i, k in enumerate(ks):
                if k % 8 == 0:
                    pe.wait_ge(lo_done, 2 * b.count() + k // 8 + 1)
                    if ready is not None:
                        ready(k // 8)
                r = k0 + i
                nc.tensor.matmul(o, whi[b.half][:, k, :], rhi[:, r, :], start=i == 0, stop=False)
                nc.tensor.matmul(o, whi[b.half][:, k, :], rlo[:, r, :], start=False, stop=False)
                ins = nc.tensor.matmul(o, wlo[b.half][:, k, :], rhi[:, r, :], start=False,
                                       stop=i == len(ks) - 1)
                if k == 7:
                    ins.then_inc(mm_half, 1)
            if last:
                ins.then_inc(mm_done, 1)

        def wait_evacuated(eng, name):
            end = FIRST[name] + COUNT[name]
            for i in range(BANKS):
                eng.wait_ge(evacuated[i], (end - 1 - i) // 4 + 1)

        def wait_early_gelu(eng, e):
            end = FIRST["experts"] + 16 * (e + 1)
            for i in range(BANKS):
                eng.wait_ge(evacuated[i], (end - 1 - i) // 4 + 1)

        EARLY = 2
        LATE = SLICES - EARLY
        U_EARLY, V_EARLY = FIRST["experts"], FIRST["experts"] + 16 * EARLY
        U_GATES, U_REST = U_EARLY + 20, U_EARLY + 28

        def expert_blocks(eng, steps, e, off, body):
            base = FIRST["experts"] + 32 * EARLY + off
            if isinstance(e, int) and off == 16:
                for i in range(16):
                    body(Block(base + 32 * e + i), i, 0)
                return
            with steps.loop(4, 0) as g:
                for i in range(4):
                    body(Block(base + i, e * 8 + g), g * 4 + i, g)

        block = es.enter_context(nc.Block())

        def norm_sum(pe, buf, n):
            for c in range(n):
                ins = nc.tensor.matmul(bank(4)[:, 0:T], ones[:, :], buf[:, c, :], start=c == 0, stop=c == n - 1)
            ins.then_inc(sem("norm_sum"), 1)

        def norm_sumsq(pe, name, sq, n):
            pe.wait_ge(sem("norm_squared"), turn("squared", name))
            for c in range(n):
                ins = nc.tensor.matmul(bank(5)[:, 0:T], ones[:, :], sq[:, c, :], start=c == 0, stop=c == n - 1)
            ins.then_inc(sem("norm_sumsq"), 1)

        def norm_pe(pe, name, buf, sq, n, ready, centre=True):
            if centre:
                ready(pe)
                norm_sum(pe, buf, n)
            norm_sumsq(pe, name, sq, n)

        def sum_chunk(pe, out_bank, buf, c, done):
            ins = nc.tensor.matmul(bank(out_bank)[:, 0:T], ones[:, :], buf[:, c, :], start=c == 0, stop=c == KC - 1)
            if c == KC - 1:
                ins.then_inc(sem(done), 1)

        def block_out(eng, n):
            eng.wait_ge(evacuated[n % BANKS], n // BANKS + 1)

        def norm_centre(dve, st, name, buf, n, mean):
            dve.wait_ge(sem("norm_sum"), turn("sum", name))
            st.link(nc.vector.tensor_scalar(mean[:, :], bank(4)[:, 0:T], 1.0 / (128 * n), None, ALU.mult))
            nc.vector.tensor_tensor(buf[:, :, :], buf[:, :, :], spread(mean, n),
                                    ALU.subtract).then_inc(sem("norm_centred"), 1)

        def norm_variance(dve, name, n, var, eps):
            dve.wait_ge(sem("norm_sumsq"), turn("sumsq", name))
            nc.vector.tensor_scalar(var[:, :], bank(5)[:, 0:T], 1.0 / (128 * n), eps, ALU.mult,
                                    ALU.add).then_inc(sem("norm_var"), 1)

        def norm_root(dve, st, name, buf, n, t, scale=True):
            mean, var, r, u, sd = t[:5]
            dve.wait_ge(sem("norm_sd"), turn("sd", name))
            st.link(nc.vector.reciprocal(r[:, :], sd[:, :]))
            st.link(nc.vector.tensor_tensor(u[:, :], r[:, :], r[:, :], ALU.mult))
            st.link(nc.vector.tensor_tensor(u[:, :], u[:, :], var[:, :], ALU.mult))
            st.link(nc.vector.tensor_scalar(u[:, :], u[:, :], -0.5, 1.5, ALU.mult, ALU.add))
            st.link(nc.vector.tensor_tensor(r[:, :], r[:, :], u[:, :], ALU.mult))
            if scale:
                nc.vector.tensor_tensor(buf[:, :, :], buf[:, :, :], spread(r, n),
                                        ALU.mult).then_inc(sem("norm_normed"), 1)

        def norm_dve(dve, st, name, buf, n, t, eps, centre=True, scale=True):
            if centre:
                norm_centre(dve, st, name, buf, n, t[0])
            norm_variance(dve, name, n, t[1], eps)
            norm_root(dve, st, name, buf, n, t, scale)

        def norm_square(act, name, buf, sq, ready=None):
            if ready is None:
                act.wait_ge(sem("norm_centred"), turn("centred", name))
            else:
                ready(act)
            nc.scalar.activation(sq[:, :, :], buf[:, :, :], ACT.Square).then_inc(sem("norm_squared"), 1)

        def norm_sqrt(act, name, t):
            act.wait_ge(sem("norm_var"), turn("var", name))
            nc.scalar.activation(t[4][:, :], t[1][:, :], ACT.Sqrt).then_inc(sem("norm_sd"), 1)

        def norm_act(act, name, buf, sq, t, ready=None, centre=True):
            norm_square(act, name, buf, sq, ready)
            norm_sqrt(act, name, t)

        def affine_act(act, name, buf, n, gain, offset, func):
            act.wait_ge(sem("norm_normed"), turn("normed", name))
            for c in range(n):
                ins = nc.scalar.activation(buf[:, c, :], buf[:, c, :], func, bias=vcol(offset, c),
                                           scale=vcol(gain, c))
            ins.then_inc(sem("norm_out"), 1)

        def attend_pe(pe, name, q, k, kchunk, vt, prob, probT, extra, beside):
            def scores(c, par):
                if c:
                    pe.wait_ge(sem(name + "_exp"), 4 * (c - 1) + 2 * par + 2)
                o, kc = bank(4 + par), kchunk(c)
                for lo, w, qt in ((0, 128, 0), (128, 256, 1)):
                    more = extra(c, par, qt)
                    nc.tensor.matmul(o[:, lo:lo + w], q[par][:, c, 128 * qt:128 * qt + 128], k[:, kc, 0:w],
                                     start=True, stop=not more)
                    for i, (l, r, a, b) in enumerate(more):
                        ins = nc.tensor.matmul(o[:, lo + a:lo + b], l, r, start=False, stop=i == len(more) - 1)
                ins.then_inc(sem(name + "_scores"), 1)

            scores(0, 0)
            scores(0, 1)
            for c in range(WC):
                for par in range(2):
                    pe.wait_ge(sem(name + "_prob"), 2 * c + par + 1)
                    if c:
                        pe.wait_ge(sem(name + "_o"), 2 * (c - 1) + par + 1)
                    for j in range(3):
                        ins = nc.tensor.transpose(bank(6 + par)[:, 128 * j:128 * j + 128], prob[par][:, j, :],
                                                  ident[:, :])
                    ins.then_inc(sem(name + "_turned"), 1)
                if c + 1 < WC:
                    scores(c + 1, 0)
                    scores(c + 1, 1)
                beside(c, 0)
                for par in range(2):
                    pe.wait_ge(sem(name + "_probT"), 2 * c + par + 1)
                    o = bank(6 + par)
                    nc.tensor.matmul(o[:, 0:128], vt(0, c), probT[par][:, 0, :], start=True, stop=True)
                    nc.tensor.matmul(o[:, 128:256], vt(0, c), probT[par][:, 1, :], start=True, stop=False)
                    nc.tensor.matmul(o[:, 128:256], vt(1, c), probT[par][:, 2, :], start=False,
                                     stop=True).then_inc(sem(name + "_sums"), 1)
                beside(c, 1)

        def attend_dve(dve, st, name, prob, small, o, gate, sinks, beside):
            def maxima(c):
                for par in range(2):
                    m = small[:, 8 * par:8 * par + 2]
                    if c:
                        dve.wait_ge(sem(name + "_exp"), 4 * (c - 1) + 2 * par + 2)
                        if sinks:
                            dve.wait_ge(sem(name + "_sink"), 2 * (c - 1) + par + 1)
                    dve.wait_ge(sem(name + "_scores"), 2 * c + par + 1)
                    nc.vector.reduce_max(m[:, 0:1], bank(4 + par)[:, 0:128], AX.X)
                    st.link(nc.vector.reduce_max(m[:, 1:2], bank(4 + par)[:, 128:384], AX.X))
                    if sinks:
                        nc.vector.tensor_scalar(small[:, 8 * par + 2:8 * par + 4], m, vcol("sinks", 2 * c + par), -1.0,
                                                ALU.max, ALU.mult).then_inc(sem(name + "_max"), 1)
                    else:
                        nc.vector.tensor_scalar(small[:, 8 * par + 2:8 * par + 4], m, -1.0, None,
                                                ALU.mult).then_inc(sem(name + "_max"), 1)
            maxima(0)
            for c in range(WC):
                for par in range(2):
                    den = small[:, 8 * par + 4:8 * par + 6]
                    dve.wait_ge(sem(name + "_exp"), 4 * c + 2 * par + 2)
                    if sinks:
                        dve.wait_ge(sem(name + "_sink"), 2 * c + par + 1)
                        st.link(nc.vector.tensor_tensor(den, den, small[:, 8 * par + 6:8 * par + 8], ALU.add))
                    st.link(nc.vector.reciprocal(den, den))
                    nc.vector.tensor_scalar(prob[par][:, 0, :], prob[par][:, 0, :], den[:, 0:1], None, ALU.mult)
                    nc.vector.tensor_scalar(prob[par][:, 1:3, :], prob[par][:, 1:3, :], den[:, 1:2], None,
                                            ALU.mult).then_inc(sem(name + "_prob"), 1)
                if c + 1 < WC:
                    maxima(c + 1)
                beside(c, 0)
                for par in range(2):
                    p0, p1 = 64 * par, 64 * par + 64
                    dve.wait_ge(sem(name + "_sums"), 2 * c + par + 1)
                    dst = o[p0:p1, c, :]
                    if gate is not None:
                        nc.vector.tensor_tensor(dst, bank(6 + par)[p0:p1, 0:T], gate[p0:p1, c, :], ALU.mult
                                                ).then_inc(sem(name + "_o"), 1)
                    else:
                        nc.vector.tensor_copy(dst, bank(6 + par)[p0:p1, 0:T]).then_inc(sem(name + "_o"), 1)
                beside(c, 1)

        def attend_act(act, name, prob, probT, small, sinks, beside):
            def exponentials(c):
                for par in range(2):
                    act.wait_ge(sem(name + "_max"), 2 * c + par + 1)
                    if c:
                        act.wait_ge(sem(name + "_turned"), 2 * (c - 1) + par + 1)
                    nm = small[:, 8 * par + 2:8 * par + 4]
                    nc.scalar.activation(prob[par][:, 0, :], bank(4 + par)[:, 0:128], ACT.Exp, bias=nm[:, 0:1],
                                         accum_out=small[:, 8 * par + 4:8 * par + 5]).then_inc(sem(name + "_exp"), 1)
                    nc.scalar.activation(prob[par][:, 1:3, :], bank(4 + par)[:, 128:384], ACT.Exp,
                                         bias=nm[:, 1:2], accum_out=small[:, 8 * par + 5:8 * par + 6]
                                         ).then_inc(sem(name + "_exp"), 1)
                    if sinks:
                        nc.scalar.activation(small[:, 8 * par + 6:8 * par + 8], nm, ACT.Exp,
                                             bias=vcol("sinks", 2 * c + par)).then_inc(sem(name + "_sink"), 1)
            exponentials(0)
            for c in range(WC):
                for par in range(2):
                    act.wait_ge(sem(name + "_turned"), 2 * c + par + 1)
                    nc.scalar.copy(probT[par][:, :, :], bank(6 + par)[:, 0:384]).then_inc(sem(name + "_probT"), 1)
                if c + 1 < WC:
                    exponentials(c + 1)
                beside(c, 0)
                beside(c, 1)

        band_d = nc.dram_tensor("relative_band", [HEADS, 128, 384], f32, kind="Internal").ap()
        gate_d = nc.dram_tensor("gate_matrix", [SLICES, 128, T * 16], f32, kind="Internal").ap()
        YB, YA, YC, YD = 1, 0, 3, 2

        @block.sync
        def _(sp):
            sp.dma_start(xraw[:, :, :].rearrange("p k n -> p (k n)"), xt).then_inc(sem("x_loaded"), 16)
            for n in range(RAW):
                load(sp, Block(n))
            with sp.Fori(1, NBLOCKS // 4) as g:
                for i in range(4):
                    load(sp, Block(4 + i, g - 1))
            for n in range(NBLOCKS // 4 * 4, NBLOCKS):
                load(sp, Block(n))
            for half in range(4):
                sp.wait_ge(sem("out_ready"), 4 * half + 4)
                sp.dma_start(out[:, 1024 * half:1024 * half + 1024],
                             zsum[:, 4 * half:4 * half + 4, :].rearrange("p c n -> p (c n)")
                             ).then_inc(sem("out_stored"), 16)
            sp.wait_ge(sem("out_stored"), 64)

        @block.gpsimd
        def _(pool):
            nc.gpsimd.memset(ident[:, :], 0.0).then_inc(sem("pool_memset"), 1)
            nc.gpsimd.memset(cband[:, :], NEG).then_inc(sem("band_cleared"), 1)
            nc.gpsimd.memset(ones[:, :], 1.0).then_inc(sem("ones_ready"), 1)
            nc.gpsimd.iota(iota[:, :], [[1, 128]], base=0, channel_multiplier=0,
                           allow_small_or_imprecise_dtypes=True).then_inc(sem("iota_ready"), 1)
            pool.wait_ge(sem("pool_memset"), 1)
            nc.gpsimd.affine_select(out=ident[:, :], in_=ident[:, :], compare_op=ALU.not_equal, fill=1.0, base=0,
                                    pattern=[[-1, 128]], channel_multiplier=1).then_inc(sem("ident_ready"), 1)
            nc.gpsimd.memset(cq[:, :, :, :], 0.0).then_inc(sem("cq_cleared"), 1)
            pool.wait_ge(sem("xlo_ready"), 1)
            nc.gpsimd.memset(glu[:, :, 0:CONV_K - 1], 0.0).then_inc(sem("glu_padded"), 1)
            pool.wait_ge(sem("band_ready"), 1)
            pool.dma_start(band_d, cband[:, :].rearrange("h (a m) -> h a m", a=1).to_broadcast([HEADS, 128, 384])
                           ).then_inc(sem("band_stored"), 16)
            pool.wait_ge(sem("band_stored"), 16)
            pool.dma_start(cbias[:, :, :], bass.AP(band_d.tensor, 127, [[383, 128], [128 * 384, HEADS], [1, T]])
                           ).then_inc(sem("bias_ready"), 16)
            pool.wait_ge(sem("c_done"), 1)
            nc.gpsimd.memset(ain[:, :, 0:PAD], 0.0).then_inc(sem("ain_padded"), 1)
            pool.wait_ge(sem("d_done"), 1)
            pool.dma_start(sguw[:, :, :].rearrange("p h n -> p (h n)"), sgu_wt).then_inc(sem("sguw_loaded"), 16)
            pool.dma_start(sgub[:, :, :].rearrange("p h n -> p (h n)"), sgu_b.partition_broadcast(128)
                           ).then_inc(sem("sgub_loaded"), 16)
            pool.wait_ge(sem("sguw_loaded"), 16)
            nc.gpsimd.affine_select(out=sguw[:, :, :], in_=sguw[:, :, :], compare_op=ALU.is_ge, fill=0.0, base=0,
                                    pattern=[[0, WC], [1, 128]], channel_multiplier=-1
                                    ).then_inc(sem("sguw_masked"), 1)
            pool.wait_ge(sem("b_done"), 1)
            pool.dma_start(cnt[:, :, :].rearrange("p g n -> p (g n)"), inv_cnt.partition_broadcast(128)
                           ).then_inc(sem("cnt_loaded"), 16)
            pool.wait_ge(mm_done, FIRST["w_out"])
            pool.dma_start(xagain[:, :, :].rearrange("p k n -> p (k n)"), xt).then_inc(sem("xagain_loaded"), 16)
            pool.wait_ge(sem("h1_lo"), 4)
            nc.gpsimd.memset(xpad[:, :, 0:CONV2_K - 1], 0.0).then_inc(sem("xpad_ready"), 1)
            nc.gpsimd.memset(cmask[:, :], 0.0).then_inc(sem("cmask_cleared"), 1)
            pool.wait_ge(sem("cmask_cleared"), 1)
            nc.gpsimd.affine_select(out=cmask[:, :], in_=cmask[:, :], compare_op=ALU.is_ge, fill=NEG, base=0,
                                    pattern=[[-1, 128]], channel_multiplier=1).then_inc(sem("cmask_ready"), 1)
            pool.wait_ge(sem("cb_copied"), 2)
            nc.gpsimd.affine_select(out=cb[:, :, 0:256], in_=cb[:, :, 0:256], compare_op=ALU.is_ge, fill=0.0, base=0,
                                    pattern=[[0, 2], [1, 256]], channel_multiplier=-1).then_inc(sem("cb_masked"), 1)
            nc.gpsimd.affine_select(out=cb[:, :, 256:384], in_=cb[:, :, 256:384], compare_op=ALU.is_ge, fill=0.0,
                                    base=0, pattern=[[0, 2], [1, 128]], channel_multiplier=-1
                                    ).then_inc(sem("cb_masked"), 1)
            pool.wait_ge(sem("ssd_gated"), 1)
            nc.gpsimd.memset(fq[0][64:128, :, :], 0.0).then_inc(sem("fq_cleared"), 1)
            nc.gpsimd.memset(fq[1][0:64, :, :], 0.0).then_inc(sem("fq_cleared"), 1)
            pool.wait_ge(sem("f_done"), 1)
            pool.dma_start(pk[:, :, :].rearrange("p k n -> p (k n)"), keys).then_inc(sem("keys_loaded"), 16)
            for i in range(8):
                pool.wait_ge(sem("stage_full"), 8 * (i + 1))
                pool.dma_start(gate_d[:, :, 512 * i:512 * i + 512].rearrange("e p n -> p e n"),
                               gstage[i % 2][:, :, :, :].rearrange("p e t i -> p e (t i)")
                               ).then_inc(sem(f"gate_stored{i % 2}"), 16)
            for i in range(2):
                pool.wait_ge(sem(f"gate_stored{i}"), 64)
            for e in range(SLICES):
                if 0 < e <= EARLY:
                    pool.wait_ge(sem("early_gated"), 4 * e)
                elif e:
                    pool.wait_ge(sem("u_gated"), 16 * (e - EARLY))
                pool.dma_start(gslice[:, :, :].rearrange("p t i -> p (t i)"), gate_d[e]).then_inc(sem("gate_loaded"), 16)

        @block.tensor
        def _(pe):
            pe.wait_ge(sem("onehot_loaded"), 32)
            nc.tensor.matmul(bank(7)[0:16, 0:128], relb_sb[:, :], onehot_b[:, :], start=True,
                             stop=True).then_inc(sem("band_product"), 1)
            pe.wait_ge(sem("xlo_ready"), 1)
            def by_x(b, i, g):
                product(pe, b, xhi, xlo)
            pst = Steps(pe, sem("pe_steps"))
            for name in ("c_kv", "c_q", "c_gate"):
                blocks(pe, pst, FIRST[name], COUNT[name], by_x)
            wait_evacuated(pe, "c_gate")
            pe.wait_ge(sem("ident_ready"), 1)
            for j in range(NT):
                ins = nc.tensor.transpose(bank(4 + 3 * j)[:, 0:128], ckv[:, 1, 128 * j:128 * j + 128], ident[:, :])
            ins.then_inc(sem("cv_turned"), 1)
            pe.wait_ge(sem("cvtok_ready"), 1)
            pe.wait_ge(sem("bias_ready"), 16)
            def band(c, par, qt):
                h = 2 * c + par
                return [(ident[:, :], cbias[:, h, 128:256] if qt == 0 else cbias[:, h, :], 0, 128 if qt == 0 else 256)]
            def beside_c(c, i):
                by_x(Block(FIRST["d_val"] + 2 * c + i), 0, 0)
            attend_pe(pe, "c", [cq[:, i, :, :] for i in range(2)], ckv, lambda c: 0, lambda j, c: cvtok[:, j, :],
                      cprob, cprobT, band, beside_c)
            for name in ("d_gate", "b_v", "b_u", "b_gate"):
                blocks(pe, pst, FIRST[name], COUNT[name], by_x)

            def beside_a(first, end):
                for n in range(first, end):
                    by_x(Block(FIRST["a_in"] + n), 0, 0)
            pe.wait_ge(sem("conv_done"), 1)
            pe.wait_ge(sem("ones_ready"), 1)
            norm_sum(pe, dacc, WC)
            beside_a(0, 2)
            norm_sumsq(pe, "d", dsq, WC)
            beside_a(2, 4)
            pe.wait_ge(sem("norm_var"), turn("var", "d"))
            wait_evacuated(pe, "b_gate")
            norm_sum(pe, bv, WC)
            beside_a(4, 6)
            norm_sumsq(pe, "b", bsq, WC)
            beside_a(6, 8)
            pe.wait_ge(sem("norm_out"), turn("out", "b"))
            for r in range(4):
                for h in range(2):
                    for j in range(NT):
                        ins = nc.tensor.transpose(bank(4 + r)[:, 256 * h + 128 * j:256 * h + 128 * j + 128],
                                                  bv[:, 2 * r + h, 128 * j:128 * j + 128], ident[:, :])
                ins.then_inc(sem("bv_turned"), 1)
            beside_a(8, 9)
            pe.wait_ge(sem("sguw_masked"), 1)
            for r in range(4):
                pe.wait_ge(sem("vtok_ready"), r + 1)
                for h in range(2):
                    for j in range(NT):
                        hh = 2 * r + h
                        ins = nc.tensor.matmul(bank(4 + r)[:, 256 * h + 128 * j:256 * h + 128 * j + 128],
                                               vtok[:, j, 128 * hh:128 * hh + 128], sguw[:, hh, :],
                                               start=True, stop=True)
                ins.then_inc(sem("b_spatial"), 1)
            beside_a(9, 16)
            pe.wait_ge(sem("mixlo_ready"), 1)
            b = Block(FIRST["a_pool"])
            pe.wait_ge(lo_done, 2 * b.count(1))
            for i in range(WC):
                o = bank(4 + i // 2)[:, T * (i % 2):T * (i % 2) + T]
                for k in range(2):
                    w, r = 2 * i + k, 2 * (i // 2) + k
                    nc.tensor.matmul(o, whi[b.half][:, w, :], mixhi[:, r, :], start=k == 0, stop=False)
                    nc.tensor.matmul(o, whi[b.half][:, w, :], mixlo[:, r, :], start=False, stop=False)
                    ins = nc.tensor.matmul(o, wlo[b.half][:, w, :], mixhi[:, r, :], start=False, stop=k == 1)
                if i == 3:
                    ins.then_inc(mm_half, 1)
            ins.then_inc(mm_done, 1)
            def merging(b, i, g):
                j = i % 6
                if j < 4:
                    product(pe, b, xhi, xlo)
                    return
                pe.wait_ge(sem("a_done"), 1)
                for h in range(2):
                    y = (YA, YB, YC, YD)[2 * (j - 4) + h]
                    product(pe, b, yhi[y], ylo[y], ks=range(8 * h, 8 * h + 8), cols=T * h, first=h == 0, last=h == 1)
            blocks(pe, pst, FIRST["merge"], 96, merging, unit=12)
            pe.wait_ge(sem("merged"), 16)
            for n in range(18):
                if n < 16:
                    product(pe, Block(FIRST["w_out"] + n), mhi, mlo)
                if n >= 2:
                    block_out(pe, FIRST["w_out"] + n - 2)
                    sum_chunk(pe, 4, zsum, n - 2, "norm_sum")
            for c in range(KC):
                pe.wait_ge(sem("x1_sq"), c // 4 + 1)
                sum_chunk(pe, 5, sq16, c, "norm_sumsq")
            for c in range(KC):
                pe.wait_ge(sem("h1_sq"), c + 1)
                sum_chunk(pe, 5, sq16, c, "norm_sumsq")
            product(pe, Block(FIRST["dtf"]), xhi, xlo, ready=lambda h: pe.wait_ge(sem("h1_lo"), 2 * h + 2))
            for name in ("z", "xbc"):
                blocks(pe, pst, FIRST[name], COUNT[name], by_x)

            def beside_ssd(first, end):
                for n in range(first, end):
                    by_x(Block(FIRST["fk"] + n), 0, 0)
            beside_ssd(0, 1)
            pe.wait_ge(sem("cum_ready"), 1)
            for i, src in enumerate((cum, dtfs)):
                for j in range(NT):
                    ins = nc.tensor.transpose(bank(6)[:, 256 * i + 128 * j:256 * i + 128 * j + 128],
                                              src[:, 128 * j:128 * j + 128], ident[:, :])
            ins.then_inc(sem("cum_turned"), 1)

            def turn_chunks(name, src):
                for r in range(4):
                    for h in range(2):
                        for j in range(NT):
                            ins = nc.tensor.transpose(bank(4 + r)[:, 256 * h + 128 * j:256 * h + 128 * j + 128],
                                                      src[:, 2 * r + h, 128 * j:128 * j + 128], ident[:, :])
                    ins.then_inc(sem(name), 1)
            pe.wait_ge(sem("cumT_ready"), 1)
            pe.wait_ge(sem("xconv_ready"), 1)
            turn_chunks("xs_turned", xconv)
            beside_ssd(1, 3)
            pe.wait_ge(sem("xtok_ready"), 4)
            for g in range(2):
                B, C, o = xconv[:, 8 + g, :], xconv[:, 10 + g, :], bank(4 + g)
                nc.tensor.matmul(o[:, 0:256], B[:, 0:128], C, start=True, stop=True)
                nc.tensor.matmul(o[:, 256:384], B[:, 128:256], C[:, 128:256], start=True,
                                 stop=True).then_inc(sem("cb_product"), 1)
            pe.wait_ge(sem("cb_copied"), 2)

            def head_row(h):
                if h >= 2:
                    pe.wait_ge(sem("ssd_diff"), h - 1)
                nc.tensor.matmul(bank(4 + h % 2)[:, 0:T], ident[:, h:h + 1].to_broadcast([128, 128]), cum[:, :],
                                 start=True, stop=True).then_inc(sem("ssd_row"), 1)
            head_row(0)
            head_row(1)
            for h in range(HEADS):
                if h % 2 == 0:
                    beside_ssd(3 + h // 2, 4 + h // 2)
                if h >= 2:
                    pe.wait_ge(sem("ssd_out"), h - 1)
                pe.wait_ge(sem("ssd_mat"), h + 1)
                c, m, o = h // 2, dec[h % 2], bank(6 + h % 2)
                nc.tensor.matmul(o[:, 0:256], xtok[:, 0, 128 * c:128 * c + 128], m[:, 0:256], start=True, stop=False)
                nc.tensor.matmul(o[:, 128:256], xtok[:, 1, 128 * c:128 * c + 128], m[:, 256:384], start=False,
                                 stop=True).then_inc(sem("ssd_y"), 1)
                if h + 2 < HEADS:
                    head_row(h + 2)
            for g in range(2):
                beside_ssd(11 + 2 * g, 13 + 2 * g)
                norm_pe(pe, f"s{g}", None, ssq, 4, None, centre=False)
            beside_ssd(15, 16)
            blocks(pe, pst, FIRST["fq"], COUNT["fq"], by_x)
            wait_evacuated(pe, "fq")
            turn_chunks("fv_turned", fv)
            pe.wait_ge(sem("fvtok_ready"), 4)
            pe.wait_ge(sem("cmask_ready"), 1)

            def forgetting(c, par, qt):
                f = 32 + 2 * c + par
                w = 128 + 128 * qt
                return [(cum[:, 128 * qt:128 * qt + 128], ident[:, f:f + 1].to_broadcast([128, w]), 0, w),
                        (ident[:, f:f + 1].to_broadcast([128, 128]), ncum[:, 0:w], 0, w),
                        (ident[:, :], cmask[:, :], w - 128, w)]

            def by_half(b, part):
                for h in range(2):
                    product(pe, b, mhi, mlo, ks=range(8 * h, 8 * h + 8), k0=8 * part, cols=T * h, first=h == 0,
                            last=h == 1)

            def beside_f(c, i):
                if i == 0:
                    by_half(Block(FIRST["w_out2"] + c), 0)
            pe.wait_ge(sem("norm_lo"), turn("lo", "s1"))
            attend_pe(pe, "f", fq, fk, lambda c: c, lambda j, c: fvtok[:, j, 128 * c:128 * c + 128], fprob, fprobT,
                      forgetting, beside_f)
            pe.wait_ge(sem("f_done"), 1)
            for n in range(8, 18):
                if n < 16:
                    by_half(Block(FIRST["w_out2"] + n), 1)
                if n >= 10:
                    pe.wait_ge(sem("h2_sq"), n - 9)
                    for c in range(2 * (n - 10), 2 * (n - 10) + 2):
                        sum_chunk(pe, 5, sq16, c, "norm_sumsq")
            product(pe, Block(FIRST["wq"]), xhi, xlo, ready=lambda h: pe.wait_ge(sem("h2_lo"), 2 * h + 2))
            blocks(pe, pst, FIRST["wq"] + 1, 15, by_x)
            wait_evacuated(pe, "wq")
            pe.wait_ge(sem("keys_loaded"), 16)
            for n in range(8):
                j, q = n // 4, n % 4
                if n >= 4:
                    pe.wait_ge(sem("scores_out"), n - 3)
                for i in range(4):
                    hs = 4 * q + i
                    ins = nc.tensor.matmul(bank(4 + n % 4)[:, 128 * i:128 * i + 128], pq[:, hs, 128 * j:128 * j + 128],
                                           pk[:, hs, :], start=True, stop=True)
                ins.then_inc(sem("scores_ready"), 1)
            blocks(pe, pst, U_EARLY, U_GATES - U_EARLY, by_x)
            pe.wait_ge(sem("chosen_ready"), 1)
            for i in range(3):
                for j in range(NT):
                    ins = nc.tensor.transpose(bank(4 + i)[:, 128 * j:128 * j + 128],
                                              chosen[i][:, 8 * j:8 * j + 8, :].rearrange("p h k -> p (h k)"), ident[:, :])
            ins.then_inc(sem("chosen_turned"), 1)
            for part in range(8):
                for i in range(8):
                    pe.wait_ge(sem("onehots"), 8 * part + i + 1)
                    pe.wait_ge(sem("bank_free"), 8 * part + i + 1)
                    for t in range(4):
                        ins = nc.tensor.matmul(bank(4 + i % 4)[:, 128 * t:128 * t + 128], one2[i % 4][:, t, :],
                                               one1[i % 4][:, t, :], start=True, stop=True)
                    ins.then_inc(sem("gate_product"), 1)
                    if i == 3:
                        by_x(Block(U_GATES + part), 0, 0)
            blocks(pe, pst, U_REST, V_EARLY - U_REST, by_x)
            for e in range(EARLY):
                blocks(pe, pst, V_EARLY + 16 * e, 16, lambda b, i, g: product(
                    pe, b, aghi[e], aglo[e], ready=lambda h: pe.wait_ge(sem("early_lo"), 4 * e + 2 * h + 2)))

            def slice_pe(e):
                expert_blocks(pe, pst, e, 0, by_x)

                def downward(b, i, g):
                    product(pe, b, aghi[0], aglo[0], ready=lambda h: pe.wait_ge(sem("ag_lo"), e * 16 + 8 * h + 8))
                    if isinstance(e, int) and i >= 2:
                        square_sum(i - 2)

                def square_sum(c):
                    pe.wait_ge(sem("fin_sq"), c + 1)
                    sum_chunk(pe, 5, sq16, c, "norm_sumsq")
                expert_blocks(pe, pst, e, 16, downward)
                if isinstance(e, int):
                    square_sum(14)
                    square_sum(15)
            with pst.loop(LATE - 1, 0) as e:
                slice_pe(e)
            slice_pe(LATE - 1)

        @block.vector
        def _(dve):
            st = Steps(dve, sem("dve_steps"))
            dve.sem_inc(sem("sig_used"), 2)
            nc.vector.memset(csmall[:, :], 0.0)
            dve.wait_ge(sem("band_product"), 1)
            dve.wait_ge(sem("band_cleared"), 1)
            nc.vector.tensor_copy(cband[:, 128:256], bank(7)[0:16, 0:128]).then_inc(sem("band_ready"), 1)
            dve.wait_ge(sem("x_loaded"), 16)
            dve.wait_ge(sem("xhi_ready"), 1)
            nc.vector.tensor_tensor(xlo[:, :, :], xraw[:, :, :], xhi[:, :, :].bitcast(f32),
                                    ALU.subtract).then_inc(sem("xlo_ready"), 1)
            for n in range(SPLIT):
                split_lo(dve, Block(n))

            def lo_only(b, i, g):
                if exists(b.count(SPLIT)):
                    split_lo(dve, b.ahead(SPLIT))
            for name in ("c_kv", "c_q", "c_gate"):
                blocks(dve, st, FIRST[name], COUNT[name], lo_only)
            dve.wait_ge(sem("cv_turned"), 1)
            nc.vector.tensor_copy(cvtok[:, 0, :], bank(4)[:, 0:128])
            nc.vector.tensor_copy(cvtok[:, 1, :], bank(7)[:, 0:128]).then_inc(sem("cvtok_ready"), 1)
            dve.wait_ge(sem("vec_loaded"), 16)


            def glu_gate(b, i, g):
                lo_only(b, i, g)
                dve.wait_ge(evacuated[b.bank], b.uses())
                dst = chunk(glu, b.index(FIRST["d_act"]))[:, CONV_K - 1:]
                nc.vector.tensor_tensor(dst, dst, sig[b.n0 % 2][:, :], ALU.mult).then_inc(sem("sig_used"), 1)

            def beside_c(c, i):
                n = FIRST["d_val"] + 2 * c + i
                (glu_gate if n >= FIRST["d_act"] else lo_only)(Block(n), 0, 0)
            attend_dve(dve, st, "c", cprob, csmall, co, cgate, True, beside_c)
            dve.wait_ge(sem("c_hi"), 1)
            nc.vector.tensor_tensor(ylo[YC][:, :, :], co[:, :, :], yhi[YC][:, :, :].bitcast(f32),
                                    ALU.subtract).then_inc(sem("c_done"), 1)
            def taps(i, c):
                acc = chunk(dacc, c)
                g = chunk(glu, c)
                for k in range(8 * i, min(8 * i + 8, CONV_K)):
                    w = vec[:, bass.ds(c * CONV_K + (VCOL["conv_w"] + k), 1)]
                    if k == 0:
                        st.link(nc.vector.tensor_scalar(acc, g[:, 0:T], w, vec[:, bass.ds(c + VCOL["conv_b"], 1)],
                                                        ALU.mult, ALU.add))
                    else:
                        st.link(nc.vector.scalar_tensor_tensor(acc, g[:, k:k + T], w, acc, ALU.mult, ALU.add))

            def conv_body(base, mult):
                def body(b, i, g):
                    lo_only(b, i, g)
                    if mult:
                        j = b.index(FIRST["b_gate"])
                        dve.wait_ge(evacuated[b.bank], b.uses())
                        dst = chunk(bug, j)
                        nc.vector.tensor_tensor(dst, dst, sig[b.n0 % 2][:, :], ALU.mult).then_inc(sem("sig_used"), 1)
                    taps(i % 4, g + base)
                return body
            blocks(dve, st, FIRST["d_gate"], 24, conv_body(0, False), per_turn=CONV_K)
            blocks(dve, st, FIRST["b_gate"], 8, conv_body(6, True), per_turn=CONV_K)
            dve.sem_inc(sem("conv_done"), 1)

            def beside_a(first, end):
                for n in range(first, end):
                    lo_only(Block(FIRST["a_in"] + n), 0, 0)
            norm_centre(dve, st, "d", dacc, WC, stat[0])
            beside_a(0, 2)
            norm_variance(dve, "d", WC, stat[1], LN_EPS)
            beside_a(2, 3)
            norm_root(dve, st, "d", dacc, WC, stat)
            beside_a(3, 4)
            dve.wait_ge(sem("norm_out"), turn("out", "d"))
            nc.vector.tensor_tensor(dacc[:, :, :], dacc[:, :, :], dgate[:, :, :], ALU.mult).then_inc(sem("d_gated"), 1)
            norm_centre(dve, st, "b", bv, WC, stat[0])
            beside_a(4, 5)
            dve.wait_ge(sem("d_hi"), 1)
            nc.vector.tensor_tensor(ylo[YD][:, :, :], dacc[:, :, :], yhi[YD][:, :, :].bitcast(f32),
                                    ALU.subtract).then_inc(sem("d_done"), 1)
            beside_a(5, 6)
            norm_variance(dve, "b", WC, stat[1], LN_EPS)
            beside_a(6, 7)
            norm_root(dve, st, "b", bv, WC, stat)
            beside_a(7, 8)
            for r in range(4):
                dve.wait_ge(sem("bv_turned"), r + 1)
                nc.vector.tensor_copy(
                    vtok[:, :, 256 * r:256 * r + 256].rearrange("p j (h d) -> p h j d", h=2),
                    bank(4 + r)[:, :].rearrange("p (h j d) -> p h j d", h=2, j=NT)).then_inc(sem("vtok_ready"), 1)
            beside_a(8, 9)
            dve.wait_ge(sem("sgub_loaded"), 16)
            for r in range(4):
                dve.wait_ge(sem("b_spatial"), r + 1)
                t = bsq[:, 2 * r:2 * r + 2, :]
                for h in range(2):
                    bias_h = sgub[:, 2 * r + h, :].rearrange("p (a n) -> p a n", a=1).to_broadcast([128, NT, 128])
                    ins = nc.vector.tensor_tensor(bsq[:, 2 * r + h, :].rearrange("p (j n) -> p j n", j=NT),
                                                  bank(4 + r)[:, T * h:T * h + T].rearrange("p (j n) -> p j n", j=NT),
                                                  bias_h, ALU.add)
                st.link(ins)
                last = nc.vector.tensor_tensor(bug[:, 2 * r:2 * r + 2, :], bug[:, 2 * r:2 * r + 2, :], t, ALU.mult)
            last.then_inc(sem("b_gated"), 1)
            beside_a(9, 10)
            dve.wait_ge(sem("b_hi"), 1)
            nc.vector.tensor_tensor(ylo[YB][:, :, :], bug[:, :, :], yhi[YB][:, :, :].bitcast(f32),
                                    ALU.subtract).then_inc(sem("b_done"), 1)
            beside_a(10, 11)
            L = T + PAD
            wait_evacuated(dve, "a_in")
            dve.wait_ge(sem("ain_padded"), 1)
            st.link(nc.vector.tensor_tensor(win_a[:, :, 1:L], ain[:, :, 1:L], ain[:, :, 0:L - 1], ALU.add))
            st.link(nc.vector.tensor_tensor(win_b[:, :, 3:L], win_a[:, 2:8, 3:L], win_a[:, 2:8, 1:L - 2], ALU.add))
            st.link(nc.vector.tensor_tensor(win_a[:, 4:8, 7:L], win_b[:, 2:6, 7:L], win_b[:, 2:6, 3:L - 4], ALU.add))
            st.link(nc.vector.tensor_tensor(win_b[:, 4:6, 15:L], win_a[:, 6:8, 15:L], win_a[:, 6:8, 7:L - 8], ALU.add))
            beside_a(11, 12)
            dve.wait_ge(sem("cnt_loaded"), 16)
            for g, src in enumerate((win_a[:, 0:2, PAD:], win_b[:, 0:2, PAD:], win_a[:, 4:6, PAD:],
                                     win_b[:, 4:6, PAD:])):
                by = cnt[:, g, :].rearrange("p (a n) -> p a n", a=1).to_broadcast([128, 2, T])
                ins = nc.vector.tensor_tensor(src, src, by, ALU.mult)
                st.link(ins)
                dst = ain[:, 2 * g:2 * g + 2, PAD:]
                last = nc.vector.tensor_tensor(dst, src, dst, ALU.subtract)
            last.then_inc(sem("mix_ready"), 1)
            beside_a(12, 13)
            dve.wait_ge(sem("mixhi_ready"), 1)
            nc.vector.tensor_tensor(mixlo[:, :, :], ain[:, :, PAD:], mixhi[:, :, :].bitcast(f32),
                                    ALU.subtract).then_inc(sem("mixlo_ready"), 1)
            beside_a(13, 17)
            b = Block(FIRST["a_pool"])
            wait_evacuated(dve, "a_gate")
            dve.wait_ge(mm_done, b.count(1))
            for i in range(WC):
                st.link(nc.vector.scalar_tensor_tensor(win_a[:, i, 0:T], bank(4 + i // 2)[:, T * (i % 2):T * (i % 2) + T],
                                                       vcol("pool_scale", i), agate[:, i, :], ALU.mult, ALU.mult))
            dve.sem_inc(evacuated[b.bank], 1)
            dve.sem_inc(sem("a_gated"), 1)
            dve.wait_ge(sem("a_hi"), 1)
            nc.vector.tensor_tensor(ylo[YA][:, :, :], win_a[:, :, 0:T], yhi[YA][:, :, :].bitcast(f32),
                                    ALU.subtract).then_inc(sem("a_done"), 1)
            def merging(b, i, g):
                lo_only(b, i, g)
                j, m = i % 6, i // 6
                if j < 4:
                    return
                part = msum[0] if j == 4 else msum[1]
                dve.wait_ge(mm_done, b.count(1))
                o = bank(b.bank)[:, :].rearrange("p (h n) -> p h n", h=2)
                st.link(nc.vector.tensor_tensor(gates[m][:, 2 * (j - 4):2 * (j - 4) + 2, :], o,
                                                gates[m][:, 2 * (j - 4):2 * (j - 4) + 2, :], ALU.mult))
                ins = nc.vector.tensor_tensor(part[:, :], gates[m][:, 2 * (j - 4), :], gates[m][:, 2 * (j - 4) + 1, :],
                                              ALU.add)
                ins.then_inc(evacuated[b.bank], 1)
                if j == 5:
                    dve.wait_ge(evacuated[b.bank], b.uses())
                    dve.sem_inc(sem("gates_free"), 1)
                    col = 2 * g + m
                    nc.vector.tensor_tensor(msum[0][:, :], msum[0][:, :], msum[1][:, :], ALU.add
                                            ).then_inc(sem("merge_sum"), 1)
                    dve.wait_ge(sem("mhi_done"), col + 1)
                    nc.vector.tensor_tensor(chunk(mlo, col), msum[0][:, :], chunk(mhi, col).bitcast(f32),
                                            ALU.subtract).then_inc(sem("merged"), 1)
            dve.sem_inc(sem("gates_free"), 2)
            blocks(dve, st, FIRST["merge"], 96, merging, per_turn=4, unit=12)
            dve.wait_ge(sem("xagain_loaded"), 16)

            def residual(b, i, g):
                lo_only(b, i, g)
                j = b.index(FIRST["w_out"])
                dve.wait_ge(mm_done, b.count(1))
                nc.vector.scalar_tensor_tensor(chunk(zsum, j), chunk(xagain, j), ALPHA, bank(b.bank)[:, 0:T],
                                               ALU.mult, ALU.add).then_inc(evacuated[b.bank], 1)
            blocks(dve, st, FIRST["w_out"], 16, residual)
            dve.wait_ge(sem("norm_sum"), turn("sum", "x1"))
            st.link(nc.vector.tensor_scalar(st16[0][:, :], bank(4)[:, 0:T], 1.0 / D, None, ALU.mult))
            for q in range(4):
                part = zsum[:, 4 * q:4 * q + 4, :]
                nc.vector.tensor_tensor(part, part, spread(st16[0], 4), ALU.subtract).then_inc(sem("x1_centred"), 1)
            norm_variance(dve, "x1", KC, st16[1], LN_EPS)
            norm_root(dve, st, "x1", None, KC, st16, scale=False)
            for c in range(KC):
                nc.vector.scalar_tensor_tensor(zsum[:, c, :], zsum[:, c, :], vcol("ln_g", c), st16[2][:, :],
                                               ALU.mult, ALU.mult).then_inc(sem("x1_scaled"), 1)
            for c in range(KC):
                dve.wait_ge(sem("x1_scaled"), c + 1)
                ins = nc.vector.tensor_scalar(x1[:, c, :], zsum[:, c, :], vcol("ln_b", c), None, ALU.add)
            st.link(ins)

            def rms_parts(name, gain):
                norm_variance(dve, name, KC, st16[1], RMS_EPS)
                norm_root(dve, st, name, None, KC, st16, scale=False)
                for q in range(5):
                    if q < 4:
                        for c in range(4 * q, 4 * q + 4):
                            ins = nc.vector.scalar_tensor_tensor(zsum[:, c, :], x1[:, c, :], vcol(gain, c),
                                                                 st16[2][:, :], ALU.mult, ALU.mult)
                        ins.then_inc(sem(name + "_scaled"), 1)
                    if q:
                        part = slice(4 * q - 4, 4 * q)
                        dve.wait_ge(sem(name + "_hi"), q)
                        nc.vector.tensor_tensor(xlo[:, part, :], zsum[:, part, :], xhi[:, part, :].bitcast(f32),
                                                ALU.subtract).then_inc(sem(name + "_lo"), 1)
            rms_parts("h1", "ln1_w")

            def rms_split(name, src, r, gain, n, dhi, dlo, tmp, j0=0, c0=0):
                for c in range(n):
                    st.link(nc.vector.scalar_tensor_tensor(tmp[:, c, :], src[:, c, :], vcol(gain, c0 + c), r[:, :],
                                                           ALU.mult, ALU.mult))
                dve.sem_inc(sem("norm_scaled"), 1)
                dve.wait_ge(sem("norm_hi"), turn("hi", name))
                nc.vector.tensor_tensor(dlo[:, j0:j0 + n, :], tmp[:, 0:n, :], dhi[:, j0:j0 + n, :].bitcast(f32),
                                        ALU.subtract).then_inc(sem("norm_lo"), 1)
            b = Block(FIRST["dtf"])
            y, u, w1, lg = dtt
            lo_only(b, 0, 0)
            dve.wait_ge(mm_done, b.count(1))
            ins = nc.vector.tensor_scalar(y[:, :], bank(b.bank)[:, 0:T], vcol("dtf_bias"), vcol("dtf_sign"), ALU.add,
                                          ALU.mult)
            ins.then_inc(evacuated[b.bank], 1)
            dve.wait_ge(evacuated[b.bank], b.uses())
            nc.vector.scalar_tensor_tensor(u[:, :], y[:, :], -1.0, y[:, :], ALU.mult, ALU.max).then_inc(sem("dt_abs"), 1)
            dve.wait_ge(sem("dt_exp"), 1)
            nc.vector.tensor_scalar(w1[:, :], u[:, :], 1.0, None, ALU.add).then_inc(sem("dt_one"), 1)
            dve.wait_ge(sem("dt_log"), 1)
            st.link(nc.vector.tensor_scalar(cum[:, :], w1[:, :], -1.0, None, ALU.add))
            st.link(nc.vector.tensor_tensor(u[:, :], u[:, :], cum[:, :], ALU.subtract))
            st.link(nc.vector.reciprocal(w1[:, :], w1[:, :]))
            st.link(nc.vector.tensor_tensor(u[:, :], u[:, :], w1[:, :], ALU.mult))
            st.link(nc.vector.tensor_tensor(lg[:, :], lg[:, :], u[:, :], ALU.add))
            st.link(nc.vector.scalar_tensor_tensor(dtfs[:, :], y[:, :], 0.0, lg[:, :], ALU.max, ALU.add))
            dve.wait_ge(sem("acol_exp"), 1)
            st.link(nc.vector.tensor_scalar(acol[:, 1:2], acol[:, 0:1], -1.0, None, ALU.mult))
            st.link(nc.vector.tensor_scalar(u[:, :], dtfs[:, :], acol[:, 1:2], None, ALU.mult))
            st.link(nc.vector.memset(w1[:, :], 1.0))
            st.link(nc.vector.tensor_tensor_scan(cum[:, :], w1[:, :], u[:, :], 0.0, ALU.mult, ALU.add))
            nc.vector.tensor_scalar(ncum[:, :], cum[:, :], -1.0, None, ALU.mult).then_inc(sem("cum_ready"), 1)
            blocks(dve, st, FIRST["z"], COUNT["z"], lo_only)
            dve.wait_ge(sem("xpad_ready"), 1)

            def conv2(b, i, g):
                lo_only(b, i, g)
                dve.wait_ge(evacuated[b.bank], b.uses())
                c = b.index(FIRST["xbc"])
                acc, src = chunk(xconv, c), chunk(xpad, c)
                for k in range(CONV2_K):
                    w = vec[:, bass.ds(c * CONV2_K + (VCOL["conv2_w"] + k), 1)]
                    if k == 0:
                        st.link(nc.vector.tensor_scalar(acc, src[:, 0:T], w, vec[:, bass.ds(c + VCOL["conv2_b"], 1)],
                                                        ALU.mult, ALU.add))
                    else:
                        st.link(nc.vector.scalar_tensor_tensor(acc, src[:, k:k + T], w, acc, ALU.mult, ALU.add))
            blocks(dve, st, FIRST["xbc"], COUNT["xbc"], conv2, per_turn=4 * CONV2_K)
            dve.sem_inc(sem("conv2_done"), 1)

            def beside_ssd(first, end):
                for n in range(first, end):
                    lo_only(Block(FIRST["fk"] + n), 0, 0)
            beside_ssd(0, 1)
            dve.wait_ge(sem("cum_turned"), 1)
            nc.vector.tensor_copy(cumT[:, :, :], bank(6)[:, 0:256])
            nc.vector.tensor_copy(dtT[:, :, :], bank(6)[:, 256:512]).then_inc(sem("cumT_ready"), 1)
            dve.wait_ge(sem("cumT_ready"), 1)
            for r in range(4):
                dve.wait_ge(sem("xs_turned"), r + 1)
                for h in range(2):
                    c = 2 * r + h
                    ins = nc.vector.tensor_tensor(
                        xtok[:, :, 128 * c:128 * c + 128].rearrange("p j (a d) -> p j a d", a=2),
                        bank(4 + r)[:, 256 * h:256 * h + 256].rearrange("p (j a d) -> p j a d", j=NT, a=2),
                        dtT[:, :, 2 * c:2 * c + 2].rearrange("p j (a d) -> p j a d", d=1).to_broadcast([128, NT, 2, 64]),
                        ALU.mult)
                ins.then_inc(sem("xtok_ready"), 1)
            beside_ssd(1, 3)
            for g in range(2):
                dve.wait_ge(sem("cb_product"), g + 1)
                nc.vector.tensor_copy(cb[:, g, :], bank(4 + g)[:, 0:384]).then_inc(sem("cb_copied"), 1)
            dve.wait_ge(sem("cb_masked"), 2)
            for c in range(WC):
                for par in range(2):
                    h = 2 * c + par
                    m = dec[par]
                    dve.wait_ge(sem("ssd_row"), h + 1)
                    nc.vector.tensor_scalar(m[:, 0:256], bank(4 + par)[:, 0:256], cumT[:, 0, h:h + 1], 0.0,
                                            ALU.subtract, ALU.min)
                    nc.vector.tensor_scalar(m[:, 256:384], bank(4 + par)[:, 128:256], cumT[:, 1, h:h + 1],
                                            0.0, ALU.subtract, ALU.min).then_inc(sem("ssd_diff"), 1)
                for par in range(2):
                    dve.wait_ge(sem("ssd_decay"), 2 * c + par + 1)
                    nc.vector.tensor_tensor(dec[par][:, :], dec[par][:, :], cb[:, c // 4, :], ALU.mult
                                            ).then_inc(sem("ssd_mat"), 1)
                beside_ssd(3 + c, 4 + c)
                for par in range(2):
                    h = 2 * c + par
                    p0, p1 = 64 * par, 64 * par + 64
                    dve.wait_ge(sem("ssd_y"), h + 1)
                    yy = yssd[p0:p1, c, :]
                    nc.vector.scalar_tensor_tensor(yy, xconv[p0:p1, c, :], vcol("d_skip", c, p0, p1),
                                                   bank(6 + par)[p0:p1, 0:T], ALU.mult, ALU.add
                                                   ).then_inc(sem("ssd_out"), 1)
                    dve.wait_ge(sem("ssd_out"), h + 1)
                    st.link(nc.vector.tensor_tensor(yy, yy, zg[p0:p1, c, :], ALU.mult))
            dve.sem_inc(sem("ssd_gated"), 1)
            for g in range(2):
                beside_ssd(11 + 2 * g, 13 + 2 * g)
                norm_dve(dve, st, f"s{g}", None, 4, sst, RMS_EPS, centre=False, scale=False)
                rms_split(f"s{g}", yssd[:, 4 * g:4 * g + 4, :], sst[2], "ssd_norm", 4, mhi, mlo,
                          xconv[:, 4 * g:4 * g + 4, :], j0=4 * g, c0=4 * g)
            beside_ssd(15, 16)
            blocks(dve, st, FIRST["fq"], COUNT["fq"], lo_only)
            for r in range(4):
                dve.wait_ge(sem("fv_turned"), r + 1)
                nc.vector.tensor_copy(
                    fvtok[:, :, 256 * r:256 * r + 256].rearrange("p j (h d) -> p h j d", h=2),
                    bank(4 + r)[:, :].rearrange("p (h j d) -> p h j d", h=2, j=NT)).then_inc(sem("fvtok_ready"), 1)

            def add_x1_pair(b, i, g):
                lo_only(b, i, g)
                dve.wait_ge(mm_done, b.count(1))
                j = (b.n0 - FIRST["w_out2"]) % 8
                dst = x1[:, 2 * j:2 * j + 2, :]
                nc.vector.tensor_tensor(dst, dst, bank(b.bank)[:, :].rearrange("p (a n) -> p a n", a=2), ALU.add
                                        ).then_inc(evacuated[b.bank], 1)

            def beside_f(c, i):
                if i == 0:
                    add_x1_pair(Block(FIRST["w_out2"] + c), 0, 0)
            attend_dve(dve, st, "f", fprob, fsmall, fo, None, False, beside_f)
            dve.wait_ge(sem("f_hi"), 1)
            nc.vector.tensor_tensor(mlo[:, 8:16, :], fo[:, :, :], mhi[:, 8:16, :].bitcast(f32),
                                    ALU.subtract).then_inc(sem("f_done"), 1)

            def add_x1(b, i, g):
                lo_only(b, i, g)
                j = i
                dve.wait_ge(mm_done, b.count(1))
                nc.vector.tensor_tensor(chunk(x1, j), chunk(x1, j), bank(b.bank)[:, 0:T], ALU.add
                                        ).then_inc(evacuated[b.bank], 1)
            for n in range(8, 16):
                add_x1_pair(Block(FIRST["w_out2"] + n), 0, 0)
            rms_parts("h2", "ln2_w")
            blocks(dve, st, FIRST["wq"], 16, lo_only)
            PIECE = 12

            def routing():
                def best16(n, values, vals, idx, ready):
                    for r in range(n):
                        ready(r)
                        ins = nc.vector.max(vals[:, r, 0:8], values[:, r, :])
                        if r % PIECE == PIECE - 1:
                            yield
                    st.link(ins)
                    for r in range(n):
                        ins = nc.vector.max_index(idx[:, r, 0:8], vals[:, r, 0:8], values[:, r, :])
                        if r % PIECE == PIECE - 1 and r < n - 1:
                            yield
                    st.link(ins)
                    for r in range(n):
                        ins = nc.vector.match_replace(values[:, r, :], vals[:, r, 0:8], values[:, r, :], LOWEST)
                        if r % PIECE == PIECE - 1 and r < n - 1:
                            yield
                    st.link(ins)
                    for r in range(n):
                        ins = nc.vector.max(vals[:, r, 8:16], values[:, r, :])
                        if r % PIECE == PIECE - 1 and r < n - 1:
                            yield
                    st.link(ins)
                    for r in range(n):
                        ins = nc.vector.max_index(idx[:, r, 8:16], vals[:, r, 8:16], values[:, r, :])
                        if r % PIECE == PIECE - 1 and r < n - 1:
                            yield
                    st.link(ins)

                def scores_out(r):
                    if r % 4 == 0:
                        dve.wait_ge(sem("scores_out"), r // 4 + 1)
                yield from best16(NT * KC, ps_[:, :, :, :].rearrange("p j h n -> p (j h) n"), top, topi, scores_out)
                st.link(nc.vector.tensor_copy(topf[:, :, :], topi[:, :, :]))
                pair = top[:, :, :].rearrange("p (r s) a -> p r s a", s=2)
                for r0 in (0, 8):
                    first = pair[:, r0:r0 + 8, 0, :].rearrange("p r (a b) -> p r a b", b=1).to_broadcast([128, 8, 16, 16])
                    second = pair[:, r0:r0 + 8, 1, :].rearrange("p r (a b) -> p r a b", a=1).to_broadcast([128, 8, 16, 16])
                    ins = nc.vector.tensor_tensor(cand[:, r0:r0 + 8, :].rearrange("p r (a b) -> p r a b", a=16), first,
                                                  second, ALU.add)
                    yield
                st.link(ins)
                yield from best16(KC, cand, best, besti, lambda r: None)
                st.link(nc.vector.tensor_scalar(slot_i[0][:, :, :], besti[:, :, :], 4, None, ALU.logical_shift_right))
                st.link(nc.vector.tensor_scalar(slot_i[1][:, :, :], besti[:, :, :], 15, None, ALU.bitwise_and))
                idx = topf[:, :, :].rearrange("p (r s) a -> p r s a", s=2)
                for i in range(2):
                    st.link(nc.vector.tensor_copy(slot_f[i][:, :, :], slot_i[i][:, :, :]))
                    for r0 in (0, 8):
                        h4 = hit[:, r0:r0 + 8, :].rearrange("p r (k a) -> p r k a", k=16)
                        st.link(nc.vector.tensor_tensor(
                            h4, slot_f[i][:, r0:r0 + 8, :].rearrange("p r (k a) -> p r k a", a=1).to_broadcast([128, 8, 16, 16]),
                            iota[:, 0:16].rearrange("p (r k a) -> p r k a", r=1, k=1).to_broadcast([128, 8, 16, 16]),
                            ALU.is_equal))
                        yield
                        st.link(nc.vector.tensor_tensor(
                            h4, h4, idx[:, r0:r0 + 8, i, :].rearrange("p r (k a) -> p r k a", k=1).to_broadcast([128, 8, 16, 16]),
                            ALU.mult))
                        yield
                    st.link(nc.vector.reduce_sum(chosen[i][:, :, :], hit[:, :, :].rearrange("p r (k a) -> p r k a", k=16),
                                                 AX.X))
                    yield
            pieces = routing()
            for n in range(U_EARLY, U_GATES):
                lo_only(Block(n), 0, 0)
                next(pieces, None)
            for _ in pieces:
                pass
            st.link(nc.vector.tensor_tensor(best[:, :, 1:16], best[:, :, 1:16],
                                            best[:, :, 0:1].to_broadcast([128, KC, 15]), ALU.subtract))
            st.link(nc.vector.tensor_tensor(best[:, :, 0:1], best[:, :, 0:1], best[:, :, 0:1], ALU.subtract))
            dve.sem_inc(sem("best_shifted"), 1)
            dve.wait_ge(sem("best_exp"), 1)
            st.link(nc.vector.reduce_sum(gsum[:, :], best[:, :, :], AX.X))
            st.link(nc.vector.reciprocal(gsum[:, :], gsum[:, :]))
            nc.vector.tensor_tensor(chosen[2][:, :, :], best[:, :, :],
                                    gsum[:, :].rearrange("p (r a) -> p r a", a=1).to_broadcast([128, KC, 16]),
                                    ALU.mult).then_inc(sem("chosen_ready"), 1)
            dve.wait_ge(sem("chosen_turned"), 1)
            for i in range(3):
                st.link(nc.vector.tensor_copy(chosenT[i][:, :], bank(4 + i)[:, 0:T]))
            dve.sem_inc(sem("chosenT_ready"), 1)
            for part in range(8):
                for i in range(8):
                    n, o = 8 * part + i, i % 4
                    dve.wait_ge(sem("onehot_free"), n + 1)
                    nc.vector.tensor_tensor(
                        one2[o][:, :, :], iota[:, :].rearrange("p (a n) -> p a n", a=1).to_broadcast([128, 4, 128]),
                        chosenT[1][:, 4 * n:4 * n + 4].rearrange("p (a n) -> p a n", n=1).to_broadcast([128, 4, 128]),
                        ALU.is_equal)
                    for t in range(4):
                        tok = slice(4 * n + t, 4 * n + t + 1)
                        ins = nc.vector.tensor_scalar(one1[o][:, t, :], iota[:, :], chosenT[0][:, tok],
                                                      chosenT[2][:, tok], ALU.is_equal, ALU.mult)
                    ins.then_inc(sem("onehots"), 1)
                    if i == 5:
                        lo_only(Block(U_GATES + part), 0, 0)
            for n in range(U_REST, V_EARLY):
                lo_only(Block(n), 0, 0)

            def early_gate(e, q):
                dve.wait_ge(sem("gate_loaded"), e * 16 + 16)
                if q == 0:
                    wait_early_gelu(dve, e)
                part = uact[e][:, 4 * q:4 * q + 4, :]
                nc.vector.tensor_tensor(part, part, gslice[:, :, 4 * q:4 * q + 4].rearrange("p t i -> p i t"), ALU.mult
                                        ).then_inc(sem("early_gated"), 1)

            def early_split(e, q):
                dve.wait_ge(sem("early_hi"), 4 * e + q + 1)
                part = slice(4 * q, 4 * q + 4)
                nc.vector.tensor_tensor(aglo[e][:, part, :], uact[e][:, part, :], aghi[e][:, part, :].bitcast(f32),
                                        ALU.subtract).then_inc(sem("early_lo"), 1)
            for q in range(4):
                early_gate(0, q)
            for q in range(4):
                early_split(0, q)
            for e in range(EARLY):
                for n in range(16):
                    add_x1(Block(V_EARLY + 16 * e + n), n, 0)
                    if e == 0 and n >= 4 and n < 12:
                        (early_split if n % 2 else early_gate)(1, (n - 4) // 2)

            def slice_dve(e):
                def upward(b, i, g):
                    if exists(b.count(SPLIT)):
                        split_lo(dve, b.ahead(SPLIT), (0,))
                    dve.wait_ge(sem("gate_loaded"), e * 16 + (16 * EARLY + 16))
                    p = b.n0 % 2
                    dve.wait_ge(evacuated[b.bank], b.uses())
                    nc.vector.tensor_tensor(gated[p][:, :], gelu[p][:, :],
                                            gslice[:, :, bass.ds(i, 1)].rearrange("p t a -> p (t a)"), ALU.mult
                                            ).then_inc(sem("u_gated"), 1)
                    if exists(b.count(SPLIT)):
                        split_lo(dve, b.ahead(SPLIT), (1,))
                    dve.wait_ge(sem("ag_hi"), e * 16 + i + 1)
                    nc.vector.tensor_tensor(chunk(aglo[0], i), gated[p][:, :], chunk(aghi[0], i).bitcast(f32),
                                            ALU.subtract).then_inc(sem("ag_lo"), 1)
                expert_blocks(dve, st, e, 0, upward)
                expert_blocks(dve, st, e, 16, add_x1)
            with st.loop(LATE - 1, 0) as e:
                slice_dve(e)
            slice_dve(LATE - 1)
            norm_dve(dve, st, "fin", x1, KC, fst, RMS_EPS, centre=False, scale=False)
            for c in range(KC):
                ins = nc.vector.scalar_tensor_tensor(zsum[:, c, :], x1[:, c, :], vcol("lnf_w", c), fst[2][:, :],
                                                     ALU.mult, ALU.mult)
                ins.then_inc(sem("out_ready"), 1)

        @block.scalar
        def _(act):
            st = Steps(act, sem("act_steps"))
            act.dma_start(onehot_b[:, :], buckets).then_inc(sem("onehot_loaded"), 16)
            act.dma_start(relb_sb[:, :], relb).then_inc(sem("onehot_loaded"), 16)
            act.dma_start(vec[:, :], vecs).then_inc(sem("vec_loaded"), 16)
            act.wait_ge(sem("x_loaded"), 16)
            nc.scalar.copy(xhi[:, :, :], xraw[:, :, :]).then_inc(sem("xhi_ready"), 1)
            for n in range(SPLIT):
                split_hi(act, Block(n))

            def evac(first, put):
                def body(b, i, g):
                    if exists(b.count(SPLIT)):
                        split_hi(act, b.ahead(SPLIT))
                    act.wait_ge(mm_done, b.count(1))
                    put(bank(b.bank)[:, 0:T], b.index(first), b)
                return body

            def to(buf, func=ACT.Copy, off=0):
                def put(ps, j, b):
                    nc.scalar.activation(chunk(buf, j)[:, off:off + T], ps, func).then_inc(evacuated[b.bank], 1)
                return put

            def run(name, put):
                blocks(act, st, FIRST[name], COUNT[name], evac(FIRST[name], put))

            run("c_kv", to(ckv))
            act.wait_ge(sem("cq_cleared"), 1)

            def put_q(q):
                def put(ps, j, b):
                    for par in range(2):
                        p0, p1 = 64 * par, 64 * par + 64
                        dst = q[par][p0:p1, :, :]
                        dst = dst[:, j, :] if isinstance(j, int) else \
                            dst[:, bass.ds(j, 1), :].rearrange("p a n -> p (a n)")
                        ins = nc.scalar.mul(dst, ps[p0:p1, :], 0.125)
                    ins.then_inc(evacuated[b.bank], 1)
                return put
            run("c_q", put_q([cq[:, i, :, :] for i in range(2)]))
            run("c_gate", to(cgate, ACT.Silu))
            act.wait_ge(sem("vec_loaded"), 16)
            def put_sig(func, used0):
                def put(ps, j, b):
                    act.wait_ge(sem("sig_used"), j + used0 + 1)
                    nc.scalar.activation(sig[b.n0 % 2][:, :], ps, func).then_inc(evacuated[b.bank], 1)
                return put
            act.wait_ge(sem("glu_padded"), 1)

            def beside_c(c, i):
                n = FIRST["d_val"] + 2 * c + i
                if n < FIRST["d_act"]:
                    evac(FIRST["d_val"], to(glu, off=CONV_K - 1))(Block(n), 0, 0)
                else:
                    evac(FIRST["d_act"], put_sig(ACT.Sigmoid, 0))(Block(n), 0, 0)
            attend_act(act, "c", cprob, cprobT, csmall, True, beside_c)
            act.wait_ge(sem("c_o"), 2 * WC)
            nc.scalar.copy(yhi[YC][:, :, :], co[:, :, :]).then_inc(sem("c_hi"), 1)
            act.wait_ge(sem("c_done"), 1)
            run("d_gate", to(dgate, ACT.Silu))
            run("b_v", to(bv))
            run("b_u", to(bug))
            run("b_gate", put_sig(ACT.Silu, 8))
            act.wait_ge(sem("conv_done"), 1)
            act.wait_ge(sem("ain_padded"), 1)

            def beside_a(first, end):
                for n in range(first, end):
                    if n < 8:
                        evac(FIRST["a_in"], to(ain, off=PAD))(Block(FIRST["a_in"] + n), 0, 0)
                    else:
                        evac(FIRST["a_gate"], to(agate, ACT.Silu))(Block(FIRST["a_in"] + n), 0, 0)
            norm_square(act, "d", dacc, dsq)
            beside_a(0, 2)
            norm_sqrt(act, "d", stat)
            beside_a(2, 3)
            affine_act(act, "d", dacc, WC, "conv_ln_g", "conv_ln_b", ACT.Silu)
            beside_a(3, 4)
            act.wait_ge(sem("d_gated"), 1)
            nc.scalar.copy(yhi[YD][:, :, :], dacc[:, :, :]).then_inc(sem("d_hi"), 1)
            norm_square(act, "b", bv, bsq)
            beside_a(4, 6)
            norm_sqrt(act, "b", stat)
            beside_a(6, 7)
            affine_act(act, "b", bv, WC, "sgu_ln_g", "sgu_ln_b", ACT.Identity)
            beside_a(7, 9)
            act.wait_ge(sem("b_gated"), 1)
            nc.scalar.copy(yhi[YB][:, :, :], bug[:, :, :]).then_inc(sem("b_hi"), 1)
            beside_a(9, 12)
            act.wait_ge(sem("mix_ready"), 1)
            nc.scalar.copy(mixhi[:, :, :], ain[:, :, PAD:]).then_inc(sem("mixhi_ready"), 1)
            beside_a(12, 16)
            if exists(FIRST["a_pool"] + SPLIT):
                split_hi(act, Block(FIRST["a_pool"] + SPLIT))
            act.wait_ge(sem("a_gated"), 1)
            act.wait_ge(mm_done, FIRST["a_pool"] + 1)
            nc.scalar.copy(yhi[YA][:, :, :], win_a[:, :, 0:T]).then_inc(sem("a_hi"), 1)
            def merging(b, i, g):
                if exists(b.count(SPLIT)):
                    split_hi(act, b.ahead(SPLIT))
                j, m = i % 6, i // 6
                if j < 4:
                    act.wait_ge(mm_done, b.count(1))
                    if j == 0:
                        act.wait_ge(sem("gates_free"), 2 * g + m + 1)
                    nc.scalar.activation(gates[m][:, j, :], bank(b.bank)[:, 0:T], ACT.Sigmoid
                                         ).then_inc(evacuated[b.bank], 1)
                elif j == 5:
                    col = 2 * g + m
                    act.wait_ge(sem("merge_sum"), col + 1)
                    nc.scalar.copy(chunk(mhi, col), msum[0][:, :]).then_inc(sem("mhi_done"), 1)
            blocks(act, st, FIRST["merge"], 96, merging, unit=12)

            def hi_only(b, i, g):
                if exists(b.count(SPLIT)):
                    split_hi(act, b.ahead(SPLIT))
            blocks(act, st, FIRST["w_out"], 16, hi_only)
            for q in range(4):
                act.wait_ge(sem("x1_centred"), q + 1)
                nc.scalar.activation(sq16[:, 4 * q:4 * q + 4, :], zsum[:, 4 * q:4 * q + 4, :], ACT.Square
                                     ).then_inc(sem("x1_sq"), 1)
            norm_sqrt(act, "x1", st16)
            for c in range(KC):
                act.wait_ge(sem("x1_scaled"), c + 1)
                nc.scalar.activation(sq16[:, c, :], zsum[:, c, :], ACT.Square, bias=vcol("ln_b", c)
                                     ).then_inc(sem("h1_sq"), 1)
            norm_sqrt(act, "h1", st16)

            def hi_parts(name):
                for q in range(4):
                    act.wait_ge(sem(name + "_scaled"), q + 1)
                    nc.scalar.copy(xhi[:, 4 * q:4 * q + 4, :], zsum[:, 4 * q:4 * q + 4, :]
                                   ).then_inc(sem(name + "_hi"), 1)
            hi_parts("h1")
            nc.scalar.activation(acol[:, 0:1], vcol("a_log"), ACT.Exp).then_inc(sem("acol_exp"), 1)
            hi_only(Block(FIRST["dtf"]), 0, 0)
            act.wait_ge(sem("dt_abs"), 1)
            nc.scalar.activation(dtt[1][:, :], dtt[1][:, :], ACT.Exp, scale=-1.0).then_inc(sem("dt_exp"), 1)
            act.wait_ge(sem("dt_one"), 1)
            nc.scalar.activation(dtt[3][:, :], dtt[2][:, :], ACT.Ln).then_inc(sem("dt_log"), 1)
            run("z", to(zg, ACT.Silu))
            run("xbc", to(xpad, off=CONV2_K - 1))
            act.wait_ge(sem("conv2_done"), 1)
            nc.scalar.activation(xconv[:, :, :], xconv[:, :, :], ACT.Silu).then_inc(sem("xconv_ready"), 1)

            def beside_ssd(first, end):
                for n in range(first, end):
                    name, dst = ("fk", fk) if n < 8 else ("fv", fv)
                    evac(FIRST[name], to(dst))(Block(FIRST["fk"] + n), 0, 0)
            beside_ssd(0, 3)
            for c in range(WC):
                for par in range(2):
                    act.wait_ge(sem("ssd_diff"), 2 * c + par + 1)
                    nc.scalar.activation(dec[par][:, :], dec[par][:, :], ACT.Exp).then_inc(sem("ssd_decay"), 1)
                beside_ssd(3 + c, 4 + c)
            for g in range(2):
                beside_ssd(11 + 2 * g, 13 + 2 * g)
                norm_act(act, f"s{g}", yssd[:, 4 * g:4 * g + 4, :], ssq, sst,
                         lambda e: e.wait_ge(sem("ssd_gated"), 1), centre=False)
                act.wait_ge(sem("norm_scaled"), turn("scaled", f"s{g}"))
                nc.scalar.copy(mhi[:, 4 * g:4 * g + 4, :], xconv[:, 4 * g:4 * g + 4, :]).then_inc(sem("norm_hi"), 1)
            beside_ssd(15, 16)
            act.wait_ge(sem("fq_cleared"), 2)
            run("fq", put_q(fq))

            def beside_f(c, i):
                if i == 0:
                    hi_only(Block(FIRST["w_out2"] + c), 0, 0)
            attend_act(act, "f", fprob, fprobT, fsmall, False, beside_f)
            act.wait_ge(sem("f_o"), HEADS)
            nc.scalar.copy(mhi[:, 8:16, :], fo[:, :, :]).then_inc(sem("f_hi"), 1)
            for n in range(8, 17):
                if n < 16:
                    hi_only(Block(FIRST["w_out2"] + n), 0, 0)
                if n >= 9:
                    pair = slice(2 * (n - 9), 2 * (n - 9) + 2)
                    block_out(act, FIRST["w_out2"] + n - 1)
                    nc.scalar.activation(sq16[:, pair, :], x1[:, pair, :], ACT.Square).then_inc(sem("h2_sq"), 1)
            norm_sqrt(act, "h2", st16)
            hi_parts("h2")
            run("wq", to(pq))
            for n in range(8):
                act.wait_ge(sem("scores_ready"), n + 1)
                nc.scalar.copy(ps_[:, n // 4, 4 * (n % 4):4 * (n % 4) + 4, :], bank(4 + n % 4)[:, :]
                               ).then_inc(sem("scores_out"), 1)
            def early_gelu(first, end):
                for n in range(first, end):
                    e = (n - U_EARLY) // 16
                    evac(U_EARLY + 16 * e, to(uact[e], ACT.Gelu))(Block(n), 0, 0)
            early_gelu(U_EARLY, U_GATES)
            act.wait_ge(sem("best_shifted"), 1)
            nc.scalar.activation(best[:, :, :], best[:, :, :], ACT.Exp).then_inc(sem("best_exp"), 1)
            act.wait_ge(sem("chosenT_ready"), 1)
            act.sem_inc(sem("bank_free"), 4)
            act.sem_inc(sem("onehot_free"), 4)
            for half in range(8):
                if half >= 2:
                    act.wait_ge(sem(f"gate_stored{half % 2}"), 16 * (half // 2))
                for i in range(8):
                    act.wait_ge(sem("gate_product"), 8 * half + i + 1)
                    act.sem_inc(sem("onehot_free"), 1)
                    nc.scalar.copy(gstage[half % 2][:, :, 4 * i:4 * i + 4, :],
                                   bank(4 + i % 4)[:, :].rearrange("p (t e i) -> p e t i", t=4, e=SLICES)
                                   ).then_inc(sem("stage_full"), 1)
                    act.wait_ge(sem("stage_full"), 8 * half + i + 1)
                    act.sem_inc(sem("bank_free"), 1)
                    if i == 3:
                        early_gelu(U_GATES + half, U_GATES + half + 1)
            early_gelu(U_REST, V_EARLY)
            for i in range(2):
                act.wait_ge(sem(f"gate_stored{i}"), 64)

            def early_hi(e, q):
                act.wait_ge(sem("early_gated"), 4 * e + q + 1)
                nc.scalar.copy(aghi[e][:, 4 * q:4 * q + 4, :], uact[e][:, 4 * q:4 * q + 4, :]
                               ).then_inc(sem("early_hi"), 1)
            for q in range(4):
                early_hi(0, q)
            for n in range(16 * EARLY):
                hi_only(Block(V_EARLY + n), 0, 0)
                if n >= 4 and n < 12 and n % 2 == 0:
                    early_hi(1, (n - 4) // 2)

            def slice_act(e):
                def upward(b, i, g):
                    if exists(b.count(SPLIT)):
                        split_hi(act, b.ahead(SPLIT), (0,))
                    p = b.n0 % 2
                    act.wait_ge(mm_done, b.count(1))
                    nc.scalar.activation(gelu[p][:, :], bank(b.bank)[:, 0:T], ACT.Gelu).then_inc(evacuated[b.bank], 1)
                    if exists(b.count(SPLIT)):
                        split_hi(act, b.ahead(SPLIT), (1,))
                    act.wait_ge(sem("u_gated"), e * 16 + i + 1)
                    nc.scalar.copy(chunk(aghi[0], i), gated[p][:, :]).then_inc(sem("ag_hi"), 1)
                expert_blocks(act, st, e, 0, upward)

                def downward(b, i, g):
                    hi_only(b, i, g)
                    if isinstance(e, int) and i:
                        square(i - 1)

                def square(c):
                    block_out(act, NBLOCKS - 16 + c)
                    nc.scalar.activation(sq16[:, c, :], x1[:, c, :], ACT.Square).then_inc(sem("fin_sq"), 1)
                expert_blocks(act, st, e, 16, downward)
                if isinstance(e, int):
                    square(15)
            with st.loop(LATE - 1, 0) as e:
                slice_act(e)
            slice_act(LATE - 1)
            norm_sqrt(act, "fin", fst)


def layout(x, w_in, pool_w, pool_scale, sgu_ln_g, sgu_ln_b, sgu_w, sgu_b, attn_sinks, rel_bias, conv_w, conv_b,
           conv_ln_g, conv_ln_b, w_branch, w_out, ln_g, ln_b, ln1_w_2, w_in_2, conv_w_2, conv_b_2, dt_bias_2,
           a_log_2, d_skip_2, ssd_norm_w_2, fox_f_bias_2, w_out_2, ln2_w_2, peer_wq_2, peer_k1_2, peer_k2_2,
           peer_u_2, peer_v_2, lnf_w_2):
    f = np.float32
    stream = np.empty((NBLOCKS, 128, KC * 128), f)

    def put(name, w):
        n = w.shape[1] // 128
        assert n == COUNT[name]
        stream[FIRST[name]:FIRST[name] + n] = w.reshape(KC, 128, n, 128).transpose(2, 1, 0, 3).reshape(n, 128, -1)

    def pairs(w):
        return w.reshape(*w.shape[:-1], 2, 8, 64).swapaxes(-3, -2).reshape(*w.shape[:-1], 1024)

    w = w_in[0]
    at = 0
    for name, n in [("a_in", 1024), ("a_gate", 1024), ("b_u", 1024), ("b_v", 1024), ("b_gate", 1024),
                    ("c_q", 1024), ("c_kv", 256), ("c_gate", 1024), ("d_val", 1024), ("d_act", 1024),
                    ("d_gate", 1024)]:
        cols = w[:, at:at + n]
        put(name, pairs(cols) if name in ("c_q", "c_gate") else cols)
        at += n
    merge = stream[FIRST["merge"]:FIRST["merge"] + 96].reshape(16, 6, 128, 2048)
    merge[:, 0:4] = w[:, at:].reshape(KC, 128, 4, 16, 128).transpose(3, 2, 1, 0, 4).reshape(16, 4, 128, 2048)
    wb = [w_branch[0, 0], w_branch[0, 1], pairs(w_branch[0, 2].T).T, w_branch[0, 3]]
    for i in range(4):
        merge[:, 4 + i // 2].reshape(16, 128, 2, 1024)[:, :, i % 2] = \
            wb[i].reshape(8, 128, 16, 128).transpose(2, 1, 0, 3).reshape(16, 128, 1024)
    stream[FIRST["a_pool"]] = pool_w[0].reshape(4, 2, 128, 2, 128).transpose(2, 0, 3, 1, 4).reshape(128, 2048)
    put("w_out", w_out[0])
    w = w_in_2
    put("z", w[:, 0:1024])
    put("xbc", w[:, 1024:2560])
    dtf = np.zeros((D, 128), f)
    dtf[:, 0:16], dtf[:, 32:48] = w[:, 2560:2576], w[:, 5648:5664]
    put("dtf", dtf)
    for i, name in enumerate(("fq", "fk", "fv")):
        put(name, w[:, 2576 + 1024 * i:3600 + 1024 * i])
    stream[FIRST["w_out2"]:FIRST["w_out2"] + 16] = \
        w_out_2.reshape(2, 8, 128, 8, 2, 128).transpose(0, 3, 2, 4, 1, 5).reshape(16, 128, 2048)
    put("wq", peer_wq_2)
    ex = stream[FIRST["experts"]:].reshape(2 * SLICES, 16, 128, 2048)
    for e in range(SLICES):
        up, down = (e, 2 + e) if e < 2 else (2 * e, 2 * e + 1)
        rows = slice(2048 * e, 2048 * e + 2048)
        ex[up] = peer_u_2[rows].reshape(16, 128, KC, 128).transpose(0, 3, 2, 1).reshape(16, 128, 2048)
        ex[down] = peer_v_2[rows].reshape(16, 128, 16, 128).transpose(2, 1, 0, 3).reshape(16, 128, 2048)

    vecs = np.zeros((128, NVEC), f)

    def vput(name, a):
        vecs[:, VCOL[name]:VCOL[name] + a.shape[1]] = a

    for name, a in [("pool_scale", pool_scale[0]), ("sgu_ln_g", sgu_ln_g[0]), ("sgu_ln_b", sgu_ln_b[0]),
                    ("conv_b", conv_b[0]), ("conv_ln_g", conv_ln_g[0]), ("conv_ln_b", conv_ln_b[0]),
                    ("ln_g", ln_g[0]), ("ln_b", ln_b[0]), ("ln1_w", ln1_w_2), ("conv2_b", conv_b_2),
                    ("ssd_norm", ssd_norm_w_2), ("ln2_w", ln2_w_2), ("lnf_w", lnf_w_2)]:
        vput(name, a.reshape(-1, 128).T)
    vput("conv_w", conv_w[0].reshape(CONV_K, 8, 128).transpose(2, 1, 0).reshape(128, -1))
    vput("conv2_w", conv_w_2.reshape(CONV2_K, 12, 128).transpose(2, 1, 0).reshape(128, -1))
    vput("d_skip", np.repeat(d_skip_2.reshape(8, 2).T, 64, axis=0))
    vput("sinks", np.broadcast_to(attn_sinks[0].reshape(2, 8).T.reshape(1, 16), (128, 16)))
    vecs[0:16, VCOL["dtf_bias"]], vecs[32:48, VCOL["dtf_bias"]] = dt_bias_2, fox_f_bias_2
    vecs[0:16, VCOL["dtf_sign"]], vecs[32:48, VCOL["dtf_sign"]] = 1.0, -1.0
    vecs[0:16, VCOL["a_log"]] = a_log_2
    dist = 127 - np.arange(128)
    large = 16 + (np.log(np.maximum(dist, 1).astype(f) / 16) / np.log(8.0) * 16).astype(np.int32)
    buckets = (np.where(dist < 16, dist, np.minimum(large, 31))[None, :] == np.arange(32)[:, None]).astype(f)
    count = np.minimum(np.arange(T)[None, :] + 1, np.array([2, 4, 8, 16])[:, None])
    return {
        "stream": stream,
        "xt": x[0].reshape(T, KC, 128).transpose(2, 1, 0).reshape(128, -1),
        "vecs": vecs,
        "sgu_wt": sgu_w[0].transpose(2, 0, 1).reshape(128, -1),
        "sgu_b": sgu_b[0].reshape(-1),
        "relb": rel_bias.reshape(32, 2, 8).transpose(0, 2, 1).reshape(32, 16),
        "buckets": buckets,
        "keys": np.stack([peer_k1_2, peer_k2_2], axis=1).transpose(3, 0, 1, 2).reshape(128, -1),
        "inv_cnt": (1.0 / count).astype(f).reshape(-1),
    }


def kernel(**inputs):
    import concourse.bacc as bacc
    from concourse.bass_utils import run_bass_kernel_spmd

    nc = bacc.Bacc("TRN2", target_bir_lowering=False, num_devices=1)
    arrays = {n: np.ascontiguousarray(a) for n, a in layout(**{n: np.asarray(a) for n, a in inputs.items()}).items()}
    args = {n: nc.dram_tensor(n, a.shape, mybir.dt.from_np(a.dtype), kind="ExternalInput").ap()
            for n, a in arrays.items()}
    out = nc.dram_tensor("out", (128, KC * T), mybir.dt.float32, kind="ExternalOutput").ap()
    build(nc, out=out, **args)
    r = run_bass_kernel_spmd(nc, [arrays], core_ids=[0])
    got = r.results[0]["out"]
    return got.reshape(128, KC, T).transpose(2, 1, 0).reshape(1, T, D)
```
